# Optimizing a Trainium2 kernel written in Bass

```python
import math
import jax, jax.numpy as jnp
from jax import lax
import numpy as np
import jax
import jax.numpy as jnp

D_MODEL = 1024
BATCH = 1
SEQ = 512
DEPTH = 1

CHUNK = 64
RET_HEADS = 4
RET_HEAD_DIM = D_MODEL // 8
RET_WIDTH = RET_HEADS * RET_HEAD_DIM
POOL_WINDOWS = (2, 4, 8, 16)
POOL_GROUPS = len(POOL_WINDOWS)
POOL_GROUP_DIM = D_MODEL // 8
POOL_WIDTH = POOL_GROUPS * POOL_GROUP_DIM
MIX_WIDTH = RET_WIDTH + POOL_WIDTH
IN_WIDTH = 4 * RET_WIDTH + POOL_WIDTH
D_FF = ((8 * D_MODEL // 3 + 127) // 128) * 128
CONV_WIDTH = 3
ROPE_BASE = 10000.0
LN_EPS = 1e-5
RMS_EPS = 1e-6
DEEPNORM_ALPHA = (2.0 * DEPTH) ** 0.25
DEEPNORM_BETA = (8.0 * DEPTH) ** -0.25


def _layernorm(x, g, b):
    xf = x.astype(jnp.float32)
    mu = jnp.mean(xf, axis=-1, keepdims=True)
    var = jnp.mean(jnp.square(xf - mu), axis=-1, keepdims=True)
    y = (xf - mu) * lax.rsqrt(var + LN_EPS) * g.astype(jnp.float32) + b.astype(jnp.float32)
    return y.astype(x.dtype)

def _rope(t):
    s, dh = t.shape[1], t.shape[-1]
    inv_freq = ROPE_BASE ** (-jnp.arange(0, dh, 2, dtype=jnp.float32) / dh)
    ang = jnp.arange(s, dtype=jnp.float32)[:, None] * inv_freq[None, :]
    cos = jnp.cos(ang)[None, :, None, :]
    sin = jnp.sin(ang)[None, :, None, :]
    tf = t.astype(jnp.float32)
    t1, t2 = tf[..., : dh // 2], tf[..., dh // 2:]
    return jnp.concatenate([t1 * cos - t2 * sin, t1 * sin + t2 * cos], axis=-1)

def _retention(q, k, v):
    b, s, h, dh = q.shape
    nc = s // CHUNK
    log_gamma = jnp.log(1.0 - 2.0 ** (-5.0 - jnp.arange(h, dtype=jnp.float32)))
    idx = jnp.arange(CHUNK, dtype=jnp.float32)
    inner_decay = jnp.exp(log_gamma[:, None, None] * jnp.abs(idx[:, None] - idx[None, :]))
    q_decay = jnp.exp(log_gamma[None, :] * (idx[:, None] + 1.0))
    k_decay = jnp.exp(log_gamma[None, :] * (CHUNK - 1.0 - idx[:, None]))
    chunk_decay = jnp.exp(log_gamma * CHUNK)

    qc = q.reshape(b, nc, CHUNK, h, dh)
    kc = k.reshape(b, nc, CHUNK, h, dh)
    vc = v.reshape(b, nc, CHUNK, h, dh)

    scores = jnp.einsum('bnihd,bnjhd->bnhij', qc, kc) * inner_decay[None, None]
    inner = jnp.einsum('bnhij,bnjhe->bnihe', scores, vc)

    def step(state, inp):
        q_n, k_n, v_n = inp
        cross = jnp.einsum('bihd,bhde->bihe', q_n * q_decay[None, :, :, None], state)
        new_state = state * chunk_decay[None, :, None, None] + jnp.einsum(
            'bjhd,bjhe->bhde', k_n * k_decay[None, :, :, None], v_n)
        return new_state, cross

    state0 = jnp.zeros((b, h, dh, dh), jnp.float32)
    xs = (jnp.moveaxis(qc, 1, 0), jnp.moveaxis(kc, 1, 0), jnp.moveaxis(vc, 1, 0))
    _, cross = lax.scan(step, state0, xs)
    out = inner + jnp.moveaxis(cross, 0, 1)
    return out.reshape(b, s, h, dh)

def _pool_mixer(p, w_pool, pool_scale):
    b, s, _ = p.shape
    pf = p.astype(jnp.float32).reshape(b, s, POOL_GROUPS, POOL_GROUP_DIM)
    cs = jnp.cumsum(pf, axis=1)
    pos = jnp.arange(1, s + 1, dtype=jnp.float32)
    outs = []
    for gi, w in enumerate(POOL_WINDOWS):
        c = cs[:, :, gi]
        prev = jnp.pad(c, ((0, 0), (w, 0), (0, 0)))[:, :s]
        mean = (c - prev) / jnp.minimum(pos, float(w))[None, :, None]
        outs.append(mean - pf[:, :, gi])
    pooled = jnp.stack(outs, axis=2).astype(p.dtype)
    y = jnp.einsum('bsgc,gcd->bsgd', pooled, w_pool).reshape(b, s, POOL_WIDTH)
    return y * pool_scale

def _conv_ffn(x, w_up, conv_w, conv_b, w_down):
    s = x.shape[1]
    u = x @ w_up
    val, gate = u[..., :D_FF], u[..., D_FF:]
    gp = jnp.pad(gate, ((0, 0), (CONV_WIDTH - 1, 0), (0, 0)))
    h = conv_b + sum(gp[:, j:j + s] * conv_w[j] for j in range(CONV_WIDTH))
    return (jax.nn.silu(h) * val) @ w_down

def first_inputs(seed: int = 0) -> dict:
    key = jax.random.key(seed)
    ks = jax.random.split(key, 20)
    f32 = jnp.float32
    L = DEPTH
    x = jax.random.normal(ks[0], (BATCH, SEQ, D_MODEL), f32)
    sd = D_MODEL ** -0.5
    w_qk = jax.random.normal(ks[1], (L, D_MODEL, 2 * RET_WIDTH), f32) * sd
    w_v = jax.random.normal(ks[2], (L, D_MODEL, RET_WIDTH), f32) * sd * DEEPNORM_BETA
    w_g = jax.random.normal(ks[3], (L, D_MODEL, RET_WIDTH), f32) * sd
    w_p = jax.random.normal(ks[4], (L, D_MODEL, POOL_WIDTH), f32) * sd * DEEPNORM_BETA
    w_in = jnp.concatenate([w_qk, w_v, w_g, w_p], axis=-1)
    w_pool = jax.random.normal(ks[5], (L, POOL_GROUPS, POOL_GROUP_DIM, POOL_GROUP_DIM), f32) * POOL_GROUP_DIM ** -0.5
    pool_scale = 1.0 + 0.1 * jax.random.normal(ks[6], (L, POOL_WIDTH), f32)
    w_out = jax.random.normal(ks[7], (L, MIX_WIDTH, D_MODEL), f32) * MIX_WIDTH ** -0.5 * DEEPNORM_BETA
    ln1_g = 1.0 + 0.05 * jax.random.normal(ks[8], (L, D_MODEL), f32)
    ln1_b = 0.02 * jax.random.normal(ks[9], (L, D_MODEL), f32)
    w_up = jax.random.normal(ks[10], (L, D_MODEL, 2 * D_FF), f32) * sd * DEEPNORM_BETA
    conv_w = jax.random.normal(ks[11], (L, CONV_WIDTH, D_FF), f32) * CONV_WIDTH ** -0.5
    conv_b = 0.02 * jax.random.normal(ks[12], (L, D_FF), f32)
    w_down = jax.random.normal(ks[13], (L, D_FF, D_MODEL), f32) * D_FF ** -0.5 * DEEPNORM_BETA
    ln2_g = 1.0 + 0.05 * jax.random.normal(ks[14], (L, D_MODEL), f32)
    ln2_b = 0.02 * jax.random.normal(ks[15], (L, D_MODEL), f32)
    return {"x": x, "w_in": w_in, "w_pool": w_pool, "pool_scale": pool_scale, "w_out": w_out,
            "ln1_g": ln1_g, "ln1_b": ln1_b, "w_up": w_up, "conv_w": conv_w, "conv_b": conv_b,
            "w_down": w_down, "ln2_g": ln2_g, "ln2_b": ln2_b}

def first_block(x, w_in, w_pool, pool_scale, w_out, ln1_g, ln1_b, w_up, conv_w, conv_b,
              w_down, ln2_g, ln2_b):
    b, s, _ = x.shape
    for l in range(DEPTH):
        proj = x @ w_in[l]
        q, k, v, g, p = jnp.split(proj, [RET_WIDTH, 2 * RET_WIDTH, 3 * RET_WIDTH, 4 * RET_WIDTH], axis=-1)
        q = _rope(q.reshape(b, s, RET_HEADS, RET_HEAD_DIM))
        k = _rope(k.reshape(b, s, RET_HEADS, RET_HEAD_DIM)) * (RET_HEAD_DIM ** -0.5)
        v = v.reshape(b, s, RET_HEADS, RET_HEAD_DIM).astype(jnp.float32)
        ret = _retention(q, k, v)
        ret = ret * lax.rsqrt(jnp.mean(jnp.square(ret), axis=-1, keepdims=True) + RMS_EPS)
        ret = ret.reshape(b, s, RET_WIDTH).astype(x.dtype) * jax.nn.silu(g)
        pool = _pool_mixer(p, w_pool[l], pool_scale[l])
        mix = jnp.concatenate([ret, pool], axis=-1) @ w_out[l]
        x = _layernorm(DEEPNORM_ALPHA * x + mix, ln1_g[l], ln1_b[l])
        ffn = _conv_ffn(x, w_up[l], conv_w[l], conv_b[l], w_down[l])
        x = _layernorm(DEEPNORM_ALPHA * x + ffn, ln2_g[l], ln2_b[l])
    return x


DEPTH_2 = 2

N_A_LAYERS = max(1, DEPTH_2 // 2)
N_B_LAYERS = DEPTH_2 - N_A_LAYERS

SSM_GROUP = 16
SSM_GROUPS = D_MODEL // SSM_GROUP
SSM_STATE = 64
STEP_MIN = 1e-3
STEP_MAX = 1e-1

N_HEADS = 16
QK_NOPE_DIM = 64
QK_ROPE_DIM = 32
QK_DIM = QK_NOPE_DIM + QK_ROPE_DIM
V_DIM = 64
Q_LORA_RANK = 384
KV_LORA_RANK = 256
ROPE_THETA = 10000.0
Q_BLOCK = 128

D_FF_2 = -(-8 * D_MODEL // (3 * 256)) * 256

EPS = 1e-6
NEG_INF = -1e30


def rms_norm(x, gain):
    xf = x.astype(jnp.float32)
    y = xf * lax.rsqrt(jnp.mean(xf * xf, axis=-1, keepdims=True) + EPS)
    return (y * gain.astype(jnp.float32)).astype(x.dtype)

def swiglu_ffn(h, w_gate_up, w_down):
    gate, up = jnp.split(h @ w_gate_up, 2, axis=-1)
    return (jax.nn.silu(gate) * up) @ w_down

def cmul(ar, ai, br, bi):
    return ar * br - ai * bi, ar * bi + ai * br

def s5_mixer(h, w_in, lam_re, lam_im, log_step, b_re, b_im, c_re, c_im, d_skip, w_glu):
    bsz, seq, _ = h.shape
    f32 = jnp.float32
    u = (h @ w_in).reshape(bsz, seq, SSM_GROUPS, SSM_GROUP).astype(f32)
    step = jnp.exp(log_step.astype(f32))[:, None]
    lr, li = lam_re.astype(f32), lam_im.astype(f32)
    decay = jnp.exp(lr * step)
    a_re, a_im = decay * jnp.cos(li * step), decay * jnp.sin(li * step)
    den = lr * lr + li * li
    f_re = ((a_re - 1.0) * lr + a_im * li) / den
    f_im = (a_im * lr - (a_re - 1.0) * li) / den
    br, bi = cmul(f_re[..., None], f_im[..., None], b_re.astype(f32), b_im.astype(f32))
    cr, ci = c_re.astype(f32), c_im.astype(f32)

    def combine(e_i, e_j):
        ar_i, ai_i, xr_i, xi_i = e_i
        ar_j, ai_j, xr_j, xi_j = e_j
        ar, ai = cmul(ar_j, ai_j, ar_i, ai_i)
        xr, xi = cmul(ar_j, ai_j, xr_i, xi_i)
        return ar, ai, xr + xr_j, xi + xi_j

    def scan_sequence(u_seq):
        bu_re = jnp.einsum('gnk,lgk->lgn', br, u_seq)
        bu_im = jnp.einsum('gnk,lgk->lgn', bi, u_seq)
        ar_seq = jnp.broadcast_to(a_re, bu_re.shape)
        ai_seq = jnp.broadcast_to(a_im, bu_im.shape)
        _, _, xr, xi = lax.associative_scan(combine, (ar_seq, ai_seq, bu_re, bu_im), axis=0)
        return jnp.einsum('gkn,lgn->lgk', cr, xr) - jnp.einsum('gkn,lgn->lgk', ci, xi)

    y = lax.map(scan_sequence, u)
    y = y + d_skip.astype(f32).reshape(SSM_GROUPS, SSM_GROUP) * u
    z = jax.nn.gelu(y.reshape(bsz, seq, D_MODEL)).astype(h.dtype)
    val, gate = jnp.split(z @ w_glu, 2, axis=-1)
    return val * jax.nn.sigmoid(gate)

def rope_tables(positions):
    inv_freq = ROPE_THETA ** (-jnp.arange(0, QK_ROPE_DIM, 2, dtype=jnp.float32) / QK_ROPE_DIM)
    ang = positions.astype(jnp.float32)[..., None] * inv_freq
    return jnp.cos(ang), jnp.sin(ang)

def apply_rope(x, cos, sin):
    x1, x2 = jnp.split(x.astype(jnp.float32), 2, axis=-1)
    return jnp.concatenate([x1 * cos - x2 * sin, x1 * sin + x2 * cos], axis=-1).astype(x.dtype)

def mla_shared_kv(h, w_kv_a, kv_a_norm, w_kv_b, k_nope_norm, k_rope_norm, cos, sin):
    bsz, seq, _ = h.shape
    ckv = h @ w_kv_a
    c_kv = rms_norm(ckv[..., :KV_LORA_RANK], kv_a_norm)
    k_rope = apply_rope(rms_norm(ckv[..., KV_LORA_RANK:], k_rope_norm), cos, sin)
    kv = (c_kv @ w_kv_b).reshape(bsz, seq, N_HEADS, QK_NOPE_DIM + V_DIM)
    k_nope = rms_norm(kv[..., :QK_NOPE_DIM], k_nope_norm)
    v = kv[..., QK_NOPE_DIM:]
    k_rope = jnp.broadcast_to(k_rope[:, :, None, :], (bsz, seq, N_HEADS, QK_ROPE_DIM))
    k = jnp.concatenate([k_nope, k_rope], axis=-1)
    return k.transpose(0, 2, 1, 3), v.transpose(0, 2, 1, 3)

def mla_queries(h, w_q_a, q_a_norm, w_q_b, q_nope_norm, q_rope_norm, cos, sin):
    bsz, seq, _ = h.shape
    c_q = rms_norm(h @ w_q_a, q_a_norm)
    q = (c_q @ w_q_b).reshape(bsz, seq, N_HEADS, QK_DIM)
    q_nope = rms_norm(q[..., :QK_NOPE_DIM], q_nope_norm)
    q_rope = apply_rope(rms_norm(q[..., QK_NOPE_DIM:], q_rope_norm),
                        cos[:, :, None, :], sin[:, :, None, :])
    return jnp.concatenate([q_nope, q_rope], axis=-1).transpose(0, 2, 1, 3)

def causal_block_attention(q, k, v):
    bsz, n_heads, seq, dk = q.shape
    dv = v.shape[-1]
    n_blocks = seq // Q_BLOCK
    q_blocks = q.reshape(bsz, n_heads, n_blocks, Q_BLOCK, dk).transpose(2, 0, 1, 3, 4)
    scale = 1.0 / math.sqrt(dk)
    key_pos = jnp.arange(seq)

    def one_block(args):
        q_blk, blk_idx = args
        s = jnp.einsum('bhqd,bhkd->bhqk', q_blk, k).astype(jnp.float32) * scale
        query_pos = blk_idx * Q_BLOCK + jnp.arange(Q_BLOCK)
        s = jnp.where(key_pos[None, :] <= query_pos[:, None], s, NEG_INF)
        p = jax.nn.softmax(s, axis=-1).astype(v.dtype)
        return jnp.einsum('bhqk,bhkd->bhqd', p, v)

    o = lax.map(one_block, (q_blocks, jnp.arange(n_blocks)))
    return o.transpose(1, 2, 0, 3, 4).reshape(bsz, n_heads, seq, dv)

def second_inputs(seed: int = 0) -> dict:
    key = jax.random.key(seed)
    ks = jax.random.split(key, 32)
    f32 = jnp.float32

    def dense(k, shape, fan_in):
        return jax.random.normal(k, shape, f32) * fan_in ** -0.5

    def gain(k, shape):
        return 1.0 + 0.02 * jax.random.normal(k, shape, f32)

    na, nb = N_A_LAYERS, N_B_LAYERS
    g, n, kk = SSM_GROUPS, SSM_STATE, SSM_GROUP
    x = jax.random.normal(ks[0], (BATCH, SEQ, D_MODEL), f32)
    positions = (jnp.arange(SEQ, dtype=jnp.int32)[None, :]
                 + jax.random.randint(ks[1], (BATCH, 1), 0, SEQ, dtype=jnp.int32))
    mix_norm = gain(ks[2], (DEPTH_2, D_MODEL))
    ffn_norm = gain(ks[3], (DEPTH_2, D_MODEL))
    ffn_w_gate_up = dense(ks[4], (DEPTH_2, D_MODEL, 2 * D_FF_2), D_MODEL)
    ffn_w_down = dense(ks[5], (DEPTH_2, D_FF_2, D_MODEL), D_FF_2)
    ssm_w_in = dense(ks[6], (na, D_MODEL, D_MODEL), D_MODEL)
    ssm_lambda_re = -0.5 + 0.01 * jax.random.normal(ks[7], (na, g, n), f32)
    ssm_lambda_im = (jnp.pi * jnp.arange(n, dtype=f32)
                     + 0.01 * jax.random.normal(ks[8], (na, g, n), f32))
    ssm_log_step = jax.random.uniform(ks[9], (na, g), f32,
                                      minval=math.log(STEP_MIN), maxval=math.log(STEP_MAX))
    ssm_b_re = dense(ks[10], (na, g, n, kk), 2 * kk)
    ssm_b_im = dense(ks[11], (na, g, n, kk), 2 * kk)
    ssm_c_re = dense(ks[12], (na, g, kk, n), 2 * n)
    ssm_c_im = dense(ks[13], (na, g, kk, n), 2 * n)
    ssm_d = jax.random.normal(ks[14], (na, D_MODEL), f32)
    ssm_w_glu = dense(ks[15], (na, D_MODEL, 2 * D_MODEL), D_MODEL)
    kv_in_norm = gain(ks[16], (D_MODEL,))
    mla_w_kv_a = dense(ks[17], (D_MODEL, KV_LORA_RANK + QK_ROPE_DIM), D_MODEL)
    mla_kv_a_norm = gain(ks[18], (KV_LORA_RANK,))
    mla_w_kv_b = dense(ks[19], (KV_LORA_RANK, N_HEADS * (QK_NOPE_DIM + V_DIM)), KV_LORA_RANK)
    mla_k_nope_norm = gain(ks[20], (QK_NOPE_DIM,))
    mla_k_rope_norm = gain(ks[21], (QK_ROPE_DIM,))
    mla_w_q_a = dense(ks[22], (nb, D_MODEL, Q_LORA_RANK), D_MODEL)
    mla_q_a_norm = gain(ks[23], (nb, Q_LORA_RANK))
    mla_w_q_b = dense(ks[24], (nb, Q_LORA_RANK, N_HEADS * QK_DIM), Q_LORA_RANK)
    mla_q_nope_norm = gain(ks[25], (nb, QK_NOPE_DIM))
    mla_q_rope_norm = gain(ks[26], (nb, QK_ROPE_DIM))
    mla_w_o = dense(ks[27], (nb, N_HEADS * V_DIM, D_MODEL), N_HEADS * V_DIM)
    return {
        'x': x, 'positions': positions,
        'mix_norm': mix_norm, 'ffn_norm': ffn_norm,
        'ffn_w_gate_up': ffn_w_gate_up, 'ffn_w_down': ffn_w_down,
        'ssm_w_in': ssm_w_in, 'ssm_lambda_re': ssm_lambda_re, 'ssm_lambda_im': ssm_lambda_im,
        'ssm_log_step': ssm_log_step, 'ssm_b_re': ssm_b_re, 'ssm_b_im': ssm_b_im,
        'ssm_c_re': ssm_c_re, 'ssm_c_im': ssm_c_im, 'ssm_d': ssm_d, 'ssm_w_glu': ssm_w_glu,
        'kv_in_norm': kv_in_norm, 'mla_w_kv_a': mla_w_kv_a, 'mla_kv_a_norm': mla_kv_a_norm,
        'mla_w_kv_b': mla_w_kv_b, 'mla_k_nope_norm': mla_k_nope_norm,
        'mla_k_rope_norm': mla_k_rope_norm,
        'mla_w_q_a': mla_w_q_a, 'mla_q_a_norm': mla_q_a_norm, 'mla_w_q_b': mla_w_q_b,
        'mla_q_nope_norm': mla_q_nope_norm, 'mla_q_rope_norm': mla_q_rope_norm,
        'mla_w_o': mla_w_o,
    }

def second_block(x, positions, mix_norm, ffn_norm, ffn_w_gate_up, ffn_w_down,
              ssm_w_in, ssm_lambda_re, ssm_lambda_im, ssm_log_step, ssm_b_re, ssm_b_im,
              ssm_c_re, ssm_c_im, ssm_d, ssm_w_glu,
              kv_in_norm, mla_w_kv_a, mla_kv_a_norm, mla_w_kv_b, mla_k_nope_norm,
              mla_k_rope_norm, mla_w_q_a, mla_q_a_norm, mla_w_q_b, mla_q_nope_norm,
              mla_q_rope_norm, mla_w_o):
    bsz, seq, _ = x.shape
    cos, sin = rope_tables(positions)
    k_shared, v_shared = None, None
    for layer in range(DEPTH_2):
        h = rms_norm(x, mix_norm[layer])
        if layer < N_A_LAYERS:
            i = layer
            x = x + s5_mixer(h, ssm_w_in[i], ssm_lambda_re[i], ssm_lambda_im[i], ssm_log_step[i],
                             ssm_b_re[i], ssm_b_im[i], ssm_c_re[i], ssm_c_im[i], ssm_d[i],
                             ssm_w_glu[i])
        else:
            j = layer - N_A_LAYERS
            if j == 0:
                k_shared, v_shared = mla_shared_kv(rms_norm(x, kv_in_norm), mla_w_kv_a,
                                                   mla_kv_a_norm, mla_w_kv_b, mla_k_nope_norm,
                                                   mla_k_rope_norm, cos, sin)
            q = mla_queries(h, mla_w_q_a[j], mla_q_a_norm[j], mla_w_q_b[j],
                            mla_q_nope_norm[j], mla_q_rope_norm[j], cos, sin)
            o = causal_block_attention(q, k_shared, v_shared)
            o = o.transpose(0, 2, 1, 3).reshape(bsz, seq, N_HEADS * V_DIM)
            x = x + o @ mla_w_o[j]
        x = x + swiglu_ffn(rms_norm(x, ffn_norm[layer]), ffn_w_gate_up[layer], ffn_w_down[layer])
    return x


def setup_inputs(seed=0):
    out = dict(first_inputs(seed))
    for name, value in second_inputs(seed + 1).items():
        if name != "x":
            out[name + "_2"] = value
    return out


def reference(
    x, w_in, w_pool, pool_scale, w_out, ln1_g, ln1_b, w_up, conv_w, conv_b, w_down, ln2_g,
    ln2_b, positions_2, mix_norm_2, ffn_norm_2, ffn_w_gate_up_2, ffn_w_down_2, ssm_w_in_2,
    ssm_lambda_re_2, ssm_lambda_im_2, ssm_log_step_2, ssm_b_re_2, ssm_b_im_2, ssm_c_re_2,
    ssm_c_im_2, ssm_d_2, ssm_w_glu_2, kv_in_norm_2, mla_w_kv_a_2, mla_kv_a_norm_2, mla_w_kv_b_2,
    mla_k_nope_norm_2, mla_k_rope_norm_2, mla_w_q_a_2, mla_q_a_norm_2, mla_w_q_b_2,
    mla_q_nope_norm_2, mla_q_rope_norm_2, mla_w_o_2,
):
    x = first_block(
        x, w_in, w_pool, pool_scale, w_out, ln1_g, ln1_b, w_up, conv_w, conv_b, w_down, ln2_g,
        ln2_b,
    )
    return second_block(
        x, positions_2, mix_norm_2, ffn_norm_2, ffn_w_gate_up_2, ffn_w_down_2, ssm_w_in_2,
        ssm_lambda_re_2, ssm_lambda_im_2, ssm_log_step_2, ssm_b_re_2, ssm_b_im_2, ssm_c_re_2,
        ssm_c_im_2, ssm_d_2, ssm_w_glu_2, kv_in_norm_2, mla_w_kv_a_2, mla_kv_a_norm_2,
        mla_w_kv_b_2, mla_k_nope_norm_2, mla_k_rope_norm_2, mla_w_q_a_2, mla_q_a_norm_2,
        mla_w_q_b_2, mla_q_nope_norm_2, mla_q_rope_norm_2, mla_w_o_2,
    )


_drawn_inputs = setup_inputs


def setup_inputs(seed=0):
    import zlib

    import numpy as np

    out = dict(_drawn_inputs(seed))
    spreads = {}
    factors = {'conv_b': 8.0,
     'mix_norm_2': 6.412,
     'ffn_norm_2': 2.838,
     'ssm_lambda_re_2': 8.0,
     'ssm_b_re_2': 3.376,
     'ssm_b_im_2': 3.442,
     'ssm_c_re_2': 3.458,
     'ssm_c_im_2': 3.424,
     'kv_in_norm_2': 8.0,
     'mla_kv_a_norm_2': 8.0,
     'mla_k_nope_norm_2': 8.0,
     'mla_k_rope_norm_2': 8.0,
     'mla_q_a_norm_2': 8.0,
     'mla_q_nope_norm_2': 8.0,
     'mla_q_rope_norm_2': 8.0}
    for name, (base, spread) in spreads.items():
        noise = np.random.default_rng([zlib.crc32(name.encode()), seed]).standard_normal(out[name].shape)
        drawn = base * np.exp(spread * noise) if base else spread * noise
        out[name] = jnp.asarray(drawn.astype(out[name].dtype))
    for name, factor in factors.items():
        out[name] = (out[name] * factor).astype(out[name].dtype)
    return out
```

```python
from contextlib import ExitStack

import numpy as np

import concourse.bass as bass
from concourse import mybir

F = mybir.dt.float32
R = mybir.dt.float32r
I32 = mybir.dt.int32
ALU = mybir.AluOpType
ACT = mybir.ActivationFunctionType
AX = mybir.AxisListType

P = 128
SEQ, D = 512, 1024
TT = SEQ // P
KT = D // P
FF = 2816
FT = FF // P
GROUPS = ((0, 8), (8, 15), (15, 22))
HALF = 512
RH, POOLG = 4, 4
CHUNK = 64
ALPHA = 2.0 ** 0.25
RING = 3
CW = 1024
G, GK, NS = 64, 16, 64
T = P // GK
NC = SEQ // T
GB = 4
NB = G // GB
EB = 16
W_O, P_O, Q_O, M_O, C_O, S_O = 0, 768, 1344, 1856, 2368, 2624
REC = 2880
NH, NOPE, ROPE, VD = 16, 64, 32, 64
QK = NOPE + ROPE
KVR, QR = 256, 384
TWO_PI = 2.0 * np.pi
ROUNDER = 1.5 * 2.0 ** 23
PI2_A = 6.28125
PI2_B = float(np.float32(round((TWO_PI - PI2_A) * 2 ** 21) / 2 ** 21))
PI2_C = float(np.float32(TWO_PI - PI2_A - PI2_B))
PI_IN = float(np.nextafter(np.float32(np.pi), np.float32(0)))
N_CONST, N_PARAM = 16, 12


def constants():
    f8 = np.float64
    c = {}
    c["c_ident"] = np.eye(P, dtype=np.float32)
    inv = (10000.0 ** (-np.arange(0, P, 2, dtype=np.float32) / np.float32(P))).astype(np.float32)
    ang = (np.arange(SEQ, dtype=np.float32)[:, None] * inv[None, :]).astype(np.float32).astype(f8)
    c["c_rope"] = np.stack([np.cos(ang), np.sin(ang)]).astype(np.float32)
    lg = np.log(1.0 - 2.0 ** (-5.0 - np.arange(RH, dtype=f8)))
    j, i = np.arange(P)[:, None], np.arange(SEQ)[None, :]
    seen = (j // CHUNK) <= (i // CHUNK)
    c["c_decay"] = np.stack([np.where(seen, np.exp(g * np.abs(i - j)), 0.0) * P ** -0.5 for g in lg]).astype(np.float32)
    c["c_count"] = np.stack([1.0 / np.minimum(np.arange(1, SEQ + 1), w) for w in (2, 4, 8, 16)]).astype(np.float32)
    c["c_freq"] = (10000.0 ** (-np.arange(0, ROPE, 2, dtype=np.float32) / np.float32(ROPE))).astype(np.float32)
    c["c_mask"] = np.where(np.arange(SEQ)[None, :] <= SEQ - P + np.arange(P)[:, None], 0.0, -1e30).astype(np.float32)
    return c


def program(nc, stop, x, w_in, w_pool, pool_scale, w_out, ln1_g, ln1_b, w_up, conv_w, conv_b, w_down, ln2_g, ln2_b,
            positions_2, mix_norm_2, ffn_norm_2, ffn_w_gate_up_2, ffn_w_down_2, ssm_w_in_2,
            ssm_lambda_re_2, ssm_lambda_im_2, ssm_log_step_2, ssm_b_re_2, ssm_b_im_2, ssm_c_re_2,
            ssm_c_im_2, ssm_d_2, ssm_w_glu_2, kv_in_norm_2, mla_w_kv_a_2, mla_kv_a_norm_2, mla_w_kv_b_2,
            mla_k_nope_norm_2, mla_k_rope_norm_2, mla_w_q_a_2, mla_q_a_norm_2, mla_w_q_b_2,
            mla_q_nope_norm_2, mla_q_rope_norm_2, mla_w_o_2,
            c_ident, c_rope, c_decay, c_count, c_freq, c_mask, out):
    rec_dram = nc.dram_tensor("s5_records", [NB, P, REC], F, kind="Internal").ap()
    with ExitStack() as ctx:
        ctx.enter_context(nc.allow_non_contiguous_dma(reason="small parameter tables"))
        base = (nc.sbuf_base + 31) // 32 * 32
        KB = 1024
        at_now = [base]

        def fixed(name, shape, dt):
            t = nc.alloc_sbuf_tensor_at(name, shape, dt, offset=at_now[0])
            at_now[0] += (int(np.prod(shape[1:])) * 4 + 31) // 32 * 32
            return t

        x_rows = fixed("x_rows", [P, TT, D], F)
        a_hi = fixed("a_hi", [P, KT, SEQ], R)
        a_lo = fixed("a_lo", [P, KT, SEQ], R)
        w_raw = fixed("w_raw", [P, RING, CW], F)
        w_hi = fixed("w_hi", [P, RING, CW], R)
        w_lo = fixed("w_lo", [P, RING, CW], R)
        xh = fixed("xh", [P, 2, D], F)
        ev = fixed("ev", [P, 2, HALF], F)
        ident = fixed("ident", [P, P], F)
        gains = fixed("gains", [P, 5, KT], F)
        kva_g = fixed("kva_g", [P, 2], F)
        qa_g = fixed("qa_g", [P, 3], F)
        cw_c = fixed("cw_c", [P, 3, FT], F)
        cb_c = fixed("cb_c", [P, FT], F)
        ps_c = fixed("ps_c", [P, POOLG], F)
        st = fixed("st", [P, 192], F)
        eps_c = fixed("eps_c", [P, 4], F)
        arena = at_now[0]
        room = nc.sbuf_top - arena

        def scratch(name, shape, dt, kb, extra=0):
            size = int(np.prod(shape[1:])) * 4
            off = int(kb * KB) + extra
            assert off + size <= room, (name, off + size, room)
            return nc.alloc_sbuf_tensor_at(name, shape, dt, offset=arena + off)

        h_hi = scratch("h_hi", [P, 8, SEQ], R, 0)
        h_lo = scratch("h_lo", [P, 8, SEQ], R, 16)
        q_r = scratch("q_r", [P, TT, RH, P], F, 0)
        k_r = scratch("k_r", [P, TT, RH, P], F, 8)
        v_r = scratch("v_r", [P, TT, RH, P], F, 16)
        g_r = scratch("g_r", [P, TT, RH, P], F, 24)
        q_t = scratch("q_t", [P, RH, SEQ], F, 32)
        k_t = scratch("k_t", [P, RH, SEQ], F, 40)
        decay = scratch("decay", [P, RH, SEQ], F, 48)
        PADW = 16
        pool_p = scratch("pool_p", [P, PADW + SEQ], F, 56)
        pool_a = scratch("pool_a", [P, PADW + SEQ], F, 56, 4 * (PADW + SEQ))
        pool_b = scratch("pool_b", [P, PADW + SEQ], F, 84)
        wpool = scratch("wpool", [P, POOLG, P], F, 80)
        rope_c = scratch("rope_c", [P, 2, TT, 64], F, 78)
        rtmp = scratch("rtmp", [P, 2, HALF // 2], F, 84)
        s_t = [scratch(f"s_t{i}", [P, 1280], F, 8 * i) for i in range(2)]
        ln_g = [scratch("ln1_gb", [P, 2, D], F, 32), scratch("ln2_gb", [P, 2, D], F, 62)]
        cnt16 = scratch("cnt16", [P, POOLG, PADW], F, 82)
        b_p = scratch("b_p", [P, 2, G, GK], F, 62)
        c_p = scratch("c_p", [P, 2, G, GK], F, 70)
        c_nat = scratch("c_nat", [P, 2, 8, 2, NS], F, 40)
        lam_nat = scratch("lam_nat", [G, 2, 2, NS], F, 96)
        pri = scratch("pri", [P, 2, T + 1, G], F, 32)
        sm = scratch("sm", [P, 18, G], F, 37)
        bt = scratch("bt", [P, 2, HALF], F, 42)
        pw = scratch("pw", [P, 2, T + 1, G], F, 88)
        turn = scratch("turn", [P, 2, 6, G], F, 92.75)
        r8 = scratch("r8", [P, G], F, 95.75)
        lam = scratch("lam", [P, 3, G], F, 97)
        d_t = scratch("d_t", [GK, G], F, 97.75)
        stage = scratch("stage", [P, M_O], F, 41)
        tmp1 = scratch("tmp1", [P, 576], F, 48.5)
        tmp2 = scratch("tmp2", [P, 576], F, 50.75)
        h_b = scratch("h_b", [P, GB, T, GK], F, 53)
        KPAD = P - GK
        k_s = scratch("k_s", [GK, GB, KPAD + P], F, 55)
        e_t = scratch("e_t", [P, 2, EB, NC], F, 78)
        u_c = scratch("u_c", [NC, G, T, GK], F, 0)
        rec = [scratch(f"rec{i}", [P, REC], F, 32 + 11.25 * i) for i in range(3)]
        u_t = scratch("u_t", [P, 3, GB * NC], F, 66)
        z1 = scratch("z1", [P, GB * NC], F, 69)
        z2 = scratch("z2", [P, GB * NC], F, 70)
        z3 = scratch("z3", [P, GB * NC], F, 71)
        zc = scratch("zc", [P, 2, 2, GB, NC], F, 72)
        y_c = scratch("y_c", [NC, 2, T, P], F, 76)
        sig = scratch("sig", [P, TT, HALF], F, 68)
        q_n = scratch("q_n", [P, TT, NH, QK], F, 0)
        v_n = scratch("v_n", [P, TT, NH, VD], F, 24)
        k_n = scratch("k_n", [P, TT, NH, QK], F, 40)
        ckv = scratch("ckv", [P, TT, KVR + ROPE], F, 64)
        cq = scratch("cq", [P, TT, QR], F, 68.5)
        sq = scratch("sq", [P, NH * QK], F, 75)
        rot = scratch("rot", [P, 2, NH, ROPE // 2], F, 81)
        o_n = nc.alloc_sbuf_tensor_at("o_n", [P, TT, NH * VD], F, offset=base + 32 * KB)
        qk_t = scratch("qk_t", [QK, 2, 2, SEQ], F, 64)
        prob = scratch("prob", [P, 2, SEQ], F, 72)
        p_t = scratch("p_t", [P, TT, SEQ], F, 76)
        hg = scratch("hg", [P, 2 * QK], F, 94)
        mask = scratch("mask", [P, SEQ], F, 92)
        trig = scratch("trig", [P, 2, TT, ROPE // 2], F, 94.75)
        frq = scratch("frq", [P, ROPE // 2], F, 95.25)
        pos_i = scratch("pos_i", [P, TT], I32, 95.5)
        gconv = xh[:, 1, :].rearrange("p (a c) -> p a c", a=2)
        sqs = scratch("sqs", [P, SEQ], F, 84)

        ps = ctx.enter_context(nc.psum_tensor("ps", [P, 8, HALF], F))

        def sem(name):
            return ctx.enter_context(nc.semaphore(name))

        bank_full = [sem(f"bank_full{b}") for b in range(8)]
        bank_free = [sem(f"bank_free{b}") for b in range(8)]
        w_landed = [sem(f"w_landed{b}") for b in range(RING)]
        hi_made = sem("hi_made")
        lo_made = sem("lo_made")
        w_used = sem("w_used")
        ev_ready = sem("ev_ready")
        hi_ready = sem("hi_ready")
        lo_ready = sem("lo_ready")
        xh_ready = sem("xh_ready")
        sq_ready = sem("sq_ready")
        dve_step = sem("dve_step")
        act_step = sem("act_step")
        var_ready = sem("var_ready")
        ln_ready = sem("ln_ready")
        rope_ready = sem("rope_ready")
        pool_ready = sem("pool_ready")
        decayed = sem("decayed")
        ret_raw = sem("ret_raw")
        ret_dev = sem("ret_dev")
        ret_ready = sem("ret_ready")
        tab_dve = sem("tab_dve")
        tab_act = sem("tab_act")
        tables_ready = sem("tables_ready")
        gate_pre = sem("gate_pre")
        gate_conv = sem("gate_conv")
        gate_act = sem("gate_act")
        u_even = sem("u_even")
        zc_ready = sem("zc_ready")
        sig_ready = sem("sig_ready")
        ckv_ready = sem("ckv_ready")
        cq_ready = sem("cq_ready")
        lat_in = sem("lat_in")
        lat_dev = sem("lat_dev")
        sq_made = sem("sq_made")
        sum_made = sem("sum_made")
        dev_made = sem("dev_made")
        qk_rows = sem("qk_rows")
        max_ready = sem("max_ready")
        prob_ready = sem("prob_ready")
        x_in = sem("x_in")
        id_in = sem("id_in")
        c_in = sem("c_in")
        p_in = sem("p_in")
        ln_in = [sem("ln1_in"), sem("ln2_in")]
        m_in = sem("m_in")
        st_out = sem("st_out")
        e_out = sem("e_out")
        k_out = sem("k_out")
        stage_w = sem("stage_w")
        e_w = sem("e_w")
        k_w = sem("k_w")
        rec_in = [sem(f"rec_in{i}") for i in range(3)]
        o_out = sem("o_out")
        last_add = sem("last_add")

        block = ctx.enter_context(nc.Block())

        up_batch = {1: 0, 4: 1, 9: 6, 12: 7, 15: 12, 17: 13, 19: 14}
        down_batch = {(0, 0): (2, 3), (0, 1): (4, 5), (1, 0): (8, 9), (1, 1): (10, 11), (2, 0): (15,)}
        bank_no, freed, free_count = {}, [], [0] * 8
        chunks_at = {}
        chunk_src, chunk_done = [], []

        w_in0, w_out0 = w_in[0], w_out[0]

        def rows_of(w, k0, kn, c0, cn):
            return w[k0 * P:(k0 + kn) * P, c0:c0 + cn].rearrange("(k p) c -> p k c", p=P)

        def pool_out(h):
            return xh[:, h // 2, (h % 2) * HALF:(h % 2) * HALF + HALF]

        @block.tensor
        def _(pe):
            n_split = [0]

            def open_bank(name, freed_by=None):
                i = len(bank_no)
                bank_no[name] = i
                if i >= 8:
                    pe.wait_ge(*freed[i - 8])
                if freed_by is None:
                    free_count[i % 8] += 1
                    freed_by = (bank_free[i % 8], free_count[i % 8])
                freed.append(freed_by)
                return ps[:, i % 8, :]

            def close_bank(name, ins):
                i = bank_no[name]
                ins.then_inc(bank_full[i % 8], 1)
                chunks_at[name] = len(chunk_src)
                return bank_full[i % 8], i // 8 + 1

            def take_chunk(src, kn, cn):
                n = len(chunk_src)
                chunk_src.append((src, kn, cn))
                pe.wait_ge(hi_made, n + 1)
                pe.wait_ge(lo_made, n + 1)
                hi = w_hi[:, n % RING, 0:kn * cn].rearrange("p (k c) -> p k c", k=kn)
                lo = w_lo[:, n % RING, 0:kn * cn].rearrange("p (k c) -> p k c", k=kn)
                return hi, lo

            def chunk_over(ins):
                ins.then_inc(w_used, 1)
                n_plain[0] += 1
                chunk_done.append((w_used, n_plain[0]))

            n_plain = [0]

            def three(bank, wh, wl, xh_, xl_, first, last):
                pe.matmul(bank, wh, xh_, start=first, stop=False)
                pe.matmul(bank, wh, xl_, start=False, stop=False)
                return pe.matmul(bank, wl, xh_, start=False, stop=last)

            def rows_product(stage, w, ah, al, nk, c0, cn, per, row0=0, wait_k=None, between=None):
                stage = stage if isinstance(stage, tuple) else (stage,)
                banks = [open_bank((*stage, t)) for t in range(TT)]
                k = 0
                while k < nk:
                    kn = min(per, nk - k)
                    wh, wl = take_chunk(rows_of(w, row0 + k, kn, c0, cn), kn, cn)
                    for t in range(TT):
                        for kk in range(kn):
                            if wait_k is not None and t == 0:
                                pe.wait_ge(lo_ready, wait_k(k + kk))
                            s = slice(t * P, t * P + P)
                            o = banks[t][:, 0:cn]
                            end = k + kk == nk - 1
                            pe.matmul(o, ah[:, k + kk, s], wh[:, kk, :], start=(k + kk == 0), stop=False)
                            pe.matmul(o, ah[:, k + kk, s], wl[:, kk, :], start=False, stop=False)
                            m = pe.matmul(o, al[:, k + kk, s], wh[:, kk, :], start=False, stop=end)
                            if end:
                                over = close_bank((*stage, t), m)
                    k += kn
                    if k < nk:
                        chunk_over(m)
                    else:
                        chunk_done.append(over)
                    if between:
                        between(k)

            def cols_product(stage, w, c0, freed_by=None):
                b = open_bank(stage, freed_by=freed_by)
                wh, wl = take_chunk(rows_of(w, 0, KT, c0, P), KT, P)
                for k in range(KT):
                    m = three(b, wh[:, k, :], wl[:, k, :], a_hi[:, k, :], a_lo[:, k, :], k == 0, k == KT - 1)
                chunk_done.append(close_bank(stage, m))

            def turn_rows(stage, src, nk, splits=1, ready=None):
                for t in range(TT):
                    if ready:
                        ready(t)
                    k = 0
                    while k < nk:
                        kn = min(4, nk - k)
                        n_split[0] += splits
                        b = open_bank((stage, t, k // 4), freed_by=(ev_ready, n_split[0]))
                        for q in range(kn):
                            m = pe.transpose(b[:, q * P:q * P + P], src(t, k + q), ident[:, :])
                        close_bank((stage, t, k // 4), m)
                        k += kn

            def xh_turn(stage, splits=1):
                def ready(t):
                    n_xh[0] += 1
                    pe.wait_ge(xh_ready, n_xh[0])
                turn_rows(stage, lambda t, k: xh[:, t % 2, k * P:k * P + P], KT, splits, ready)

            n_xh = [0]

            def ffn(stage, wup, wdown, swap, extra=None):
                gate0, val0 = swap
                for g, (f0, f1) in enumerate(GROUPS):
                    base_split = n_split[0]
                    for f in range(f0, f1):
                        n_split[0] += 1
                        cols_product((stage, "gate", f), wup, gate0 + f * P, freed_by=(ev_ready, n_split[0]))
                        cols_product((stage, "val", f), wup, val0 + f * P, freed_by=(ev_ready, n_split[0]))
                        if extra and f in up_batch:
                            extra(up_batch[f])
                    for half in range(2):
                        batches = list(down_batch.get((g, half), ())) if extra else []
                        between = (lambda k: extra(batches.pop(0)) if batches and k in (2, 6) else None)
                        rows_product((stage, "down", g, half), wdown, h_hi, h_lo, f1 - f0, half * HALF, HALF, 2,
                                     row0=f0, wait_k=lambda k: base_split + k + 1, between=between)

            pe.wait_ge(id_in, 16)
            def turn_parameters():
                pe.wait_ge(c_in, 16 * N_CONST)
                pe.wait_ge(p_in, 16 * N_PARAM)
                b = open_bank("lam")
                for i in range(2):
                    m = pe.transpose(b[:, i * G:i * G + G], lam_nat[:, i, :, :].rearrange("g a n -> g (a n)"),
                                     ident[0:G, 0:G])
                close_bank("lam", m)
                for i in range(2):
                    for h in range(2):
                        b = open_bank(("c", i, h))
                        for q in range(4):
                            m = pe.transpose(b[:, q * P:q * P + P],
                                             c_nat[:, i, 4 * h + q, :, :].rearrange("p a n -> p (a n)"), ident[:, :])
                        close_bank(("c", i, h), m)

            pe.wait_ge(x_in, 16)
            turn_rows("x", lambda t, k: x_rows[:, t, k * P:k * P + P], KT)
            pe.wait_ge(lo_ready, n_split[0])
            for i, nm in enumerate("qkvg"):
                if nm == "v" and stop > 1:
                    turn_parameters()
                rows_product(nm, w_in0, a_hi, a_lo, KT, i * HALF, HALF, 2)
            for h in range(RH):
                for nm, src in (("q", q_r), ("k", k_r)):
                    if h == 0:
                        pe.wait_ge(rope_ready, TT)
                    b = open_bank((nm, "t", h))
                    for t in range(TT):
                        m = pe.transpose(b[:, t * P:t * P + P], src[:, t, h, :], ident[:, :])
                    close_bank((nm, "t", h), m)
                cols_product(("p", h), w_in0, 4 * HALF + h * P)
            pe.wait_ge(c_in, 16 * N_CONST)
            for h in range(RH):
                if h == 0:
                    for nm in "qk":
                        for hh in range(RH):
                            pe.wait_ge(*freed[bank_no[(nm, "t", hh)]])
                    pe.wait_ge(*freed[bank_no[("v", TT - 1)]])
                    pe.wait_ge(pool_ready, RH)
                for j in range(TT):
                    b = open_bank(("s", h, j), freed_by=(decayed, TT * h + j + 1))
                    m = pe.matmul(b[:, 0:SEQ - j * P], k_t[:, h, j * P:j * P + P], q_t[:, h, j * P:SEQ],
                                  start=True, stop=True)
                    close_bank(("s", h, j), m)
                pe.wait_ge(decayed, TT * (h + 1))
                b = open_bank(("ret", h))
                for t in range(TT):
                    for j in range(t + 1):
                        off = j * SEQ - P * (j * (j - 1) // 2)
                        m = pe.matmul(b[:, t * P:t * P + P], s_t[h % 2][:, off + (t - j) * P:off + (t - j) * P + P],
                                      v_r[:, j, h, :], start=(j == 0), stop=(j == t))
                close_bank(("ret", h), m)
                n_split[0] += 1
                b = open_bank(("pool", h), freed_by=(ev_ready, n_split[0]))
                m = pe.matmul(b, wpool[:, h, :], pool_out(h), start=True, stop=True)
                close_bank(("pool", h), m)
            for h in range(RH):
                pe.wait_ge(ret_ready, h + 1)
                n_split[0] += 1
                b = open_bank(("ret_t", h), freed_by=(ev_ready, n_split[0]))
                for t in range(TT):
                    m = pe.transpose(b[:, t * P:t * P + P], v_r[:, t, h, :], ident[:, :])
                close_bank(("ret_t", h), m)
            pe.wait_ge(lo_ready, n_split[0])
            for half in range(2):
                rows_product(("w_out", half), w_out0, a_hi, a_lo, KT, half * HALF, HALF, 2)
            if stop == 1:
                return

            def ready_x(t):
                n_xh[0] += 1
                pe.wait_ge(xh_ready, n_xh[0])
            turn_rows("ln1", lambda t, k: x_rows[:, t, k * P:k * P + P], KT, ready=ready_x)
            pe.wait_ge(lo_ready, n_split[0])

            def prepare(f):
                pe.wait_ge(tables_ready, f + 1)
                b = open_bank(("s5w", f))
                for g in range(GB):
                    m = pe.transpose(b[:, g * P:g * P + P], h_b[:, g, :, :].rearrange("p s k -> p (s k)"), ident[:, :])
                close_bank(("s5w", f), m)
                b = open_bank(("s5k", f))
                for g in range(GB):
                    m = pe.matmul(b[0:GK, g * P:g * P + P], h_b[:, g, T - 1, :],
                                  stage[:, P_O + g * 144:P_O + g * 144 + P], start=True, stop=True)
                close_bank(("s5k", f), m)

            ffn("f1", w_up[0], w_down[0], (FF, 0), prepare)
            if stop == 2:
                return

            xh_turn("mix0")
            pe.wait_ge(lo_ready, n_split[0])
            for half in range(2):
                rows_product(("u", half), ssm_w_in_2[0], a_hi, a_lo, KT, half * HALF, HALF, 2)

            def s5_states(b_):
                if b_ == 0:
                    pe.wait_ge(*freed[bank_no[("u", 1, 3)]])
                b = open_bank(("ut", b_))
                for g in range(GB):
                    gg = b_ * GB + g
                    m = pe.transpose(b[:, g * NC:g * NC + NC], u_c[:, gg, :, :].rearrange("c s k -> c (s k)"),
                                     ident[0:NC, 0:NC])
                close_bank(("ut", b_), m)

            def s5_inc(b_):
                i = b_ % 2
                pe.wait_ge(rec_in[b_ % 3], 16 * (b_ // 3 + 1))
                pe.wait_ge(*freed[bank_no[("ut", b_)]])
                b = open_bank(("sv", b_))
                for sw in range(2):
                    for g in range(GB):
                        o = W_O + g * 192 + 64 * sw
                        m = pe.matmul(b[:, sw * 256 + g * NC:sw * 256 + g * NC + NC], rec[b_ % 3][:, o:o + P],
                                      u_t[:, b_ % 3, g * NC:g * NC + NC], start=True, stop=True)
                close_bank(("sv", b_), m)

            def s5_out(b_):
                i = b_ % 2
                pe.wait_ge(zc_ready, b_ + 1)
                b = open_bank(("y", b_))
                for g in range(GB):
                    o = b[0:NC, g * P:g * P + P]
                    pe.matmul(o, u_t[:, b_ % 3, g * NC:g * NC + NC], rec[b_ % 3][:, M_O + g * P:M_O + g * P + P],
                              start=True, stop=False)
                    pe.matmul(o, zc[:, i, 0, g, :], rec[b_ % 3][:, P_O + g * 144 + GK:P_O + g * 144 + 144],
                              start=False, stop=False)
                    m = pe.matmul(o, zc[:, i, 1, g, :], rec[b_ % 3][:, Q_O + g * P:Q_O + g * P + P],
                                  start=False, stop=True)
                close_bank(("y", b_), m)

            def s5_turn_back(k):
                pe.wait_ge(*freed[bank_no[("y", 2 * k + 1)]])
                n_split[0] += 1
                b = open_bank(("zt", k), freed_by=(ev_ready, n_split[0]))
                for s in range(T):
                    m = pe.transpose(b[:, s * NC:s * NC + NC], y_c[:, k % 2, s, :], ident[0:NC, 0:NC])
                close_bank(("zt", k), m)

            s5_states(0)
            for b_ in range(NB):
                if b_ + 1 < NB:
                    s5_states(b_ + 1)
                s5_inc(b_)
                if b_:
                    s5_out(b_ - 1)
                if b_ >= 3 and b_ % 2:
                    s5_turn_back((b_ - 3) // 2)
            s5_out(NB - 1)
            s5_turn_back(KT - 1)
            pe.wait_ge(lo_ready, n_split[0])
            for half in range(2):
                rows_product(("glu_g", half), ssm_w_glu_2[0], a_hi, a_lo, KT, D + half * HALF, HALF, 2)
                rows_product(("glu_v", half), ssm_w_glu_2[0], a_hi, a_lo, KT, half * HALF, HALF, 2)
            if stop == 3:
                return
            xh_turn("ffn0")
            pe.wait_ge(lo_ready, n_split[0])
            ffn("f2", ffn_w_gate_up_2[0], ffn_w_down_2[0], (0, FF))
            if stop == 4:
                return

            xh_turn("mla", splits=2)
            pe.wait_ge(lo_ready, n_split[0])
            rows_product("kv_a", mla_w_kv_a_2, a_hi, a_lo, KT, 0, KVR + ROPE, 2)
            rows_product("q_a", mla_w_q_a_2[0], h_hi, h_lo, KT, 0, QR, 2)

            turn_rows("ckv_t", lambda t, k: ckv[:, t, k * P:k * P + P], KVR // P,
                      ready=lambda t: pe.wait_ge(ckv_ready, t + 1))
            turn_rows("cq_t", lambda t, k: cq[:, t, k * P:k * P + P], QR // P,
                      ready=lambda t: pe.wait_ge(cq_ready, t + 1))
            pe.wait_ge(lo_ready, n_split[0])
            for c in range(4):
                rows_product(("kv_b", c), mla_w_kv_b_2, a_hi, a_lo, KVR // P, c * HALF, HALF, 2)
            for c in range(3):
                rows_product(("q_b", c), mla_w_q_b_2[0], a_hi[:, 2:5, :], a_lo[:, 2:5, :], QR // P, c * HALF, HALF, 2)
            pe.wait_ge(qk_rows, 2 * TT)

            def head_turn(h):
                for i, src in enumerate((q_n, k_n)):
                    b = open_bank(("ht", i, h))
                    for t in range(TT):
                        m = pe.transpose(b[0:QK, t * P:t * P + P], src[:, t, h, :], ident[:, :])
                    close_bank(("ht", i, h), m)

            def head_scores(h):
                pe.wait_ge(*freed[bank_no[("ht", 0, h)]])
                pe.wait_ge(*freed[bank_no[("ht", 1, h)]])
                for t in range(TT):
                    b = open_bank(("sc", h, t), freed_by=(prob_ready, h * TT + t + 1))
                    m = pe.matmul(b[:, 0:(t + 1) * P], qk_t[:, h % 2, 0, t * P:t * P + P],
                                  qk_t[:, h % 2, 1, 0:(t + 1) * P], start=True, stop=True)
                    close_bank(("sc", h, t), m)

            def head_out(h):
                for t in range(TT):
                    pe.wait_ge(prob_ready, h * TT + t + 1)
                    b = open_bank(("pt", h, t))
                    for j in range(t + 1):
                        m = pe.transpose(b[:, j * P:j * P + P], prob[:, t % 2, j * P:j * P + P], ident[:, :])
                    close_bank(("pt", h, t), m)
                b = open_bank(("o", h))
                for t in range(TT):
                    pe.wait_ge(*freed[bank_no[("pt", h, t)]])
                    for j in range(t + 1):
                        m = pe.matmul(b[:, t * VD:t * VD + VD], p_t[:, t, j * P:j * P + P], v_n[:, j, h, :],
                                      start=(j == 0), stop=(j == t))
                close_bank(("o", h), m)

            head_turn(0)
            for h in range(NH):
                head_scores(h)
                if h + 1 < NH:
                    head_turn(h + 1)
                head_out(h)
            pe.wait_ge(*freed[bank_no[("o", NH - 1)]])
            turn_rows("o_t", lambda t, k: o_n[:, t, k * P:k * P + P], KT)
            pe.wait_ge(lo_ready, n_split[0])
            for half in range(2):
                rows_product(("w_o", half), mla_w_o_2[0], h_hi, h_lo, KT, half * HALF, HALF, 2)
            if stop == 5:
                return
            xh_turn("ffn1")
            pe.wait_ge(lo_ready, n_split[0])
            ffn("f3", ffn_w_gate_up_2[1], ffn_w_down_2[1], (0, FF))

        def full(eng, name):
            i = bank_no[name]
            eng.wait_ge(bank_full[i % 8], i // 8 + 1)
            return ps[:, i % 8, :]

        def release(name, ins):
            sem_, value = freed[bank_no[name]]
            assert sem_ is bank_free[bank_no[name] % 8]
            ins.then_inc(sem_, 1)
            return sem_, value

        def closed(name):
            i = bank_no[name]
            return bank_full[i % 8], i // 8 + 1

        def tile_split(hi, lo, k0, kn, t):
            s = slice(t * P, t * P + P)
            return (lambda e: e[:, 0:kn * P].rearrange("p (k c) -> p k c", k=kn),
                    hi[:, k0:k0 + kn, s], lo[:, k0:k0 + kn, s])

        def tile_split_s5(k0, t):
            c = slice(t * P // T, (t + 1) * P // T)
            dst = [a[:, k0:k0 + 4, :].rearrange("p k (s c) -> p k s c", s=T)[:, :, :, c] for a in (a_hi, a_lo)]
            return dst

        def ev_s5(e):
            return e.rearrange("p (k c s) -> p k s c", k=4, s=T)

        def turned_back(k):
            return (lambda e: e.rearrange("p (s c) -> p s c", s=T),
                    *[a[:, k, :].rearrange("p (c s) -> p s c", s=T) for a in (a_hi, a_lo)])

        def row_split(hi, lo, k):
            return lambda e: e, hi[:, k, :], lo[:, k, :]

        @block.gpsimd
        def _(pool):
            pool.dma_start(wpool[:, :, :], w_pool[0].rearrange("g c d -> c g d")).then_inc(c_in, 16)
            pool.dma_start(decay[:, :, :], c_decay.rearrange("h j i -> j h i")).then_inc(c_in, 16)
            pool.dma_start(rope_c[:, :, :, :], c_rope.rearrange("a (t p) d -> p a t d", p=P)).then_inc(c_in, 16)
            pool.dma_start(ps_c[:, :], pool_scale[0].rearrange("(g p) -> p g", p=P)).then_inc(c_in, 16)
            pool.dma_start(cnt16[:, :, :], c_count[:, 0:PADW].partition_broadcast(P)).then_inc(c_in, 16)
            cols = ((gains[:, 0, :], mix_norm_2[0]), (gains[:, 1, :], ffn_norm_2[0]), (gains[:, 2, :], kv_in_norm_2),
                    (gains[:, 3, :], mix_norm_2[1]), (gains[:, 4, :], ffn_norm_2[1]), (kva_g[:, :], mla_kv_a_norm_2),
                    (qa_g[:, :], mla_q_a_norm_2[0]), (cb_c[:, :], conv_b[0]))
            for dst, src in cols:
                pool.dma_start(dst, src.rearrange("(k p) -> p k", p=P)).then_inc(c_in, 16)
            for j in range(3):
                pool.dma_start(cw_c[:, j, :], conv_w[0, j].rearrange("(k p) -> p k", p=P)).then_inc(c_in, 16)

            def load_parameters():
                for i, src in enumerate((ssm_lambda_re_2, ssm_lambda_im_2)):
                    for a in range(2):
                        pool.dma_start(lam_nat[:, i, a, :], src[0]).then_inc(p_in, 16)
                for i, src in enumerate((ssm_c_re_2, ssm_c_im_2)):
                    v = src[0].rearrange("(h g) k n -> (g k) h n", g=8)
                    for a in range(2):
                        pool.dma_start(c_nat[:, i, :, a, :], v).then_inc(p_in, 16)
                pool.dma_start(lam[:, 2, :], ssm_log_step_2.to_broadcast([P, G])).then_inc(p_in, 16)
                for i, src in enumerate((ssm_b_re_2, ssm_b_im_2)):
                    pool.dma_start(b_p[0:NS, i, :, :], src[0].rearrange("g n k -> n g k")).then_inc(p_in, 16)
                pool.dma_start(d_t[:, :], ssm_d_2[0].rearrange("(g k) -> k g", g=G)).then_inc(p_in, 16)

            for n, (_, kn, cn) in enumerate(chunk_src):
                w = kn * cn
                if n == 3 and stop > 1:
                    load_parameters()
                pool.wait_ge(hi_made, n + 1)
                if n >= RING:
                    pool.wait_ge(*chunk_done[n - RING])
                pool.tensor_tensor(w_lo[:, n % RING, 0:w], w_raw[:, n % RING, 0:w],
                                   w_hi[:, n % RING, 0:w].bitcast(F), ALU.subtract).then_inc(lo_made, 1)

        end_waits = []
        last_bank = {1: ("w_out", 1), 2: None, 3: ("glu_v", 1), 4: ("f2", "down", 2, 1), 5: ("w_o", 1),
                     9: ("f3", "down", 2, 1)}[stop]

        @block.sync
        def _(sp):
            sp.dma_start(x_rows[:, :, :], x[0].rearrange("(t p) d -> p t d", p=P)).then_inc(x_in, 16)

            def store_batch(f):
                sp.wait_ge(stage_w, f + 1)
                sp.dma_start(rec_dram[f, :, 0:M_O], stage[:, :]).then_inc(st_out, 16)
                sp.wait_ge(k_w, f + 1)
                for s in range(T):
                    o = KPAD - GK * s
                    sp.dma_start(rec_dram[f, GK * s:GK * s + GK, M_O:C_O].rearrange("p (g c) -> p g c", g=GB),
                                 k_s[:, :, o:o + P]).then_inc(k_out, 16)
                if f % (EB // GB) == 0:
                    sp.wait_ge(e_w, f * GB // EB + 1)
                    for i in range(EB // GB):
                        sp.dma_start(rec_dram[f + i, :, C_O:REC].rearrange("p (a g c) -> p a g c", a=2, g=GB),
                                     e_t[:, :, GB * i:GB * i + GB, :]).then_inc(e_out, 16)

            for n, (src, kn, cn) in enumerate(chunk_src):
                if n >= RING:
                    sp.wait_ge(hi_made, n - RING + 1)
                    sp.wait_ge(lo_made, n - RING + 1)
                sp.dma_start(w_raw[:, n % RING, 0:kn * cn].rearrange("p (k c) -> p k c", k=kn), src)\
                  .then_inc(w_landed[n % RING], 16)
                if stop >= 2:
                    for f in range(NB):
                        if chunks_at[("s5k", f)] + RING == n:
                            store_batch(f)
            if stop == 2:
                sp.wait_ge(ln_ready, TT)
            else:
                for t in range(TT):
                    sp.wait_ge(*freed[bank_no[(*last_bank, t)]])
            if stop >= 2:
                sp.wait_ge(st_out, 16 * NB)
                sp.wait_ge(k_out, 16 * NB * T)
                sp.wait_ge(e_out, 16 * NB)
            sp.dma_start(out[0].rearrange("(t p) d -> p t d", p=P), x_rows[:, :, :]).then_inc(o_out, 16)
            sp.wait_ge(o_out, 16)

        @block.scalar
        def _(act):
            made = [0]

            def ahead(count):
                while made[0] < min(count + RING, len(chunk_src)):
                    n = made[0]
                    _, kn, cn = chunk_src[n]
                    w = kn * cn
                    act.wait_ge(w_landed[n % RING], 16 * (n // RING + 1))
                    if n >= RING:
                        act.wait_ge(*chunk_done[n - RING])
                    act.activation(w_hi[:, n % RING, 0:w], w_raw[:, n % RING, 0:w], ACT.Copy).then_inc(hi_made, 1)
                    made[0] += 1

            def at(name):
                ahead(chunks_at[name])
                return full(act, name)

            steps, splits = [0], [0]

            def step(ins):
                ins.then_inc(act_step, 1)
                steps[0] += 1
                act.wait_ge(act_step, steps[0])

            def split(name, view, hi, lo):
                ahead(chunks_at[name])
                i = splits[0]
                act.wait_ge(ev_ready, i + 1)
                act.activation(hi, view(ev[:, i % 2, :]), ACT.Copy).then_inc(hi_ready, 1)
                splits[0] += 1

            def split_rows(stage, nk=KT, hi=a_hi, lo=a_lo, off=0):
                for t in range(TT):
                    for k in range(0, nk, 4):
                        kn = min(4, nk - k)
                        split((stage, t, k // 4), *tile_split(hi, lo, off + k, kn, t))

            def rms_and_split(stage, added, ready, tile_splits):
                def deviation(t):
                    ahead(chunks_at[added(t)])
                    act.wait_ge(*ready(t))
                    if t >= 2:
                        act.wait_ge(*closed((stage, t - 2, 1)))
                    step(act.activation(xh[:, t % 2, :], x_rows[:, t, :], ACT.Square, accum_out=st[:, t:t + 1]))
                    act.activation(st[:, 4 + t:5 + t], st[:, t:t + 1], ACT.Sqrt, scale=1.0 / D,
                                   bias=eps_c[:, 1:2]).then_inc(sq_ready, 1)

                deviation(0)
                for t in range(TT):
                    if t + 1 < TT:
                        deviation(t + 1)
                    for k in range(2):
                        for dst in tile_splits(t, k):
                            split((stage, t, k), *dst)

            def bank_ready(added):
                return lambda t: freed[bank_no[added(t)]]

            def to_a(t, k):
                return [tile_split(a_hi, a_lo, 4 * k, 4, t)]

            def to_a_and_h(t, k):
                return [tile_split(a_hi, a_lo, 4 * k, 4, t), tile_split(h_hi, h_lo, 4 * k, 4, t)]

            def to_a_s5(t, k):
                return [(ev_s5, *tile_split_s5(4 * k, t))]

            def ffn(stage, swish_from_conv):
                ft = 0
                for g, (f0, f1) in enumerate(GROUPS):
                    for f in range(f0, f1):
                        b = at((stage, "gate", f))
                        if swish_from_conv:
                            if f >= 1:
                                act.wait_ge(gate_conv, f)
                            step(act.activation(gbuf[:, 2:2 + SEQ], b, ACT.Copy))
                            act.activation(gconv[:, f % 2, :], b, ACT.Identity, scale=cw_c[:, 2, f:f + 1],
                                           bias=cb_c[:, f:f + 1]).then_inc(gate_pre, 1)
                            act.wait_ge(gate_conv, f + 1)
                            act.activation(gconv[:, f % 2, :], gconv[:, f % 2, :], ACT.Silu).then_inc(gate_act, 1)
                        else:
                            if f >= 2:
                                act.wait_ge(ev_ready, ev0[0] + f - 1)
                            act.activation(xh[:, f % 2, 0:SEQ], b, ACT.Silu).then_inc(gate_act, 1)
                        split((stage, "val", f), *row_split(h_hi, h_lo, f - f0))

            ev0 = [0]
            act.dma_start(ident[:, :], c_ident).then_inc(id_in, 16)
            split_rows("x")
            if stop > 1:
                ahead(chunks_at["lam"])
                act.wait_ge(*closed(("c", 1, 1)))
                act.wait_ge(p_in, 16 * N_PARAM)
                act.activation(sm[:, 0, :], lam[:, 2, :], ACT.Exp).then_inc(tab_act, 1)
                act.wait_ge(tab_dve, 1)
                act.activation(sm[:, 3, :], sm[:, 1, :], ACT.Exp).then_inc(tab_act, 1)
                act.wait_ge(tab_dve, 2)
                act.activation(sm[:, 7, :], sm[:, 5, :], ACT.Sin).then_inc(tab_act, 1)
                act.activation(sm[:, 8, :], sm[:, 6, :], ACT.Sin).then_inc(tab_act, 1)
            for t in range(TT):
                release(("v", t), act.activation(v_r[:, t, :, :].rearrange("p h e -> p (h e)"), at(("v", t)), ACT.Copy))
            for t in range(TT):
                release(("g", t), act.activation(g_r[:, t, :, :].rearrange("p h e -> p (h e)"), at(("g", t)), ACT.Silu))
            for h in range(RH):
                ahead(chunks_at[("ret", h)])
                act.wait_ge(ret_raw, h + 1)
                act.activation(st[:, 16 + 4 * h:20 + 4 * h], st[:, 4 * h:4 * h + 4], ACT.Sqrt, scale=1.0 / P,
                               bias=eps_c[:, 1:2]).then_inc(ret_dev, 1)
                split(("pool", h), *row_split(a_hi, a_lo, RH + h))
            act.wait_ge(*closed(("ret", RH - 1)))
            for i, src in enumerate((ln1_g, ln1_b)):
                act.dma_start(ln_g[0][:, i, :], src.to_broadcast([P, D])).then_inc(ln_in[0], 16)
            for h in range(RH):
                split(("ret_t", h), *row_split(a_hi, a_lo, h))
            if stop == 1:
                ahead(len(chunk_src))
                act.wait_ge(ln_in[0], 32)
                return

            def ln_rows(added, first):
                for t in range(TT):
                    ahead(chunks_at[added(t)])
                    act.wait_ge(var_ready, first + t + 1)
                    act.activation(st[:, 36 + t:37 + t], st[:, 24 + 2 * t + 1:24 + 2 * t + 2], ACT.Sqrt,
                                   bias=eps_c[:, 0:1]).then_inc(sq_ready, 1)

            ln_rows(lambda t: ("w_out", 1, t), 0)
            split_rows("ln1")
            gbuf = xh[:, 0, 0:SEQ + 2]
            ffn("f1", True)
            act.wait_ge(tables_ready, NB)
            for i, src in enumerate((ln2_g, ln2_b)):
                act.dma_start(ln_g[1][:, i, :], src.to_broadcast([P, D])).then_inc(ln_in[1], 16)
            if stop == 2:
                ahead(len(chunk_src))
            ln_rows(lambda t: ("f1", "down", 2, 1, t), TT)
            if stop == 2:
                return

            act.wait_ge(st_out, 16 * NB)
            act.wait_ge(k_out, 16 * NB * T)
            act.wait_ge(e_out, 16 * NB)

            def load_rec(b_):
                act.dma_start(rec[b_ % 3][:, :], rec_dram[b_]).then_inc(rec_in[b_ % 3], 16)

            load_rec(0)
            load_rec(1)
            for dst, src in ((hg[:, 0:64], mla_k_nope_norm_2), (hg[:, 64:96], mla_k_rope_norm_2),
                             (hg[:, 96:160], mla_q_nope_norm_2[0]), (hg[:, 160:192], mla_q_rope_norm_2[0]),
                             (frq[:, :], c_freq)):
                act.dma_start(dst, src.partition_broadcast(P)).then_inc(m_in, 16)
            act.dma_start(mask[:, :], c_mask).then_inc(m_in, 16)
            act.dma_start(pos_i[:, :], positions_2[0].rearrange("(t p) -> p t", p=P)).then_inc(m_in, 16)
            rms_and_split("mix0", lambda t: ("f1", "down", 2, 1, t), lambda t: (ln_ready, t + 1), to_a_s5)
            load_rec(2)
            for half in range(2):
                for j in range(4):
                    b = at(("u", half, j))
                    act.wait_ge(u_even, 4 * half + j + 1)
                    release(("u", half, j), act.activation(u_c[:, 32 * half:32 * half + 32, 2 * j + 1, :],
                                                           b[NC:P, :].rearrange("c (g k) -> c g k", k=GK), ACT.Copy))

            def s5_turned(b_):
                if b_ >= 3:
                    act.wait_ge(*closed(("y", b_ - 3)))
                release(("ut", b_), act.activation(u_t[:, b_ % 3, :], at(("ut", b_))[:, 0:GB * NC], ACT.Copy))

            def s5_gelu(b_):
                y = at(("y", b_))[0:NC, :].rearrange("c (g t k) -> c t g k", g=GB, t=T)
                k, j = divmod(b_, 2)
                if j == 0 and k >= 2:
                    act.wait_ge(*closed(("zt", k - 2)))
                o = y_c[:, k % 2, :, 64 * j:64 * j + 64].rearrange("c t (g k) -> c t g k", g=GB)
                release(("y", b_), act.activation(o, y, ACT.Gelu_apprx_tanh))
                if b_ + 3 < NB:
                    load_rec(b_ + 3)

            s5_turned(0)
            for b_ in range(NB):
                if b_ + 1 < NB:
                    s5_turned(b_ + 1)
                if b_:
                    s5_gelu(b_ - 1)
                if b_ >= 3 and b_ % 2:
                    split(("zt", (b_ - 3) // 2), *turned_back((b_ - 3) // 2))
            s5_gelu(NB - 1)
            split(("zt", KT - 1), *turned_back(KT - 1))
            for half in range(2):
                for t in range(TT):
                    b = at(("glu_g", half, t))
                    if half:
                        act.wait_ge(*freed[bank_no[("glu_v", 0, t)]])
                    release(("glu_g", half, t), act.activation(sig[:, t, :], b, ACT.Sigmoid))
                ahead(chunks_at[("glu_v", half, TT - 1)])
            if stop == 3:
                return
            added = lambda t: ("glu_v", 1, t)
            rms_and_split("ffn0", added, bank_ready(added), to_a)
            ev0[0] = splits[0]
            ffn("f2", False)
            if stop == 4:
                ahead(len(chunk_src))
                return

            added = lambda t: ("f2", "down", 2, 1, t)
            rms_and_split("mla", added, bank_ready(added), to_a_and_h)
            act.wait_ge(tab_dve, 3)
            act.activation(trig[:, 1, :, :], rot[:, 0, 0:TT, :], ACT.Sin).then_inc(tab_act, 1)
            act.activation(trig[:, 0, :, :], rot[:, 1, 0:TT, :], ACT.Sin).then_inc(tab_act, 1)
            for t in range(TT):
                ahead(chunks_at[("kv_a", t)])
                act.wait_ge(lat_in, t + 1)
                step(act.activation(sq[:, 0:KVR], ckv[:, t, 0:KVR], ACT.Square, accum_out=st[:, 2 * t:2 * t + 1]))
                step(act.activation(sq[:, 0:ROPE], ckv[:, t, KVR:], ACT.Square, accum_out=st[:, 2 * t + 1:2 * t + 2]))
                step(act.activation(st[:, 8 + 2 * t:9 + 2 * t], st[:, 2 * t:2 * t + 1], ACT.Sqrt, scale=1.0 / KVR,
                                    bias=eps_c[:, 1:2]))
                act.activation(st[:, 9 + 2 * t:10 + 2 * t], st[:, 2 * t + 1:2 * t + 2], ACT.Sqrt, scale=1.0 / ROPE,
                               bias=eps_c[:, 1:2]).then_inc(lat_dev, 1)
            for t in range(TT):
                ahead(chunks_at[("q_a", t)])
                act.wait_ge(lat_in, TT + t + 1)
                step(act.activation(sq[:, 0:QR], cq[:, t, :], ACT.Square, accum_out=st[:, 32 + t:33 + t]))
                act.activation(st[:, 40 + t:41 + t], st[:, 32 + t:33 + t], ACT.Sqrt, scale=1.0 / QR,
                               bias=eps_c[:, 1:2]).then_inc(lat_dev, 1)
            split_rows("ckv_t", KVR // P)
            split_rows("cq_t", QR // P, off=2)
            for c in range(4):
                for t in range(TT):
                    b = at(("kv_b", c, t)).rearrange("p (h e) -> p h e", h=4)
                    step(act.activation(k_n[:, t, 4 * c:4 * c + 4, 0:NOPE], b[:, :, 0:NOPE], ACT.Copy))
                    release(("kv_b", c, t), act.activation(v_n[:, t, 4 * c:4 * c + 4, :], b[:, :, NOPE:], ACT.Copy))
            for c in range(3):
                for t in range(TT):
                    b = at(("q_b", c, t))
                    o = q_n[:, t, :, :].rearrange("p h e -> p (h e)")[:, c * HALF:c * HALF + HALF]
                    release(("q_b", c, t), act.activation(o, b, ACT.Copy))
            sq_k = sq[:, 0:NH * NOPE].rearrange("p (h e) -> p h e", h=NH)
            sq_q = sq[:, :].rearrange("p (h e) -> p h e", h=NH)
            n = 0
            for which in range(2):
                for t in range(TT):
                    if n:
                        act.wait_ge(sum_made, n)
                    if which == 0:
                        act.wait_ge(*freed[bank_no[("kv_b", 3, t)]])
                        act.activation(sq_k, k_n[:, t, :, 0:NOPE], ACT.Square).then_inc(sq_made, 1)
                    else:
                        act.wait_ge(*freed[bank_no[("q_b", 2, t)]])
                        act.activation(sq_q, q_n[:, t, :, :], ACT.Square).then_inc(sq_made, 1)
                    act.wait_ge(sum_made, n + 1)
                    o = st[:, 96:112]
                    if which:
                        step(act.activation(st[:, 112:128], st[:, 80:96], ACT.Sqrt, scale=1.0 / ROPE,
                                            bias=eps_c[:, 1:2]))
                    act.activation(o, st[:, 64:80], ACT.Sqrt, scale=1.0 / NOPE,
                                   bias=eps_c[:, 1:2]).then_inc(dev_made, 1)
                    n += 1

            def q_turned(h):
                release(("ht", 0, h), act.activation(qk_t[:, h % 2, 0, :], full(act, ("ht", 0, h))[0:QK, :], ACT.Copy))

            ahead(chunks_at[("ht", 0, 0)])
            q_turned(0)
            for h in range(NH):
                for t in range(TT):
                    i = h * TT + t
                    act.wait_ge(max_ready, i + 1)
                    if i >= 2:
                        act.wait_ge(*closed(("pt", (i - 2) // TT, (i - 2) % TT)))
                    b = full(act, ("sc", h, t))
                    act.activation(prob[:, t % 2, 0:(t + 1) * P], b[:, 0:(t + 1) * P], ACT.Exp, scale=-1.0,
                                   bias=st[:, 8 * (h % 2) + t:8 * (h % 2) + t + 1],
                                   accum_out=st[:, 16 + 8 * (h % 2) + t:17 + 8 * (h % 2) + t]).then_inc(prob_ready, 1)
                    if t == 1 and h + 1 < NH:
                        q_turned(h + 1)
            split_rows("o_t", hi=h_hi, lo=h_lo)
            if stop == 5:
                ahead(len(chunk_src))
                return
            added = lambda t: ("w_o", 1, t)
            rms_and_split("ffn1", added, bank_ready(added), to_a)
            ev0[0] = splits[0]
            ffn("f3", False)
            ahead(len(chunk_src))

        @block.vector
        def _(v):
            steps, splits, added = [0], [0], [0]
            pending = []

            def step(ins):
                ins.then_inc(dve_step, 1)
                steps[0] += 1
                v.wait_ge(dve_step, steps[0])

            def go(ins):
                ins.then_inc(dve_step, 1)
                steps[0] += 1

            def settle():
                v.wait_ge(dve_step, steps[0])

            def finish_split():
                if pending:
                    i, view, hi, lo = pending.pop()
                    v.wait_ge(hi_ready, i + 1)
                    v.tensor_tensor(lo, view(ev[:, i % 2, :]), hi.bitcast(F), ALU.subtract).then_inc(lo_ready, 1)

            def split(name, write, view, hi, lo):
                i = splits[0]
                b = full(v, name)
                if i >= 2:
                    v.wait_ge(lo_ready, i - 1)
                write(b, ev[:, i % 2, :]).then_inc(ev_ready, 1)
                finish_split()
                pending.append((i, view, hi, lo))
                splits[0] += 1

            def scaled(gain, kn=4):
                def write(b, e):
                    r = lambda a: a[:, 0:kn * P].rearrange("p (k c) -> p k c", k=kn)
                    g = gain.unsqueeze(2).to_broadcast([P, kn, P])
                    return v.tensor_tensor(r(e), r(b), g, ALU.mult)
                return write

            def copied(w):
                return lambda b, e: v.tensor_copy(e[:, 0:w], b[:, 0:w])

            def split_rows(stage, nk=KT, gain=None, hi=a_hi, lo=a_lo, off=0):
                for t in range(TT):
                    for k in range(0, nk, 4):
                        kn = min(4, nk - k)
                        wr = scaled(gain[:, k:k + kn], kn) if gain is not None else copied(kn * P)
                        split((stage, t, k // 4), wr, *tile_split(hi, lo, off + k, kn, t))
                finish_split()

            def xh_rows(first, t):
                v.wait_ge(sq_ready, first + t + 1)
                step(v.reciprocal(st[:, 8 + t:9 + t], st[:, 4 + t:5 + t]))
                v.tensor_scalar(xh[:, t % 2, :], x_rows[:, t, :], st[:, 8 + t:9 + t], None, ALU.mult)\
                 .then_inc(xh_ready, 1)

            def rms_and_split(stage, first, tile_splits):
                xh_rows(first, 0)
                for t in range(TT):
                    if t + 1 < TT:
                        xh_rows(first, t + 1)
                    for k in range(2):
                        for write, dst in tile_splits(t, k):
                            split((stage, t, k), write, *dst)
                finish_split()

            def to_a(gain):
                return lambda t, k: [(scaled(gain[:, 4 * k:4 * k + 4]), tile_split(a_hi, a_lo, 4 * k, 4, t))]

            def add_rows(name, half, scale=None):
                for t in range(TT):
                    b = full(v, (*name, t))
                    o = x_rows[:, t, half * HALF:half * HALF + HALF]
                    if scale is None:
                        ins = v.tensor_tensor(o, b, o, ALU.add)
                    else:
                        ins = v.scalar_tensor_tensor(o, o, scale, b, ALU.mult, ALU.add)
                    last[t] = release((*name, t), ins)

            last = [None] * TT

            def ln_stats(t):
                v.wait_ge(*last[t])
                for c in range(2):
                    go(v.bn_stats(st[:, 48 + 6 * c:54 + 6 * c], x_rows[:, t, c * HALF:c * HALF + HALF]))
                settle()
                v.bn_aggr(st[:, 24 + 2 * t:26 + 2 * t], st[:, 48:60]).then_inc(var_ready, 1)
                n_var[0] += 1

            n_var = [0]

            def ln_rows(t, i, first, sem_):
                v.wait_ge(ln_in[i], 32)
                v.wait_ge(sq_ready, first + t + 1)
                step(v.reciprocal(st[:, 40 + t:41 + t], st[:, 36 + t:37 + t]))
                o = x_rows[:, t, :]
                step(v.tensor_scalar(o, o, st[:, 24 + 2 * t:25 + 2 * t], st[:, 40 + t:41 + t], ALU.subtract, ALU.mult))
                step(v.tensor_tensor(o, o, ln_g[i][:, 0, :], ALU.mult))
                v.tensor_tensor(o, o, ln_g[i][:, 1, :], ALU.add).then_inc(sem_, 1)

            def layer_norm(i, first, sem_):
                for t in range(TT):
                    ln_stats(t)
                    v.wait_ge(var_ready, n_var[0])
                for t in range(TT):
                    ln_rows(t, i, first, sem_)

            def cmul(o_re, o_im, a_re, a_im, b_re, b_im, t1, t2):
                go(v.tensor_tensor(t1, a_re, b_re, ALU.mult))
                go(v.tensor_tensor(t2, a_im, b_im, ALU.mult))
                go(v.tensor_tensor(o_re, a_re, b_im, ALU.mult))
                go(v.tensor_tensor(o_im, a_im, b_re, ALU.mult))
                settle()
                go(v.tensor_tensor(o_im, o_im, o_re, ALU.add))
                settle()
                step(v.tensor_tensor(o_re, t1, t2, ALU.subtract))

            def reduced(ang, turns, out_):
                step(v.tensor_scalar(turns, ang, 1.0 / TWO_PI, ROUNDER, ALU.mult, ALU.add))
                step(v.tensor_scalar(turns, turns, ROUNDER, None, ALU.subtract))
                step(v.scalar_tensor_tensor(out_, turns, -PI2_A, ang, ALU.mult, ALU.add))
                step(v.scalar_tensor_tensor(out_, turns, -PI2_B, out_, ALU.mult, ALU.add))
                step(v.scalar_tensor_tensor(out_, turns, -PI2_C, out_, ALU.mult, ALU.add))
                step(v.tensor_scalar(out_, out_, PI_IN, -PI_IN, ALU.min, ALU.max))

            def quarter(out_, ang):
                step(v.scalar_tensor_tensor(out_, ang, -1.0, ang, ALU.mult, ALU.min))
                return v.tensor_scalar(out_, out_, TWO_PI / 4, None, ALU.add)

            def s5_tables():
                v.wait_ge(p_in, 16 * N_PARAM)
                r = release("lam", v.tensor_copy(lam[:, 0:2, :].rearrange("p a g -> p (a g)"), full(v, "lam")[:, 0:P]))
                v.wait_ge(*r)
                for i in range(2):
                    for h in range(2):
                        o = c_p[:, i, 32 * h:32 * h + 32, :].rearrange("p g k -> p (g k)")
                        b = full(v, ("c", i, h))
                        go(v.tensor_copy(o[0:NS], b[0:NS]))
                        r = release(("c", i, h), v.tensor_scalar(o[NS:P], b[NS:P], -1.0, None, ALU.mult))
                v.wait_ge(*r)
                for i in range(2):
                    go(v.tensor_copy(b_p[NS:P, i, :, :], b_p[0:NS, i, :, :]))
                settle()
                lr, li = lam[:, 0, :], lam[:, 1, :]
                s = lambda i: sm[:, i, :]
                v.wait_ge(tab_act, 1)
                step(v.tensor_tensor(s(1), lr, s(0), ALU.mult))
                v.tensor_tensor(s(2), li, s(0), ALU.mult).then_inc(tab_dve, 1)
                v.wait_ge(tab_dve, 1)
                reduced(s(2), s(4), s(5))
                quarter(s(6), s(5)).then_inc(tab_dve, 1)
                v.wait_ge(tab_act, 4)
                sn, cs, r = s(7), s(8), s(3)
                go(v.memset(pri[:, 0, 0, :], 1.0))
                go(v.memset(pri[:, 1, 0, :], 0.0))
                go(v.tensor_tensor(pri[:, 0, 1, :], r, cs, ALU.mult))
                go(v.tensor_tensor(pri[:, 1, 1, :], r, sn, ALU.mult))
                go(v.tensor_copy(s(9), cs))
                go(v.tensor_copy(s(10), sn))
                go(v.tensor_copy(s(11), r))
                settle()
                for _ in range(3):
                    cmul(s(12), s(13), s(9), s(10), s(9), s(10), s(14), s(15))
                    go(v.tensor_copy(s(9), s(12)))
                    go(v.tensor_copy(s(10), s(13)))
                    go(v.tensor_tensor(s(11), s(11), s(11), ALU.mult))
                    settle()
                step(v.tensor_copy(r8[:, :], s(11)))
                go(v.tensor_copy(turn[:, 0, 0, :], s(9)))
                go(v.tensor_copy(turn[:, 1, 0, :], s(10)))
                settle()
                for i in range(5):
                    a, b = turn[:, 0, i, :], turn[:, 1, i, :]
                    cmul(turn[:, 0, i + 1, :], turn[:, 1, i + 1, :], a, b, a, b, s(14), s(15))
                for lo_, n in ((1, 1), (1, 2), (1, 4)):
                    bc = lambda a: pri[:, a, n, :].unsqueeze(1).to_broadcast([P, n, G])
                    t1, t2 = (bt[:, a, 0:n * G].rearrange("p (k g) -> p k g", k=n) for a in range(2))
                    cmul(pri[:, 0, 1 + n:1 + 2 * n, :], pri[:, 1, 1 + n:1 + 2 * n, :],
                         pri[:, 0, 1:1 + n, :], pri[:, 1, 1:1 + n, :], bc(0), bc(1), t1, t2)
                ar, ai = pri[:, 0, 1, :], pri[:, 1, 1, :]
                go(v.tensor_scalar(s(9), ar, 1.0, None, ALU.subtract))
                go(v.tensor_tensor(s(10), lr, lr, ALU.mult))
                go(v.tensor_tensor(s(11), li, li, ALU.mult))
                settle()
                step(v.tensor_tensor(s(10), s(10), s(11), ALU.add))
                go(v.reciprocal(s(11), s(10)))
                go(v.tensor_tensor(s(12), s(9), lr, ALU.mult))
                go(v.tensor_tensor(s(13), ai, li, ALU.mult))
                go(v.tensor_tensor(s(14), ai, lr, ALU.mult))
                go(v.tensor_tensor(s(15), s(9), li, ALU.mult))
                settle()
                go(v.tensor_tensor(s(12), s(12), s(13), ALU.add))
                go(v.tensor_tensor(s(14), s(14), s(15), ALU.subtract))
                settle()
                go(v.tensor_tensor(s(12), s(12), s(11), ALU.mult))
                go(v.tensor_tensor(s(14), s(14), s(11), ALU.mult))
                settle()
                for q in range(2):
                    gs = slice(32 * q, 32 * q + 32)
                    br, bi = b_p[:, 0, gs, :], b_p[:, 1, gs, :]
                    fr, fi = (s(a)[:, gs].unsqueeze(2).to_broadcast([P, 32, GK]) for a in (12, 14))
                    t1, t2 = (bt[:, a, :].rearrange("p (g k) -> p g k", g=32) for a in range(2))
                    go(v.tensor_tensor(t1, bi, fi, ALU.mult))
                    go(v.tensor_tensor(t2, br, fi, ALU.mult))
                    settle()
                    go(v.tensor_tensor(br, br, fr, ALU.mult))
                    go(v.tensor_tensor(bi, bi, fr, ALU.mult))
                    settle()
                    go(v.tensor_tensor(br, br, t1, ALU.subtract))
                    go(v.tensor_tensor(bi, bi, t2, ALU.add))
                    settle()
                top, bot = slice(0, NS), slice(NS, P)
                for i, h, a, sign in ((0, top, 0, 1.0), (0, bot, 1, 1.0), (1, top, 1, -1.0), (1, bot, 0, 1.0)):
                    go(v.tensor_scalar(pw[h, i, :, :], pri[h, a, :, :], sign, None, ALU.mult))
                settle()

            go(v.memset(eps_c[:, 0:1], 1e-5))
            go(v.memset(eps_c[:, 1:2], 1e-6))
            settle()
            split_rows("x")
            v.wait_ge(c_in, 16 * N_CONST)
            for nm, dst in (("q", q_r), ("k", k_r)):
                for t in range(TT):
                    b = full(v, (nm, t)).rearrange("p (h e) -> p h e", h=RH)
                    c_ = rope_c[:, 0, t, :].unsqueeze(1).to_broadcast([P, RH, 64])
                    s_ = rope_c[:, 1, t, :].unsqueeze(1).to_broadcast([P, RH, 64])
                    lo_, hi_ = b[:, :, 0:64], b[:, :, 64:P]
                    r0, r1 = (rtmp[:, a, :].rearrange("p (h e) -> p h e", h=RH) for a in range(2))
                    go(v.tensor_tensor(dst[:, t, :, 0:64], lo_, c_, ALU.mult))
                    go(v.tensor_tensor(dst[:, t, :, 64:P], lo_, s_, ALU.mult))
                    go(v.tensor_tensor(r0, hi_, s_, ALU.mult))
                    settle()
                    w = release((nm, t), v.tensor_tensor(r1, hi_, c_, ALU.mult))
                    go(v.tensor_tensor(dst[:, t, :, 0:64], dst[:, t, :, 0:64], r0, ALU.subtract))
                    v.wait_ge(*w)
                    settle()
                    v.tensor_tensor(dst[:, t, :, 64:P], dst[:, t, :, 64:P], r1, ALU.add)\
                     .then_inc(rope_ready if nm == "k" else dve_step, 1)
                    if nm == "q":
                        steps[0] += 1
                        settle()
                    else:
                        v.wait_ge(rope_ready, t + 1)
            if stop > 1:
                s5_tables()

            for pad in (pool_p, pool_a, pool_b):
                go(v.memset(pad[:, 0:PADW], 0.0))
            settle()
            for h in range(RH):
                for nm, dst in (("q", q_t), ("k", k_t)):
                    i = bank_no[(nm, "t", h)]
                    release((nm, "t", h), v.tensor_copy(dst[:, h, :], full(v, (nm, "t", h))))
                w = release(("p", h), v.tensor_copy(pool_p[:, PADW:], full(v, ("p", h))))
                v.wait_ge(*w)
                src, win = pool_p, 1
                for r in range(h + 1):
                    dst = (pool_a, pool_b)[r % 2]
                    step(v.tensor_tensor(dst[:, PADW:], src[:, PADW:], src[:, PADW - win:PADW - win + SEQ], ALU.add))
                    src, win = dst, 2 * win
                other = (pool_a, pool_b)[(h + 1) % 2]
                go(v.tensor_tensor(other[:, PADW:2 * PADW], src[:, PADW:2 * PADW], cnt16[:, h, :], ALU.mult))
                settle()
                o = pool_out(h)
                go(v.scalar_tensor_tensor(o[:, PADW:], src[:, 2 * PADW:], 1.0 / win, pool_p[:, 2 * PADW:],
                                          ALU.mult, ALU.subtract))
                v.tensor_tensor(o[:, 0:PADW], other[:, PADW:2 * PADW], pool_p[:, PADW:2 * PADW], ALU.subtract)\
                 .then_inc(pool_ready, 1)
                settle()
                v.wait_ge(pool_ready, h + 1)
            for h in range(RH):
                for j in range(TT):
                    n = SEQ - j * P
                    off = j * SEQ - P * (j * (j - 1) // 2)
                    b = full(v, ("s", h, j))
                    v.tensor_tensor(s_t[h % 2][:, off:off + n], b[:, 0:n], decay[:, h, 0:n], ALU.mult)\
                     .then_inc(decayed, 1)
                b = full(v, ("ret", h)).rearrange("p (t e) -> p t e", t=TT)
                vh = v_r[:, :, h, :]
                w = release(("ret", h), v.tensor_copy(vh, b))
                v.wait_ge(*w)
                sqv = sqs[:, :].rearrange("p (t e) -> p t e", t=TT)
                step(v.tensor_tensor(sqv, vh, vh, ALU.mult))
                v.tensor_reduce(st[:, 4 * h:4 * h + 4], sqv, AX.X, ALU.add).then_inc(ret_raw, 1)
                split(("pool", h), lambda b_, e: v.tensor_scalar(e, b_, ps_c[:, h:h + 1], None, ALU.mult),
                      *row_split(a_hi, a_lo, RH + h))
                v.wait_ge(ret_dev, h + 1)
                step(v.reciprocal(st[:, 32:36], st[:, 16 + 4 * h:20 + 4 * h]))
                step(v.tensor_tensor(vh, vh, st[:, 32:36].unsqueeze(2).to_broadcast([P, TT, P]), ALU.mult))
                if h == 0:
                    v.wait_ge(*freed[bank_no[("g", TT - 1)]])
                v.tensor_tensor(vh, vh, g_r[:, :, h, :], ALU.mult).then_inc(ret_ready, 1)
            for h in range(RH):
                split(("ret_t", h), copied(SEQ), *row_split(a_hi, a_lo, h))
            finish_split()
            for half in range(2):
                add_rows(("w_out", half), half, ALPHA)
            if stop == 1:
                return
            layer_norm(0, 0, xh_ready)
            split_rows("ln1")

            def s5_phases(e):
                gs = slice(e * EB, e * EB + EB)
                if e:
                    v.wait_ge(e_out, 16 * e * (EB // GB))
                go(v.memset(e_t[:, 0, :, 0:1], 1.0))
                go(v.memset(e_t[:, 1, :, 0:1], 0.0))
                settle()
                n = 1
                while n < NC:
                    k = n.bit_length() - 1
                    bc = lambda a: turn[:, a, k, gs].unsqueeze(2).to_broadcast([P, EB, n])
                    t1, t2 = (a[:, 0:EB * n].rearrange("p (g c) -> p g c", g=EB) for a in (tmp1, tmp2))
                    cmul(e_t[:, 0, :, n:2 * n], e_t[:, 1, :, n:2 * n], e_t[:, 0, :, 0:n], e_t[:, 1, :, 0:n],
                         bc(0), bc(1), t1, t2)
                    n *= 2
                v.tensor_scalar(e_t[NS:P, 1, :, :], e_t[NS:P, 1, :, :], -1.0, None, ALU.mult).then_inc(e_w, 1)
                v.wait_ge(e_w, e + 1)

            def s5_batch(f):
                gs = slice(f * GB, f * GB + GB)
                t1 = tmp1[:, 0:GB * T * GK].rearrange("p (g s k) -> p g s k", g=GB, s=T)
                if f:
                    v.wait_ge(*closed(("s5k", f - 1)))
                for g in range(GB):
                    gg = f * GB + g
                    for a, o in ((0, h_b[:, g, :, :]), (1, t1[:, g, :, :])):
                        go(v.tensor_tensor(o, b_p[:, a, gg, :].unsqueeze(1).to_broadcast([P, T, GK]),
                                           pw[:, a, T - 1::-1, gg:gg + 1].to_broadcast([P, T, GK]), ALU.mult))
                settle()
                step(v.tensor_tensor(h_b[:, :, :, :].rearrange("p g s k -> p (g s k)"),
                                     h_b[:, :, :, :].rearrange("p g s k -> p (g s k)"), tmp1[:, 0:GB * T * GK], ALU.add))
                if f:
                    v.wait_ge(st_out, 16 * f)
                cp = stage[:, P_O:P_O + GB * 144].rearrange("p (g s k) -> p g s k", g=GB, s=T + 1)
                t2 = tmp2[:, :].rearrange("p (g s k) -> p g s k", g=GB, s=T + 1)
                for g in range(GB):
                    gg = f * GB + g
                    for a, o in ((0, cp[:, g, :, :]), (1, t2[:, g, :, :])):
                        go(v.tensor_tensor(o, c_p[:, a, gg, :].unsqueeze(1).to_broadcast([P, T + 1, GK]),
                                           pw[:, a, :, gg:gg + 1].to_broadcast([P, T + 1, GK]), ALU.mult))
                settle()
                o = stage[:, P_O:P_O + GB * 144]
                step(v.tensor_tensor(o, o, tmp2[:, :], ALU.add))
                q = stage[:, Q_O:Q_O + GB * P].rearrange("p (g c) -> p g c", g=GB)
                c1 = o.rearrange("p (g c) -> p g c", g=GB)[:, :, GK:]
                go(v.tensor_copy(q[0:NS], c1[NS:P]))
                v.tensor_copy(q[NS:P], c1[0:NS]).then_inc(tables_ready, 1)

            def s5_batch_out(f):
                b = full(v, ("s5w", f)).rearrange("p (g c) -> p g c", g=GB)
                w = stage[:, W_O:W_O + 768].rearrange("p (g c) -> p g c", g=GB)
                go(v.tensor_copy(w[:, :, 0:P], b))
                r = release(("s5w", f), v.tensor_copy(w[:, :, P:], b[:, :, 0:NS]))
                v.wait_ge(*r)
                v.wait_ge(tables_ready, f + 1)
                if f:
                    v.wait_ge(k_out, 16 * T * f)
                b = full(v, ("s5k", f))[0:GK, :].rearrange("p (g c) -> p g c", g=GB)
                r = release(("s5k", f), v.tensor_copy(k_s[:, :, KPAD:], b))
                v.wait_ge(*r)
                settle()
                for g in range(GB):
                    o = k_s[:, g, KPAD:KPAD + GK]
                    ins = v.scalar_tensor_tensor(o, ident[0:GK, 0:GK], d_t[:, f * GB + g:f * GB + g + 1], o,
                                                 ALU.mult, ALU.add)
                    if g < GB - 1:
                        go(ins)
                    else:
                        ins.then_inc(k_w, 1)
                settle()
                v.memset(st[:, 191:192], 0.0).then_inc(stage_w, 1)

            def down_and_add(stage, g, scale=None):
                for half in range(2):
                    add_rows((stage, "down", g, half), half, scale if g == 0 else None)

            go(v.memset(k_s[:, :, 0:KPAD], 0.0))
            settle()
            gbuf = xh[:, 0, 0:SEQ + 2]
            step(v.memset(gbuf[:, 0:2], 0.0))
            def batch(b_):
                if b_ % (EB // GB) == 0:
                    s5_phases(b_ * GB // EB)
                s5_batch(b_)

            for g, (f0, f1) in enumerate(GROUPS):
                for f in range(f0, f1):
                    v.wait_ge(gate_pre, f + 1)
                    c_ = gconv[:, f % 2, :]
                    step(v.scalar_tensor_tensor(c_, gbuf[:, 1:1 + SEQ], cw_c[:, 1, f:f + 1], c_, ALU.mult, ALU.add))
                    v.scalar_tensor_tensor(c_, gbuf[:, 0:SEQ], cw_c[:, 0, f:f + 1], c_, ALU.mult, ALU.add)\
                     .then_inc(gate_conv, 1)
                    v.wait_ge(gate_act, f + 1)
                    split(("f1", "val", f), lambda b, e: v.tensor_tensor(e, b, gconv[:, f % 2, :], ALU.mult),
                          *row_split(h_hi, h_lo, f - f0))
                    if f in up_batch:
                        finish_split()
                        batch(up_batch[f])
                        s5_batch_out(up_batch[f])
                finish_split()
                for half in range(2):
                    for b_ in down_batch.get((g, half), ()):
                        batch(b_)
                        s5_batch_out(b_)
                    add_rows(("f1", "down", g, half), half, ALPHA if g == 0 else None)
            if stop == 2:
                layer_norm(1, TT, ln_ready)
                return
            layer_norm(1, TT, ln_ready)

            go(v.memset(zc[:, :, :, :, 0:1], 0.0))
            settle()
            rms_and_split("mix0", 2 * TT, lambda t, k: [(scaled(gains[:, 0, 4 * k:4 * k + 4]),
                                                        (ev_s5, *tile_split_s5(4 * k, t)))])
            for half in range(2):
                for j in range(4):
                    v.tensor_copy(u_c[:, 32 * half:32 * half + 32, 2 * j, :],
                                  full(v, ("u", half, j))[0:NC, :].rearrange("c (g k) -> c g k", k=GK))\
                     .then_inc(u_even, 1)
            for b_ in range(NB):
                b = full(v, ("sv", b_))
                v.wait_ge(rec_in[b_ % 3], 16 * (b_ // 3 + 1))
                cs, sn = rec[b_ % 3][:, C_O:C_O + 256], rec[b_ % 3][:, S_O:S_O + 256]
                go(v.tensor_tensor(z1[:, :], b[:, 0:256], cs, ALU.mult))
                r = release(("sv", b_), v.tensor_tensor(z2[:, :], b[:, 256:512], sn, ALU.mult))
                settle()
                v.wait_ge(*r)
                step(v.tensor_tensor(z1[:, :], z1[:, :], z2[:, :], ALU.add))
                for g in range(GB):
                    gg = b_ * GB + g
                    s = slice(g * NC, g * NC + NC)
                    go(v.tensor_tensor_scan(z3[:, s], r8[:, gg:gg + 1].to_broadcast([P, NC]), z1[:, s], 0.0,
                                            ALU.mult, ALU.add))
                settle()
                if b_ >= 2:
                    v.wait_ge(*closed(("y", b_ - 2)))
                zv = z3[:, :].rearrange("p (g c) -> p g c", g=GB)[:, :, 0:NC - 1]
                cv = cs.rearrange("p (g c) -> p g c", g=GB)[:, :, 0:NC - 1]
                sv = sn.rearrange("p (g c) -> p g c", g=GB)[:, :, 0:NC - 1]
                step(v.tensor_tensor(zc[:, b_ % 2, 0, :, 1:], zv, cv, ALU.mult))
                v.tensor_tensor(zc[:, b_ % 2, 1, :, 1:], zv, sv, ALU.mult).then_inc(zc_ready, 1)
                v.wait_ge(zc_ready, b_ + 1)
                if b_ >= 3 and b_ % 2:
                    split(("zt", (b_ - 3) // 2), copied(SEQ), *turned_back((b_ - 3) // 2))
            split(("zt", KT - 1), copied(SEQ), *turned_back(KT - 1))
            finish_split()
            for half in range(2):
                for t in range(TT):
                    b = full(v, ("glu_v", half, t))
                    v.wait_ge(*freed[bank_no[("glu_g", half, t)]])
                    o = x_rows[:, t, half * HALF:half * HALF + HALF]
                    step(v.tensor_tensor(ev[:, 0, :], b, sig[:, t, :], ALU.mult))
                    last[t] = release(("glu_v", half, t), v.tensor_tensor(o, o, ev[:, 0, :], ALU.add))
                    v.wait_ge(*last[t])
            if stop == 3:
                return

            def swiglu(stage):
                e0 = splits[0]
                for g, (f0, f1) in enumerate(GROUPS):
                    for f in range(f0, f1):
                        n_gate[0] += 1
                        v.wait_ge(gate_act, n_gate[0])
                        split((stage, "val", f), lambda b, e: v.tensor_tensor(e, b, xh[:, f % 2, 0:SEQ], ALU.mult),
                              *row_split(h_hi, h_lo, f - f0))
                    finish_split()
                    down_and_add(stage, g)

            n_gate = [FT]
            rms_and_split("ffn0", 3 * TT, to_a(gains[:, 1, :]))
            swiglu("f2")
            if stop == 4:
                return

            rms_and_split("mla", 4 * TT, lambda t, k: [
                (scaled(gains[:, 2, 4 * k:4 * k + 4]), tile_split(a_hi, a_lo, 4 * k, 4, t)),
                (scaled(gains[:, 3, 4 * k:4 * k + 4]), tile_split(h_hi, h_lo, 4 * k, 4, t))])
            v.wait_ge(m_in, 16 * 7)
            flat = lambda a: rot[:, a, 0:TT, :]
            step(v.tensor_copy(st[:, 130:134], pos_i[:, :]))
            for t in range(TT):
                go(v.tensor_scalar(rot[:, 0, 4 + t, :], frq[:, :], st[:, 130 + t:131 + t], None, ALU.mult))
            settle()
            reduced(rot[:, 0, 4:8, :], rot[:, 1, 4:8, :], rot[:, 0, 0:4, :])
            quarter(rot[:, 1, 0:4, :], rot[:, 0, 0:4, :]).then_inc(tab_dve, 1)
            for t in range(TT):
                w = release(("kv_a", t), v.tensor_copy(ckv[:, t, :], full(v, ("kv_a", t))[:, 0:KVR + ROPE]))
                v.wait_ge(*w)
                v.memset(st[:, 190:191], 0.0).then_inc(lat_in, 1)
            v.wait_ge(tab_act, 6)
            for t in range(TT):
                v.wait_ge(lat_dev, t + 1)
                step(v.reciprocal(st[:, 16 + 2 * t:18 + 2 * t], st[:, 8 + 2 * t:10 + 2 * t]))
                c_ = ckv[:, t, 0:KVR]
                v.tensor_scalar(c_, c_, st[:, 16 + 2 * t:17 + 2 * t], None, ALU.mult).then_inc(ckv_ready, 1)
                kr = ckv[:, t, KVR:]
                step(v.scalar_tensor_tensor(kr, kr, st[:, 17 + 2 * t:18 + 2 * t], hg[:, 64:96], ALU.mult, ALU.mult))
                cmul(rot[:, 0, 8, :], rot[:, 0, 9, :], ckv[:, t, KVR:KVR + 16], ckv[:, t, KVR + 16:],
                     trig[:, 0, t, :], trig[:, 1, t, :], rot[:, 0, 10, :], rot[:, 0, 11, :])
                go(v.tensor_copy(k_n[:, t, :, NOPE:NOPE + 16], rot[:, 0, 8, :].unsqueeze(1).to_broadcast([P, NH, 16])))
                go(v.tensor_copy(k_n[:, t, :, NOPE + 16:], rot[:, 0, 9, :].unsqueeze(1).to_broadcast([P, NH, 16])))
                settle()
            for t in range(TT):
                w = release(("q_a", t), v.tensor_copy(cq[:, t, :], full(v, ("q_a", t))[:, 0:QR]))
                v.wait_ge(*w)
                v.memset(st[:, 190:191], 0.0).then_inc(lat_in, 1)
            for t in range(TT):
                v.wait_ge(lat_dev, TT + t + 1)
                step(v.reciprocal(st[:, 48 + t:49 + t], st[:, 40 + t:41 + t]))
                v.tensor_scalar(cq[:, t, :], cq[:, t, :], st[:, 48 + t:49 + t], None, ALU.mult).then_inc(cq_ready, 1)
            split_rows("ckv_t", KVR // P, gain=kva_g)
            split_rows("cq_t", QR // P, gain=qa_g, off=2)
            n = 0
            for which in range(2):
                for t in range(TT):
                    v.wait_ge(sq_made, n + 1)
                    if which == 0:
                        v.tensor_reduce(st[:, 64:80], sq[:, 0:NH * NOPE].rearrange("p (h e) -> p h e", h=NH),
                                        AX.X, ALU.add).then_inc(sum_made, 1)
                    else:
                        s3 = sq[:, :].rearrange("p (h e) -> p h e", h=NH)
                        step(v.tensor_reduce(st[:, 80:96], s3[:, :, NOPE:], AX.X, ALU.add))
                        v.tensor_reduce(st[:, 64:80], s3[:, :, 0:NOPE], AX.X, ALU.add).then_inc(sum_made, 1)
                    v.wait_ge(dev_made, n + 1)
                    w_ = 16 * (1 + which)
                    step(v.reciprocal(st[:, 136:136 + w_], st[:, 96:96 + w_]))
                    buf = (k_n, q_n)[which]
                    x_ = buf[:, t, :, 0:NOPE]
                    step(v.tensor_tensor(x_, x_, st[:, 136:152].unsqueeze(2).to_broadcast([P, NH, NOPE]), ALU.mult))
                    gn = hg[:, 96 * which:96 * which + NOPE].unsqueeze(1).to_broadcast([P, NH, NOPE])
                    if which:
                        go(v.tensor_tensor(x_, x_, gn, ALU.mult))
                        x_ = buf[:, t, :, NOPE:]
                        step(v.tensor_tensor(x_, x_, st[:, 152:168].unsqueeze(2).to_broadcast([P, NH, ROPE]), ALU.mult))
                        gr = hg[:, 160:192].unsqueeze(1).to_broadcast([P, NH, ROPE])
                        step(v.tensor_tensor(x_, x_, gr, ALU.mult))
                        a_, b_ = buf[:, t, :, NOPE:NOPE + 16], buf[:, t, :, NOPE + 16:]
                        c_, s_ = (trig[:, i, t, :].unsqueeze(1).to_broadcast([P, NH, 16]) for i in range(2))
                        go(v.tensor_tensor(rot[:, 0, :, :], a_, s_, ALU.mult))
                        go(v.tensor_tensor(rot[:, 1, :, :], b_, s_, ALU.mult))
                        settle()
                        go(v.tensor_tensor(a_, a_, c_, ALU.mult))
                        go(v.tensor_tensor(b_, b_, c_, ALU.mult))
                        settle()
                        go(v.tensor_tensor(a_, a_, rot[:, 1, :, :], ALU.subtract))
                        settle()
                        v.tensor_tensor(b_, b_, rot[:, 0, :, :], ALU.add).then_inc(qk_rows, 1)
                    else:
                        v.tensor_tensor(x_, x_, gn, ALU.mult).then_inc(qk_rows, 1)
                    n += 1
                    v.wait_ge(qk_rows, n)

            def k_turned(h):
                release(("ht", 1, h), v.tensor_copy(qk_t[:, h % 2, 1, :], full(v, ("ht", 1, h))[0:QK, :]))

            def head_rows(h):
                if h:
                    v.wait_ge(*closed(("o", h - 1)))
                for t in range(TT):
                    w = (t + 1) * P
                    release(("pt", h, t), v.tensor_copy(p_t[:, t, 0:w], full(v, ("pt", h, t))[:, 0:w]))
                v.wait_ge(prob_ready, (h + 1) * TT)
                rs = st[:, 16 + 8 * (h % 2):20 + 8 * (h % 2)]
                step(v.reciprocal(st[:, 32:36], rs))
                b = full(v, ("o", h))[:, 0:TT * VD].rearrange("p (t e) -> p t e", t=TT)
                release(("o", h), v.tensor_tensor(o_n[:, :, h * VD:h * VD + VD], b,
                                                  st[:, 32:36].unsqueeze(2).to_broadcast([P, TT, VD]), ALU.mult))

            k_turned(0)
            for h in range(NH):
                for t in range(TT):
                    b = full(v, ("sc", h, t))
                    w = (t + 1) * P
                    v.tensor_tensor_reduce(b[:, 0:w], b[:, 0:w], mask[:, SEQ - w:], -QK ** -0.5, 3e38,
                                           ALU.add, ALU.min,
                                           st[:, 8 * (h % 2) + t:8 * (h % 2) + t + 1]).then_inc(max_ready, 1)
                    if t == 2 and h + 1 < NH:
                        k_turned(h + 1)
                head_rows(h)
            split_rows("o_t", hi=h_hi, lo=h_lo)
            for half in range(2):
                add_rows(("w_o", half), half)
            if stop == 5:
                return
            rms_and_split("ffn1", 5 * TT, to_a(gains[:, 4, :]))
            swiglu("f3")


_INS = ['x', 'w_in', 'w_pool', 'pool_scale', 'w_out', 'ln1_g', 'ln1_b', 'w_up', 'conv_w', 'conv_b', 'w_down',
        'ln2_g', 'ln2_b', 'positions_2', 'mix_norm_2', 'ffn_norm_2', 'ffn_w_gate_up_2', 'ffn_w_down_2',
        'ssm_w_in_2', 'ssm_lambda_re_2', 'ssm_lambda_im_2', 'ssm_log_step_2', 'ssm_b_re_2', 'ssm_b_im_2',
        'ssm_c_re_2', 'ssm_c_im_2', 'ssm_d_2', 'ssm_w_glu_2', 'kv_in_norm_2', 'mla_w_kv_a_2', 'mla_kv_a_norm_2',
        'mla_w_kv_b_2', 'mla_k_nope_norm_2', 'mla_k_rope_norm_2', 'mla_w_q_a_2', 'mla_q_a_norm_2',
        'mla_w_q_b_2', 'mla_q_nope_norm_2', 'mla_q_rope_norm_2', 'mla_w_o_2']


def kernel(**inputs):
    import concourse.bacc as bacc
    from concourse.bass_utils import run_bass_kernel_spmd as run

    nc = bacc.Bacc("TRN2", target_bir_lowering=False, num_devices=1)
    arrays, args = {}, []
    given = {name: np.ascontiguousarray(inputs[name]) for name in _INS}
    given.update(constants())
    for name, a in given.items():
        arrays[f"in_{name}_dram"] = a
        args.append(nc.dram_tensor(f"in_{name}_dram", a.shape, mybir.dt.from_np(a.dtype), kind="ExternalInput").ap())
    args.append(nc.dram_tensor("out_dram", (1, SEQ, D), F, kind="ExternalOutput").ap())
    program(nc, 9, *args)
    r = run(nc, [arrays], core_ids=[0])
    return r.results[0]["out_dram"]
```

```python
from contextlib import ExitStack

import numpy as np

import concourse.bass as bass
from concourse import mybir

F = mybir.dt.float32
R = mybir.dt.float32r
I32 = mybir.dt.int32
ALU = mybir.AluOpType
ACT = mybir.ActivationFunctionType
AX = mybir.AxisListType

P = 128
SEQ, D = 512, 1024
TT = SEQ // P
KT = D // P
FF = 2816
FT = FF // P
GROUPS = ((0, 8), (8, 15), (15, 22))
HALF = 512
RH, POOLG = 4, 4
CHUNK = 64
ALPHA = 2.0 ** 0.25
RING = 3
CW = 1024
G, GK, NS = 64, 16, 64
T = P // GK
NC = SEQ // T
GB = 4
NB = G // GB
EB = 16
W_O, P_O, Q_O, M_O, C_O, S_O = 0, 768, 1344, 1856, 2368, 2624
REC = 2880
NH, NOPE, ROPE, VD = 16, 64, 32, 64
QK = NOPE + ROPE
HN = 4
HC = NH // HN
KVR, QR = 256, 384
TWO_PI = 2.0 * np.pi
ROUNDER = 1.5 * 2.0 ** 23
PI2_A = 6.28125
PI2_B = float(np.float32(round((TWO_PI - PI2_A) * 2 ** 21) / 2 ** 21))
PI2_C = float(np.float32(TWO_PI - PI2_A - PI2_B))
PI_IN = float(np.nextafter(np.float32(np.pi), np.float32(0)))
N_CONST, N_PARAM = 13, 12


def constants():
    f8 = np.float64
    c = {}
    c["c_ident"] = np.eye(P, dtype=np.float32)
    inv = (10000.0 ** (-np.arange(0, P, 2, dtype=np.float32) / np.float32(P))).astype(np.float32)
    ang = (np.arange(SEQ, dtype=np.float32)[:, None] * inv[None, :]).astype(np.float32).astype(f8)
    c["c_rope"] = np.stack([np.cos(ang), np.sin(ang)]).astype(np.float32)
    lg = np.log(1.0 - 2.0 ** (-5.0 - np.arange(RH, dtype=f8)))
    j, i = np.arange(P)[:, None], np.arange(SEQ)[None, :]
    seen = (j // CHUNK) <= (i // CHUNK)
    c["c_decay"] = np.stack([np.where(seen, np.exp(g * np.abs(i - j)), 0.0) * P ** -0.5 for g in lg]).astype(np.float32)
    c["c_count"] = np.stack([1.0 / np.minimum(np.arange(1, SEQ + 1), w) for w in (2, 4, 8, 16)]).astype(np.float32)
    c["c_freq"] = (10000.0 ** (-np.arange(0, ROPE, 2, dtype=np.float32) / np.float32(ROPE))).astype(np.float32)
    c["c_mask"] = np.where(np.arange(SEQ)[None, :] <= SEQ - P + np.arange(P)[:, None], 0.0, -1e30).astype(np.float32)
    return c


def program(nc, stop, x, w_in, w_pool, pool_scale, w_out, ln1_g, ln1_b, w_up, conv_w, conv_b, w_down, ln2_g, ln2_b,
            positions_2, mix_norm_2, ffn_norm_2, ffn_w_gate_up_2, ffn_w_down_2, ssm_w_in_2,
            ssm_lambda_re_2, ssm_lambda_im_2, ssm_log_step_2, ssm_b_re_2, ssm_b_im_2, ssm_c_re_2,
            ssm_c_im_2, ssm_d_2, ssm_w_glu_2, kv_in_norm_2, mla_w_kv_a_2, mla_kv_a_norm_2, mla_w_kv_b_2,
            mla_k_nope_norm_2, mla_k_rope_norm_2, mla_w_q_a_2, mla_q_a_norm_2, mla_w_q_b_2,
            mla_q_nope_norm_2, mla_q_rope_norm_2, mla_w_o_2,
            c_ident, c_rope, c_decay, c_count, c_freq, c_mask, out):
    rec_dram = nc.dram_tensor("s5_records", [NB, P, REC], F, kind="Internal").ap()
    with ExitStack() as ctx:
        ctx.enter_context(nc.allow_non_contiguous_dma(reason="small parameter tables"))
        base = (nc.sbuf_base + 31) // 32 * 32
        KB = 1024
        at_now = [base]

        def fixed(name, shape, dt):
            t = nc.alloc_sbuf_tensor_at(name, shape, dt, offset=at_now[0])
            at_now[0] += (int(np.prod(shape[1:])) * 4 + 31) // 32 * 32
            return t

        x_rows = fixed("x_rows", [P, TT, D], F)
        a_hi = fixed("a_hi", [P, KT, SEQ], R)
        a_lo = fixed("a_lo", [P, KT, SEQ], R)
        w_raw = fixed("w_raw", [P, RING, CW], F)
        w_hi = fixed("w_hi", [P, RING, CW], R)
        w_lo = fixed("w_lo", [P, RING, CW], R)
        xh = fixed("xh", [P, 2, D], F)
        ev = fixed("ev", [P, 2, HALF], F)
        ident = fixed("ident", [P, P], F)
        gains = fixed("gains", [P, 2, KT], F)
        kva_g = fixed("kva_g", [P, 2], F)
        qa_g = fixed("qa_g", [P, 3], F)
        cw_c = fixed("cw_c", [P, 3, FT], F)
        cb_c = fixed("cb_c", [P, FT], F)
        ps_c = fixed("ps_c", [P, POOLG], F)
        st = fixed("st", [P, 192], F)
        eps_c = fixed("eps_c", [P, 4], F)
        arena = at_now[0]
        room = nc.sbuf_top - arena

        def scratch(name, shape, dt, kb, extra=0):
            size = int(np.prod(shape[1:])) * 4
            off = int(kb * KB) + extra
            assert off + size <= room, (name, off + size, room)
            return nc.alloc_sbuf_tensor_at(name, shape, dt, offset=arena + off)

        h_hi = scratch("h_hi", [P, 8, SEQ], R, 0)
        h_lo = scratch("h_lo", [P, 8, SEQ], R, 16)
        q_r = scratch("q_r", [P, TT, RH, P], F, 0)
        k_r = scratch("k_r", [P, TT, RH, P], F, 8)
        v_r = scratch("v_r", [P, TT, RH, P], F, 16)
        g_r = scratch("g_r", [P, TT, RH, P], F, 24)
        q_t = scratch("q_t", [P, RH, SEQ], F, 32)
        k_t = scratch("k_t", [P, RH, SEQ], F, 40)
        decay = scratch("decay", [P, RH, SEQ], F, 48)
        PADW = 16
        pool_p = scratch("pool_p", [P, PADW + SEQ], F, 56)
        pool_a = scratch("pool_a", [P, PADW + SEQ], F, 56, 4 * (PADW + SEQ))
        pool_b = scratch("pool_b", [P, PADW + SEQ], F, 84)
        wpool = scratch("wpool", [P, POOLG, P], F, 80)
        rope_c = scratch("rope_c", [P, 2, TT, 64], F, 78)
        rtmp = scratch("rtmp", [P, 2, HALF // 2], F, 84)
        s_t = [scratch(f"s_t{i}", [P, 1280], F, 8 * i) for i in range(2)]
        ln_g = [scratch("ln1_gb", [P, 2, D], F, 32), scratch("ln2_gb", [P, 2, D], F, 62)]
        cnt16 = scratch("cnt16", [P, POOLG, PADW], F, 82)
        b_p = scratch("b_p", [P, 2, G, GK], F, 62)
        c_p = scratch("c_p", [P, 2, G, GK], F, 70)
        c_nat = scratch("c_nat", [P, 2, 8, 2, NS], F, 40)
        lam_nat = scratch("lam_nat", [G, 2, 2, NS], F, 96)
        pri = scratch("pri", [P, 2, T + 1, G], F, 32)
        sm = scratch("sm", [P, 18, G], F, 37)
        bt = scratch("bt", [P, 2, HALF], F, 42)
        pw = scratch("pw", [P, 2, T + 1, G], F, 88)
        turn = scratch("turn", [P, 2, 6, G], F, 92.75)
        r8 = scratch("r8", [P, G], F, 95.75)
        lam = scratch("lam", [P, 3, G], F, 97)
        d_t = scratch("d_t", [GK, G], F, 97.75)
        stage = scratch("stage", [P, M_O], F, 41)
        tmp1 = scratch("tmp1", [P, 576], F, 48.5)
        tmp2 = scratch("tmp2", [P, 576], F, 50.75)
        h_b = scratch("h_b", [P, GB, T, GK], F, 53)
        KPAD = P - GK
        k_s = scratch("k_s", [GK, GB, KPAD + P], F, 55)
        e_t = scratch("e_t", [P, 2, EB, NC], F, 78)
        u_c = scratch("u_c", [NC, G, T, GK], F, 0)
        rec = [scratch(f"rec{i}", [P, REC], F, 32 + 11.25 * i) for i in range(3)]
        u_t = scratch("u_t", [P, 3, GB * NC], F, 66)
        z1 = scratch("z1", [P, GB * NC], F, 69)
        z2 = scratch("z2", [P, GB * NC], F, 70)
        z3 = scratch("z3", [P, GB * NC], F, 71)
        zc = scratch("zc", [P, 2, 2, GB, NC], F, 72)
        y_c = scratch("y_c", [NC, 2, T, P], F, 76)
        gain_row = [scratch("gain_row0", [P, D], F, 70), scratch("gain_row1", [P, D], F, 40)]
        sig = scratch("sig", [P, TT, HALF], F, 68)
        q_n = scratch("q_n", [P, TT, NH, QK], F, 0)
        v_n = scratch("v_n", [P, TT, NH, VD], F, 24)
        k_n = scratch("k_n", [P, TT, NH, QK], F, 40)
        ckv = scratch("ckv", [P, TT, KVR + ROPE], F, 64)
        cq = scratch("cq", [P, TT, QR], F, 68.5)
        sq = xh[:, 0, 0:2 * HALF].rearrange("p (a c) -> p a c", a=2)
        nrm = xh[:, 1, 0:9 * HC * TT * HN].rearrange("p (a b c e) -> p a b c e", a=3, b=3, c=HC)
        rot = scratch("rot", [P, 2, NH, ROPE // 2], F, 81)
        o_n = nc.alloc_sbuf_tensor_at("o_n", [P, TT, NH * VD], F, offset=base + 32 * KB)
        qk_t = scratch("qk_t", [QK, 2, 2, SEQ], F, 64)
        TRI = P * TT * (TT + 1) // 2
        tri = lambda t: slice(P * t * (t + 1) // 2, P * (t + 1) * (t + 2) // 2)
        prob = scratch("prob", [P, 2, TRI], F, 72)
        p_t = scratch("p_t", [P, TRI], F, 82)
        q_rot = scratch("q_rot", [P, 2, TT, HN, ROPE // 2], F, 87)
        q_trig = scratch("q_trig", [P, 4, TT, ROPE // 2], F, 89)
        hg = scratch("hg", [P, 2 * ROPE], F, 94)
        gcol = scratch("gcol", [QK, 2], F, 96)
        mask = scratch("mask", [P, SEQ], F, 92)
        trig = scratch("trig", [P, 2, TT, ROPE // 2], F, 94.75)
        frq = scratch("frq", [P, ROPE // 2], F, 95.25)
        pos_i = scratch("pos_i", [P, TT], I32, 95.5)
        gconv = xh[:, 1, :].rearrange("p (a c) -> p a c", a=2)
        sqs = scratch("sqs", [P, SEQ], F, 84)

        ps = ctx.enter_context(nc.psum_tensor("ps", [P, 8, HALF], F))

        def sem(name):
            return ctx.enter_context(nc.semaphore(name))

        bank_full = [sem(f"bank_full{b}") for b in range(8)]
        bank_free = [sem(f"bank_free{b}") for b in range(8)]
        w_landed = [sem(f"w_landed{b}") for b in range(RING)]
        hi_made = sem("hi_made")
        lo_made = sem("lo_made")
        w_used = sem("w_used")
        ev_ready = sem("ev_ready")
        hi_ready = sem("hi_ready")
        lo_ready = sem("lo_ready")
        xh_ready = sem("xh_ready")
        ln_dev = sem("ln_dev")
        sq_ready = sem("sq_ready")
        dve_step = sem("dve_step")
        act_step = sem("act_step")
        var_ready = sem("var_ready")
        ln_ready = sem("ln_ready")
        rope_ready = sem("rope_ready")
        pool_ready = sem("pool_ready")
        decayed = sem("decayed")
        ret_raw = sem("ret_raw")
        ret_dev = sem("ret_dev")
        ret_ready = sem("ret_ready")
        tab_dve = sem("tab_dve")
        tab_act = sem("tab_act")
        tables_ready = sem("tables_ready")
        gate_pre = sem("gate_pre")
        gate_conv = sem("gate_conv")
        gate_act = sem("gate_act")
        u_even = sem("u_even")
        zc_ready = sem("zc_ready")
        sig_ready = sem("sig_ready")
        ckv_ready = sem("ckv_ready")
        cq_ready = sem("cq_ready")
        lat_in = sem("lat_in")
        lat_dev = sem("lat_dev")
        sq_made = sem("sq_made")
        sum_made = sem("sum_made")
        k_copied = sem("k_copied")
        dev_made = sem("dev_made")
        trig_ready = sem("trig_ready")
        q_roped = sem("q_roped")
        qk_rows = sem("qk_rows")
        pool_step = sem("pool_step")
        max_ready = sem("max_ready")
        prob_ready = sem("prob_ready")
        x_in = sem("x_in")
        id_in = sem("id_in")
        c_in = sem("c_in")
        gain_in = sem("gain_in")
        p_in = sem("p_in")
        ln_in = [sem("ln1_in"), sem("ln2_in")]
        m_in = sem("m_in")
        st_out = sem("st_out")
        e_out = sem("e_out")
        k_out = sem("k_out")
        stage_w = sem("stage_w")
        e_w = sem("e_w")
        k_w = sem("k_w")
        rec_in = [sem(f"rec_in{i}") for i in range(3)]
        o_out = sem("o_out")
        last_add = sem("last_add")

        block = ctx.enter_context(nc.Block())

        out_batch = {0: 0, 1: 1}
        up_batch = {0: 2, 2: 3, 4: 4, 6: 5, 8: 8, 10: 9, 12: 10, 15: 13, 17: 14}
        down_batch = {(0, 0): 6, (0, 1): 7, (1, 0): 11, (1, 1): 12, (2, 0): 15}
        up_phases = {3: 1}
        down_phases = {(0, 1): 2, (1, 0): 3}
        bank_no, freed, free_count = {}, [], [0] * 8
        chunks_at = {}
        chunk_src, chunk_done = [], []

        w_in0, w_out0 = w_in[0], w_out[0]

        def rows_of(w, k0, kn, c0, cn):
            return w[k0 * P:(k0 + kn) * P, c0:c0 + cn].rearrange("(k p) c -> p k c", p=P)

        def pool_out(h):
            return xh[:, h // 2, (h % 2) * HALF:(h % 2) * HALF + HALF]

        @block.tensor
        def _(pe):
            n_split = [0]
            n_ev = [0]

            def split_bank(name, through_ev=False):
                n_split[0] += 1
                n_ev[0] += through_ev
                return open_bank(name, freed_by=(ev_ready, n_ev[0]) if through_ev else (lo_ready, n_split[0]))

            def open_bank(name, freed_by=None):
                i = len(bank_no)
                bank_no[name] = i
                if i >= 8:
                    pe.wait_ge(*freed[i - 8])
                if freed_by is None:
                    free_count[i % 8] += 1
                    freed_by = (bank_free[i % 8], free_count[i % 8])
                freed.append(freed_by)
                return ps[:, i % 8, :]

            def close_bank(name, ins):
                i = bank_no[name]
                ins.then_inc(bank_full[i % 8], 1)
                chunks_at[name] = len(chunk_src)
                return bank_full[i % 8], i // 8 + 1

            def take_chunk(src, kn, cn, gain=None):
                n = len(chunk_src)
                chunk_src.append((src, kn, cn, gain))
                pe.wait_ge(hi_made, n + 1)
                pe.wait_ge(lo_made, n + 1)
                hi = w_hi[:, n % RING, 0:kn * cn].rearrange("p (k c) -> p k c", k=kn)
                lo = w_lo[:, n % RING, 0:kn * cn].rearrange("p (k c) -> p k c", k=kn)
                return hi, lo

            def chunk_over(ins):
                ins.then_inc(w_used, 1)
                n_plain[0] += 1
                chunk_done.append((w_used, n_plain[0]))

            n_plain = [0]

            def three(bank, wh, wl, xh_, xl_, first, last):
                pe.matmul(bank, wh, xh_, start=first, stop=False)
                pe.matmul(bank, wh, xl_, start=False, stop=False)
                return pe.matmul(bank, wl, xh_, start=False, stop=last)

            def rows_product(stage, w, ah, al, nk, c0, cn, per, row0=0, wait_k=None, between=None,
                             gain=None):
                stage = stage if isinstance(stage, tuple) else (stage,)
                banks = [open_bank((*stage, t)) for t in range(TT)]
                k = 0
                while k < nk:
                    kn = min(per, nk - k)
                    wh, wl = take_chunk(rows_of(w, row0 + k, kn, c0, cn), kn, cn,
                                        None if gain is None else gains[:, gain, k:k + kn])
                    for t in range(TT):
                        for kk in range(kn):
                            if wait_k is not None and t == 0:
                                pe.wait_ge(lo_ready, wait_k(k + kk))
                            s = slice(t * P, t * P + P)
                            o = banks[t][:, 0:cn]
                            end = k + kk == nk - 1
                            pe.matmul(o, ah[:, k + kk, s], wh[:, kk, :], start=(k + kk == 0), stop=False)
                            pe.matmul(o, ah[:, k + kk, s], wl[:, kk, :], start=False, stop=False)
                            m = pe.matmul(o, al[:, k + kk, s], wh[:, kk, :], start=False, stop=end)
                            if end:
                                over = close_bank((*stage, t), m)
                    k += kn
                    if k < nk:
                        chunk_over(m)
                    else:
                        chunk_done.append(over)
                    if between:
                        between(k)

            def cols_product(stage, w, c0, freed_by=None):
                b = open_bank(stage, freed_by=freed_by)
                wh, wl = take_chunk(rows_of(w, 0, KT, c0, P), KT, P)
                for k in range(KT):
                    m = three(b, wh[:, k, :], wl[:, k, :], a_hi[:, k, :], a_lo[:, k, :], k == 0, k == KT - 1)
                chunk_done.append(close_bank(stage, m))

            def turn_rows(stage, src, nk, ready=None, through_ev=False):
                for t in range(TT):
                    if ready:
                        ready(t)
                    k = 0
                    while k < nk:
                        kn = min(4, nk - k)
                        b = split_bank((stage, t, k // 4), through_ev)
                        for q in range(kn):
                            m = pe.transpose(b[:, q * P:q * P + P], src(t, k + q), ident[:, :])
                        close_bank((stage, t, k // 4), m)
                        k += kn

            def xh_turn(stage):
                def ready(t):
                    n_xh[0] += 1
                    pe.wait_ge(xh_ready, n_xh[0])
                turn_rows(stage, lambda t, k: xh[:, t % 2, k * P:k * P + P], KT, ready)

            n_xh = [0]

            def ffn(stage, wup, wdown, swap, extra=None):
                gate0, val0 = swap
                for g, (f0, f1) in enumerate(GROUPS):
                    base_split = n_split[0]
                    for f in range(f0, f1):
                        n_split[0] += 1
                        n_ev[0] += 1
                        cols_product((stage, "gate", f), wup, gate0 + f * P, freed_by=(ev_ready, n_ev[0]))
                        cols_product((stage, "val", f), wup, val0 + f * P, freed_by=(ev_ready, n_ev[0]))
                        if extra and f - 1 in up_batch:
                            extra(up_batch[f - 1])
                    for half in range(2):
                        b_ = down_batch.get((g, half)) if extra else None
                        between = (lambda k, b_=b_: extra(b_) if b_ is not None and k == 6 else None)
                        rows_product((stage, "down", g, half), wdown, h_hi, h_lo, f1 - f0, half * HALF, HALF, 2,
                                     row0=f0, wait_k=lambda k: base_split + k + 1, between=between)

            pe.wait_ge(id_in, 16)
            def turn_parameters():
                pe.wait_ge(c_in, 16 * N_CONST)
                pe.wait_ge(p_in, 16 * N_PARAM)
                b = open_bank("lam")
                for i in range(2):
                    m = pe.transpose(b[:, i * G:i * G + G], lam_nat[:, i, :, :].rearrange("g a n -> g (a n)"),
                                     ident[0:G, 0:G])
                close_bank("lam", m)
                for i in range(2):
                    for h in range(2):
                        b = open_bank(("c", i, h))
                        for q in range(4):
                            m = pe.transpose(b[:, q * P:q * P + P],
                                             c_nat[:, i, 4 * h + q, :, :].rearrange("p a n -> p (a n)"), ident[:, :])
                        close_bank(("c", i, h), m)

            pe.wait_ge(x_in, 16)
            turn_rows("x", lambda t, k: x_rows[:, t, k * P:k * P + P], KT)
            pe.wait_ge(lo_ready, n_split[0])
            for i, nm in enumerate("qkvg"):
                if nm == "v" and stop > 1:
                    turn_parameters()
                rows_product(nm, w_in0, a_hi, a_lo, KT, i * HALF, HALF, 2)
            for h in range(RH):
                for nm, src in (("q", q_r), ("k", k_r)):
                    if h == 0:
                        pe.wait_ge(rope_ready, TT)
                    b = open_bank((nm, "t", h))
                    for t in range(TT):
                        m = pe.transpose(b[:, t * P:t * P + P], src[:, t, h, :], ident[:, :])
                    close_bank((nm, "t", h), m)
                cols_product(("p", h), w_in0, 4 * HALF + h * P)
            pe.wait_ge(c_in, 16 * N_CONST)
            for h in range(RH):
                if h == 0:
                    for nm in "qk":
                        for hh in range(RH):
                            pe.wait_ge(*freed[bank_no[(nm, "t", hh)]])
                    pe.wait_ge(*freed[bank_no[("v", TT - 1)]])
                    pe.wait_ge(pool_ready, RH)
                for j in range(TT):
                    b = open_bank(("s", h, j), freed_by=(decayed, TT * h + j + 1))
                    m = pe.matmul(b[:, 0:SEQ - j * P], k_t[:, h, j * P:j * P + P], q_t[:, h, j * P:SEQ],
                                  start=True, stop=True)
                    close_bank(("s", h, j), m)
                pe.wait_ge(decayed, TT * (h + 1))
                b = open_bank(("ret", h))
                for t in range(TT):
                    for j in range(t + 1):
                        off = j * SEQ - P * (j * (j - 1) // 2)
                        m = pe.matmul(b[:, t * P:t * P + P], s_t[h % 2][:, off + (t - j) * P:off + (t - j) * P + P],
                                      v_r[:, j, h, :], start=(j == 0), stop=(j == t))
                close_bank(("ret", h), m)
                b = split_bank(("pool", h))
                m = pe.matmul(b, wpool[:, h, :], pool_out(h), start=True, stop=True)
                close_bank(("pool", h), m)
            for h in range(RH):
                pe.wait_ge(ret_ready, h + 1)
                b = split_bank(("ret_t", h))
                for t in range(TT):
                    m = pe.transpose(b[:, t * P:t * P + P], v_r[:, t, h, :], ident[:, :])
                close_bank(("ret_t", h), m)
            def prepare(f):
                pe.wait_ge(tables_ready, f + 1)
                b = open_bank(("s5w", f))
                for g in range(GB):
                    m = pe.transpose(b[:, g * P:g * P + P], h_b[:, g, :, :].rearrange("p s k -> p (s k)"), ident[:, :])
                close_bank(("s5w", f), m)
                b = open_bank(("s5k", f))
                for g in range(GB):
                    m = pe.matmul(b[0:GK, g * P:g * P + P], h_b[:, g, T - 1, :],
                                  stage[:, P_O + g * 144:P_O + g * 144 + P], start=True, stop=True)
                close_bank(("s5k", f), m)

            pe.wait_ge(lo_ready, n_split[0])
            for half in range(2):
                rows_product(("w_out", half), w_out0, a_hi, a_lo, KT, half * HALF, HALF, 2,
                             between=lambda k: prepare(out_batch[half]) if k == 6 and stop > 1 else None)
            if stop == 1:
                return

            def ready_x(t):
                n_xh[0] += 1
                pe.wait_ge(xh_ready, n_xh[0])
            turn_rows("ln1", lambda t, k: x_rows[:, t, k * P:k * P + P], KT, ready=ready_x)
            pe.wait_ge(lo_ready, n_split[0])

            ffn("f1", w_up[0], w_down[0], (FF, 0), prepare)
            if stop == 2:
                return

            xh_turn("mix0")
            pe.wait_ge(lo_ready, n_split[0])
            for half in range(2):
                rows_product(("u", half), ssm_w_in_2[0], a_hi, a_lo, KT, half * HALF, HALF, 2)

            def s5_states(b_):
                if b_ == 0:
                    pe.wait_ge(*freed[bank_no[("u", 1, 3)]])
                b = open_bank(("ut", b_))
                for g in range(GB):
                    gg = b_ * GB + g
                    m = pe.transpose(b[:, g * NC:g * NC + NC], u_c[:, gg, :, :].rearrange("c s k -> c (s k)"),
                                     ident[0:NC, 0:NC])
                close_bank(("ut", b_), m)

            def s5_inc(b_):
                i = b_ % 2
                pe.wait_ge(rec_in[b_ % 3], 16 * (b_ // 3 + 1))
                pe.wait_ge(*freed[bank_no[("ut", b_)]])
                b = open_bank(("sv", b_))
                for sw in range(2):
                    for g in range(GB):
                        o = W_O + g * 192 + 64 * sw
                        m = pe.matmul(b[:, sw * 256 + g * NC:sw * 256 + g * NC + NC], rec[b_ % 3][:, o:o + P],
                                      u_t[:, b_ % 3, g * NC:g * NC + NC], start=True, stop=True)
                close_bank(("sv", b_), m)

            def s5_out(b_):
                i = b_ % 2
                pe.wait_ge(zc_ready, b_ + 1)
                b = open_bank(("y", b_))
                for g in range(GB):
                    o = b[0:NC, g * P:g * P + P]
                    pe.matmul(o, u_t[:, b_ % 3, g * NC:g * NC + NC], rec[b_ % 3][:, M_O + g * P:M_O + g * P + P],
                              start=True, stop=False)
                    pe.matmul(o, zc[:, i, 0, g, :], rec[b_ % 3][:, P_O + g * 144 + GK:P_O + g * 144 + 144],
                              start=False, stop=False)
                    m = pe.matmul(o, zc[:, i, 1, g, :], rec[b_ % 3][:, Q_O + g * P:Q_O + g * P + P],
                                  start=False, stop=True)
                close_bank(("y", b_), m)

            def s5_turn_back(k):
                pe.wait_ge(*freed[bank_no[("y", 2 * k + 1)]])
                b = split_bank(("zt", k))
                for s in range(T):
                    m = pe.transpose(b[:, s * NC:s * NC + NC], y_c[:, k % 2, s, :], ident[0:NC, 0:NC])
                close_bank(("zt", k), m)

            s5_states(0)
            for b_ in range(NB):
                if b_ + 1 < NB:
                    s5_states(b_ + 1)
                s5_inc(b_)
                if b_:
                    s5_out(b_ - 1)
                if b_ >= 3 and b_ % 2:
                    s5_turn_back((b_ - 3) // 2)
            s5_out(NB - 1)
            s5_turn_back(KT - 1)
            pe.wait_ge(lo_ready, n_split[0])
            for half in range(2):
                rows_product(("glu_g", half), ssm_w_glu_2[0], a_hi, a_lo, KT, D + half * HALF, HALF, 2)
                rows_product(("glu_v", half), ssm_w_glu_2[0], a_hi, a_lo, KT, half * HALF, HALF, 2)
            if stop == 3:
                return
            xh_turn("ffn0")
            pe.wait_ge(lo_ready, n_split[0])
            ffn("f2", ffn_w_gate_up_2[0], ffn_w_down_2[0], (0, FF))
            if stop == 4:
                return

            xh_turn("mla")
            pe.wait_ge(lo_ready, n_split[0])
            rows_product("kv_a", mla_w_kv_a_2, a_hi, a_lo, KT, 0, KVR + ROPE, 2, gain=0)
            rows_product("q_a", mla_w_q_a_2[0], a_hi, a_lo, KT, 0, QR, 2, gain=1)

            turn_rows("ckv_t", lambda t, k: ckv[:, t, k * P:k * P + P], KVR // P,
                      ready=lambda t: pe.wait_ge(ckv_ready, t + 1), through_ev=True)
            turn_rows("cq_t", lambda t, k: cq[:, t, k * P:k * P + P], QR // P,
                      ready=lambda t: pe.wait_ge(cq_ready, t + 1), through_ev=True)
            pe.wait_ge(lo_ready, n_split[0])
            for c in range(4):
                rows_product(("kv_b", c), mla_w_kv_b_2, a_hi, a_lo, KVR // P, c * HALF, HALF, 2)
            for c in range(HC):
                rows_product(("q_b", c), mla_w_q_b_2[0], a_hi[:, 2:5, :], a_lo[:, 2:5, :], QR // P,
                             c * HN * QK, HN * QK, 2)

            def head_turn(h):
                pe.wait_ge(qk_rows, HC + h // HN + 1)
                for i, src in enumerate((q_n, k_n)):
                    b = open_bank(("ht", i, h))
                    for t in range(TT):
                        m = pe.transpose(b[0:QK, t * P:t * P + P], src[:, t, h, :], ident[:, :])
                    close_bank(("ht", i, h), m)

            def head_scores(h, t):
                if t == 0:
                    pe.wait_ge(*freed[bank_no[("ht", 0, h)]])
                    pe.wait_ge(*freed[bank_no[("ht", 1, h)]])
                b = open_bank(("sc", h, t), freed_by=(prob_ready, h * TT + t + 1))
                m = pe.matmul(b[:, 0:(t + 1) * P], qk_t[:, h % 2, 0, t * P:t * P + P],
                              qk_t[:, h % 2, 1, 0:(t + 1) * P], start=True, stop=True)
                close_bank(("sc", h, t), m)

            def head_probs(h, t):
                pe.wait_ge(prob_ready, h * TT + t + 1)
                b = open_bank(("pt", h, t))
                for j in range(t + 1):
                    o = P * t * (t + 1) // 2 + j * P
                    m = pe.transpose(b[:, j * P:j * P + P], prob[:, h % 2, o:o + P], ident[:, :])
                close_bank(("pt", h, t), m)

            def head_out(h):
                b = open_bank(("o", h))
                for t in range(TT):
                    pe.wait_ge(*freed[bank_no[("pt", h, t)]])
                    for j in range(t + 1):
                        o = P * t * (t + 1) // 2 + j * P
                        m = pe.matmul(b[:, t * VD:t * VD + VD], p_t[:, o:o + P], v_n[:, j, h, :],
                                      start=(j == 0), stop=(j == t))
                close_bank(("o", h), m)

            head_turn(0)
            head_turn(1)
            for t in range(TT):
                head_scores(0, t)
            for h in range(NH):
                for t in range(TT):
                    if h + 1 < NH:
                        head_scores(h + 1, t)
                    head_probs(h, t)
                if h + 2 < NH:
                    head_turn(h + 2)
                head_out(h)
            pe.wait_ge(*freed[bank_no[("o", NH - 1)]])
            turn_rows("o_t", lambda t, k: o_n[:, t, k * P:k * P + P], KT)
            pe.wait_ge(lo_ready, n_split[0])
            for half in range(2):
                rows_product(("w_o", half), mla_w_o_2[0], h_hi, h_lo, KT, half * HALF, HALF, 2)
            if stop == 5:
                return
            xh_turn("ffn1")
            pe.wait_ge(lo_ready, n_split[0])
            ffn("f3", ffn_w_gate_up_2[1], ffn_w_down_2[1], (0, FF))

        def full(eng, name):
            i = bank_no[name]
            eng.wait_ge(bank_full[i % 8], i // 8 + 1)
            return ps[:, i % 8, :]

        def release(name, ins):
            sem_, value = freed[bank_no[name]]
            assert sem_ is bank_free[bank_no[name] % 8]
            ins.then_inc(sem_, 1)
            return sem_, value

        def closed(name):
            i = bank_no[name]
            return bank_full[i % 8], i // 8 + 1

        def tile_split(hi, lo, k0, kn, t):
            s = slice(t * P, t * P + P)
            return (lambda e: e[:, 0:kn * P].rearrange("p (k c) -> p k c", k=kn),
                    hi[:, k0:k0 + kn, s], lo[:, k0:k0 + kn, s])

        def tile_split_s5(k0, t):
            c = slice(t * P // T, (t + 1) * P // T)
            dst = [a[:, k0:k0 + 4, :].rearrange("p k (s c) -> p k s c", s=T)[:, :, :, c] for a in (a_hi, a_lo)]
            return dst

        def ev_s5(e):
            return e.rearrange("p (k c s) -> p k s c", k=4, s=T)

        def turned_back(k):
            return (lambda e: e.rearrange("p (s c) -> p s c", s=T),
                    *[a[:, k, :].rearrange("p (c s) -> p s c", s=T) for a in (a_hi, a_lo)])

        def row_split(hi, lo, k):
            return lambda e: e, hi[:, k, :], lo[:, k, :]

        @block.gpsimd
        def _(pool):
            pool.dma_start(wpool[:, :, :], w_pool[0].rearrange("g c d -> c g d")).then_inc(c_in, 16)
            pool.dma_start(decay[:, :, :], c_decay.rearrange("h j i -> j h i")).then_inc(c_in, 16)
            pool.dma_start(rope_c[:, :, :, :], c_rope.rearrange("a (t p) d -> p a t d", p=P)).then_inc(c_in, 16)
            pool.dma_start(ps_c[:, :], pool_scale[0].rearrange("(g p) -> p g", p=P)).then_inc(c_in, 16)
            pool.dma_start(cnt16[:, :, :], c_count[:, 0:PADW].partition_broadcast(P)).then_inc(c_in, 16)
            cols = ((gains[:, 0, :], kv_in_norm_2), (gains[:, 1, :], mix_norm_2[1]), (kva_g[:, :], mla_kv_a_norm_2),
                    (qa_g[:, :], mla_q_a_norm_2[0]), (cb_c[:, :], conv_b[0]))
            for dst, src in cols:
                pool.dma_start(dst, src.rearrange("(k p) -> p k", p=P)).then_inc(c_in, 16)
            for j in range(3):
                pool.dma_start(cw_c[:, j, :], conv_w[0, j].rearrange("(k p) -> p k", p=P)).then_inc(c_in, 16)

            def load_parameters():
                for i, src in enumerate((ssm_lambda_re_2, ssm_lambda_im_2)):
                    for a in range(2):
                        pool.dma_start(lam_nat[:, i, a, :], src[0]).then_inc(p_in, 16)
                for i, src in enumerate((ssm_c_re_2, ssm_c_im_2)):
                    v = src[0].rearrange("(h g) k n -> (g k) h n", g=8)
                    for a in range(2):
                        pool.dma_start(c_nat[:, i, :, a, :], v).then_inc(p_in, 16)
                pool.dma_start(lam[:, 2, :], ssm_log_step_2.to_broadcast([P, G])).then_inc(p_in, 16)
                for i, src in enumerate((ssm_b_re_2, ssm_b_im_2)):
                    pool.dma_start(b_p[0:NS, i, :, :], src[0].rearrange("g n k -> n g k")).then_inc(p_in, 16)
                pool.dma_start(d_t[:, :], ssm_d_2[0].rearrange("(g k) -> k g", g=G)).then_inc(p_in, 16)

            steps = [0]

            def step(ins):
                ins.then_inc(pool_step, 1)
                steps[0] += 1
                pool.wait_ge(pool_step, steps[0])

            def rope_queries(c):
                if c == 0:
                    pool.wait_ge(trig_ready, 1)
                for t in range(TT):
                    pool.wait_ge(*freed[bank_no[("q_b", c, t)]])
                x1, x2 = (q_n[:, :, HN * c:HN * c + HN, o:o + ROPE // 2] for o in (NOPE, NOPE + ROPE // 2))
                r1, r2 = q_rot[:, 0, :, :, :], q_rot[:, 1, :, :, :]
                tab = [q_trig[:, i, :, :].unsqueeze(2).to_broadcast([P, TT, HN, ROPE // 2]) for i in range(4)]
                step(pool.tensor_tensor(r1, x2, tab[1], ALU.mult))
                step(pool.tensor_tensor(r2, x1, tab[2], ALU.mult))
                step(pool.tensor_tensor(x1, x1, tab[0], ALU.mult))
                step(pool.tensor_tensor(x2, x2, tab[3], ALU.mult))
                step(pool.tensor_tensor(x1, x1, r1, ALU.subtract))
                pool.tensor_tensor(x2, x2, r2, ALU.add).then_inc(q_roped, 1)
                pool.wait_ge(q_roped, c + 1)

            for n, (_, kn, cn, _) in enumerate(chunk_src):
                w = kn * cn
                if n == 3 and stop > 1:
                    load_parameters()
                pool.wait_ge(hi_made, n + 1)
                if n >= RING:
                    pool.wait_ge(*chunk_done[n - RING])
                pool.tensor_tensor(w_lo[:, n % RING, 0:w], w_raw[:, n % RING, 0:w],
                                   w_hi[:, n % RING, 0:w].bitcast(F), ALU.subtract).then_inc(lo_made, 1)
                for c in range(HC if stop > 4 else 0):
                    if n == chunks_at[("q_b", c, 0)] + 1:
                        rope_queries(c)

        end_waits = []
        last_bank = {1: ("w_out", 1), 2: None, 3: ("glu_v", 1), 4: ("f2", "down", 2, 1), 5: ("w_o", 1),
                     9: ("f3", "down", 2, 1)}[stop]

        @block.sync
        def _(sp):
            sp.dma_start(x_rows[:, :, :], x[0].rearrange("(t p) d -> p t d", p=P)).then_inc(x_in, 16)

            def store_batch(f):
                sp.wait_ge(stage_w, f + 1)
                sp.dma_start(rec_dram[f, :, 0:M_O], stage[:, :]).then_inc(st_out, 16)
                sp.wait_ge(k_w, f + 1)
                for s in range(T):
                    o = KPAD - GK * s
                    sp.dma_start(rec_dram[f, GK * s:GK * s + GK, M_O:C_O].rearrange("p (g c) -> p g c", g=GB),
                                 k_s[:, :, o:o + P]).then_inc(k_out, 16)
                if f % (EB // GB) == 0:
                    sp.wait_ge(e_w, f * GB // EB + 1)
                    for i in range(EB // GB):
                        sp.dma_start(rec_dram[f + i, :, C_O:REC].rearrange("p (a g c) -> p a g c", a=2, g=GB),
                                     e_t[:, :, GB * i:GB * i + GB, :]).then_inc(e_out, 16)

            for n, (src, kn, cn, _) in enumerate(chunk_src):
                if n >= RING:
                    sp.wait_ge(hi_made, n - RING + 1)
                    sp.wait_ge(lo_made, n - RING + 1)
                sp.dma_start(w_raw[:, n % RING, 0:kn * cn].rearrange("p (k c) -> p k c", k=kn), src)\
                  .then_inc(w_landed[n % RING], 16)
                if stop >= 2:
                    for f in range(NB):
                        if chunks_at[("s5k", f)] + RING == n:
                            store_batch(f)
            if stop == 2:
                sp.wait_ge(ln_ready, TT)
            else:
                for t in range(TT):
                    sp.wait_ge(*freed[bank_no[(*last_bank, t)]])
            if stop >= 2:
                sp.wait_ge(st_out, 16 * NB)
                sp.wait_ge(k_out, 16 * NB * T)
                sp.wait_ge(e_out, 16 * NB)
            sp.dma_start(out[0].rearrange("(t p) d -> p t d", p=P), x_rows[:, :, :]).then_inc(o_out, 16)
            sp.wait_ge(o_out, 16)

        @block.scalar
        def _(act):
            steps, evs = [0], [0]

            def step(ins):
                ins.then_inc(act_step, 1)
                steps[0] += 1
                act.wait_ge(act_step, steps[0])

            made = [0]

            def ahead(count):
                while made[0] < min(count + RING, len(chunk_src)):
                    n = made[0]
                    _, kn, cn, gain = chunk_src[n]
                    w = kn * cn
                    act.wait_ge(w_landed[n % RING], 16 * (n // RING + 1))
                    if n >= RING:
                        act.wait_ge(*chunk_done[n - RING])
                    if gain is not None:
                        for k in range(kn):
                            r = w_raw[:, n % RING, k * cn:k * cn + cn]
                            ins = act.activation(r, r, ACT.Copy, scale=gain[:, k:k + 1])
                            if k < kn - 1:
                                ins.then_inc(act_step, 1)
                                steps[0] += 1
                        step(ins)
                    act.activation(w_hi[:, n % RING, 0:w], w_raw[:, n % RING, 0:w], ACT.Copy).then_inc(hi_made, 1)
                    made[0] += 1

            def at(name):
                ahead(chunks_at[name])
                return full(act, name)

            def split(name, view, hi, lo, scale=1.0):
                act.activation(hi, view(at(name)), ACT.Copy, scale=scale).then_inc(hi_ready, 1)

            def split_ev(name, view, hi, lo):
                ahead(chunks_at[name])
                i = evs[0]
                act.wait_ge(ev_ready, i + 1)
                act.activation(hi, view(ev[:, i % 2, :]), ACT.Copy).then_inc(hi_ready, 1)
                evs[0] += 1

            def split_rows(stage, nk=KT, hi=a_hi, lo=a_lo, off=0, splitter=split):
                for t in range(TT):
                    for k in range(0, nk, 4):
                        kn = min(4, nk - k)
                        splitter((stage, t, k // 4), *tile_split(hi, lo, off + k, kn, t))

            def deviation(stage, added, ready, t):
                ahead(chunks_at[added(t)])
                act.wait_ge(*ready(t))
                if t >= 2:
                    act.wait_ge(*closed((stage, t - 2, 1)))
                step(act.activation(xh[:, t % 2, :], x_rows[:, t, :], ACT.Square, accum_out=st[:, t:t + 1]))
                act.activation(st[:, 4 + t:5 + t], st[:, t:t + 1], ACT.Sqrt, scale=1.0 / D,
                               bias=eps_c[:, 1:2]).then_inc(sq_ready, 1)

            def split_tile(stage, t, dst):
                for k in range(2):
                    split((stage, t, k), *dst(t, k))

            def rms_and_split(stage, added, ready, dst):
                deviation(stage, added, ready, 0)
                for t in range(TT):
                    if t + 1 < TT:
                        deviation(stage, added, ready, t + 1)
                    split_tile(stage, t, dst)

            def load_gain(i, src):
                act.dma_start(gain_row[i][:, :], src.partition_broadcast(P)).then_inc(gain_in, 16)

            def bank_ready(added):
                return lambda t: freed[bank_no[added(t)]]

            def to_a(t, k):
                return tile_split(a_hi, a_lo, 4 * k, 4, t)

            def to_a_s5(t, k):
                return (ev_s5, *tile_split_s5(4 * k, t))

            def ffn(stage, swish_from_conv):
                ft = 0
                for g, (f0, f1) in enumerate(GROUPS):
                    for f in range(f0, f1):
                        b = at((stage, "gate", f))
                        if swish_from_conv:
                            if f >= 1:
                                act.wait_ge(gate_conv, f)
                            step(act.activation(gbuf[:, 2:2 + SEQ], b, ACT.Copy))
                            act.activation(gconv[:, f % 2, :], b, ACT.Identity, scale=cw_c[:, 2, f:f + 1],
                                           bias=cb_c[:, f:f + 1]).then_inc(gate_pre, 1)
                            act.wait_ge(gate_conv, f + 1)
                            act.activation(gconv[:, f % 2, :], gconv[:, f % 2, :], ACT.Silu).then_inc(gate_act, 1)
                        else:
                            if f >= 2:
                                act.wait_ge(ev_ready, ev0[0] + f - 1)
                            act.activation(xh[:, f % 2, 0:SEQ], b, ACT.Silu).then_inc(gate_act, 1)
                        split_ev((stage, "val", f), *row_split(h_hi, h_lo, f - f0))

            ev0 = [0]
            act.dma_start(ident[:, :], c_ident).then_inc(id_in, 16)
            split_rows("x")
            if stop > 1:
                ahead(chunks_at["lam"])
                act.wait_ge(*closed(("c", 1, 1)))
                act.wait_ge(p_in, 16 * N_PARAM)
                act.activation(sm[:, 0, :], lam[:, 2, :], ACT.Exp).then_inc(tab_act, 1)
                act.wait_ge(tab_dve, 1)
                act.activation(sm[:, 3, :], sm[:, 1, :], ACT.Exp).then_inc(tab_act, 1)
                act.wait_ge(tab_dve, 2)
                act.activation(sm[:, 7, :], sm[:, 5, :], ACT.Sin).then_inc(tab_act, 1)
                act.activation(sm[:, 8, :], sm[:, 6, :], ACT.Sin).then_inc(tab_act, 1)
            for t in range(TT):
                release(("v", t), act.activation(v_r[:, t, :, :].rearrange("p h e -> p (h e)"), at(("v", t)), ACT.Copy))
            for t in range(TT):
                release(("g", t), act.activation(g_r[:, t, :, :].rearrange("p h e -> p (h e)"), at(("g", t)), ACT.Silu))
            for h in range(RH):
                ahead(chunks_at[("ret", h)])
                act.wait_ge(ret_raw, h + 1)
                act.activation(st[:, 16 + 4 * h:20 + 4 * h], st[:, 4 * h:4 * h + 4], ACT.Sqrt, scale=1.0 / P,
                               bias=eps_c[:, 1:2]).then_inc(ret_dev, 1)
                split(("pool", h), *row_split(a_hi, a_lo, RH + h), scale=ps_c[:, h:h + 1])
            act.wait_ge(*closed(("ret", RH - 1)))
            for i, src in enumerate((ln1_g, ln1_b)):
                act.dma_start(ln_g[0][:, i, :], src.to_broadcast([P, D])).then_inc(ln_in[0], 16)
            for h in range(RH):
                split(("ret_t", h), *row_split(a_hi, a_lo, h))
            if stop == 1:
                ahead(len(chunk_src))
                act.wait_ge(ln_in[0], 32)
                return

            def ln_deviation(added, i, t):
                ahead(chunks_at[added(t)])
                act.wait_ge(var_ready, i * TT + t + 1)
                act.activation(st[:, 36 + t:37 + t], st[:, 24 + 2 * t + 1:24 + 2 * t + 2], ACT.Sqrt,
                               bias=eps_c[:, 0:1]).then_inc(ln_dev, 1)

            ln_deviation(lambda t: ("w_out", 1, t), 0, 0)
            for t in range(TT):
                if t + 1 < TT:
                    ln_deviation(lambda t: ("w_out", 1, t), 0, t + 1)
                if t:
                    split_tile("ln1", t - 1, to_a)
            split_tile("ln1", TT - 1, to_a)
            gbuf = xh[:, 0, 0:SEQ + 2]
            ffn("f1", True)
            act.wait_ge(tables_ready, NB)
            for i, src in enumerate((ln2_g, ln2_b)):
                act.dma_start(ln_g[1][:, i, :], src.to_broadcast([P, D])).then_inc(ln_in[1], 16)
            load_gain(0, mix_norm_2[0])
            down = lambda t: ("f1", "down", 2, 1, t)
            if stop == 2:
                ahead(len(chunk_src))
                for t in range(TT):
                    ln_deviation(down, 1, t)
                act.wait_ge(gain_in, 16)
                return

            whole = lambda t: (ln_ready, t + 1)
            ln_deviation(down, 1, 0)
            for t in range(TT):
                if t + 1 < TT:
                    ln_deviation(down, 1, t + 1)
                deviation("mix0", down, whole, t)
                if t:
                    split_tile("mix0", t - 1, to_a_s5)
            split_tile("mix0", TT - 1, to_a_s5)
            act.wait_ge(st_out, 16 * NB)
            act.wait_ge(k_out, 16 * NB * T)
            act.wait_ge(e_out, 16 * NB)

            def load_rec(b_):
                act.dma_start(rec[b_ % 3][:, :], rec_dram[b_]).then_inc(rec_in[b_ % 3], 16)

            load_rec(0)
            load_rec(1)
            load_rec(2)
            for dst, src in ((hg[:, 0:ROPE], mla_k_rope_norm_2), (hg[:, ROPE:], mla_q_rope_norm_2[0]),
                             (frq[:, :], c_freq)):
                act.dma_start(dst, src.partition_broadcast(P)).then_inc(m_in, 16)
            for i, src in enumerate((mla_q_nope_norm_2[0], mla_k_nope_norm_2)):
                act.dma_start(gcol[0:NOPE, i:i + 1], src.rearrange("(e a) -> e a", a=1)).then_inc(m_in, 16)
            act.dma_start(mask[:, :], c_mask).then_inc(m_in, 16)
            act.dma_start(pos_i[:, :], positions_2[0].rearrange("(t p) -> p t", p=P)).then_inc(m_in, 16)
            for half in range(2):
                for j in range(4):
                    b = at(("u", half, j))
                    act.wait_ge(u_even, 4 * half + j + 1)
                    release(("u", half, j), act.activation(u_c[:, 32 * half:32 * half + 32, 2 * j + 1, :],
                                                           b[NC:P, :].rearrange("c (g k) -> c g k", k=GK), ACT.Copy))

            def s5_turned(b_):
                if b_ >= 3:
                    act.wait_ge(*closed(("y", b_ - 3)))
                release(("ut", b_), act.activation(u_t[:, b_ % 3, :], at(("ut", b_))[:, 0:GB * NC], ACT.Copy))

            def s5_gelu(b_):
                y = at(("y", b_))[0:NC, :].rearrange("c (g t k) -> c t g k", g=GB, t=T)
                k, j = divmod(b_, 2)
                if j == 0 and k >= 2:
                    act.wait_ge(*closed(("zt", k - 2)))
                o = y_c[:, k % 2, :, 64 * j:64 * j + 64].rearrange("c t (g k) -> c t g k", g=GB)
                release(("y", b_), act.activation(o, y, ACT.Gelu_apprx_tanh))
                if b_ + 3 < NB:
                    load_rec(b_ + 3)

            s5_turned(0)
            for b_ in range(NB):
                if b_ + 1 < NB:
                    s5_turned(b_ + 1)
                if b_:
                    s5_gelu(b_ - 1)
                if b_ >= 3 and b_ % 2:
                    split(("zt", (b_ - 3) // 2), *turned_back((b_ - 3) // 2))
            s5_gelu(NB - 1)
            load_gain(1, ffn_norm_2[0])
            split(("zt", KT - 1), *turned_back(KT - 1))
            for half in range(2):
                for t in range(TT):
                    b = at(("glu_g", half, t))
                    if half:
                        act.wait_ge(*freed[bank_no[("glu_v", 0, t)]])
                    release(("glu_g", half, t), act.activation(sig[:, t, :], b, ACT.Sigmoid))
                ahead(chunks_at[("glu_v", half, TT - 1)])
            if stop == 3:
                return
            added = lambda t: ("glu_v", 1, t)
            rms_and_split("ffn0", added, bank_ready(added), to_a)
            ev0[0] = evs[0]
            ffn("f2", False)
            if stop == 4:
                ahead(len(chunk_src))
                return

            added = lambda t: ("f2", "down", 2, 1, t)
            rms_and_split("mla", added, bank_ready(added), to_a)
            act.wait_ge(tab_dve, 3)
            act.activation(trig[:, 1, :, :], rot[:, 0, 0:TT, :], ACT.Sin).then_inc(tab_act, 1)
            act.activation(trig[:, 0, :, :], rot[:, 1, 0:TT, :], ACT.Sin).then_inc(tab_act, 1)
            for t in range(TT):
                ahead(chunks_at[("kv_a", t)])
                act.wait_ge(lat_in, t + 1)
                step(act.activation(sq[:, 0, 0:KVR], ckv[:, t, 0:KVR], ACT.Square, accum_out=st[:, 2 * t:2 * t + 1]))
                step(act.activation(sq[:, 1, 0:ROPE], ckv[:, t, KVR:], ACT.Square, accum_out=st[:, 2 * t + 1:2 * t + 2]))
                step(act.activation(st[:, 8 + 2 * t:9 + 2 * t], st[:, 2 * t:2 * t + 1], ACT.Sqrt, scale=1.0 / KVR,
                                    bias=eps_c[:, 1:2]))
                act.activation(st[:, 9 + 2 * t:10 + 2 * t], st[:, 2 * t + 1:2 * t + 2], ACT.Sqrt, scale=1.0 / ROPE,
                               bias=eps_c[:, 1:2]).then_inc(lat_dev, 1)
            for t in range(TT):
                ahead(chunks_at[("q_a", t)])
                act.wait_ge(lat_in, TT + t + 1)
                step(act.activation(sq[:, 0, 0:QR], cq[:, t, :], ACT.Square, accum_out=st[:, 32 + t:33 + t]))
                act.activation(st[:, 40 + t:41 + t], st[:, 32 + t:33 + t], ACT.Sqrt, scale=1.0 / QR,
                               bias=eps_c[:, 1:2]).then_inc(lat_dev, 1)
            split_rows("ckv_t", KVR // P, splitter=split_ev)
            split_rows("cq_t", QR // P, off=2, splitter=split_ev)

            def row_deviations(n):
                act.wait_ge(sum_made, (n + 1) * TT)
                q, c = divmod(n, HC)
                if q:
                    step(act.activation(nrm[:, 1, 2, c, :], nrm[:, 0, 2, c, :], ACT.Sqrt, scale=1.0 / ROPE,
                                        bias=eps_c[:, 1:2]))
                act.activation(nrm[:, 1, q, c, :], nrm[:, 0, q, c, :], ACT.Sqrt, scale=1.0 / NOPE,
                               bias=eps_c[:, 1:2]).then_inc(dev_made, 1)

            for n in range(2 * HC):
                q, c = divmod(n, HC)
                for t in range(TT):
                    i = n * TT + t
                    name = (("kv_b", "q_b")[q], c, t)
                    b = at(name)
                    if i >= 2:
                        act.wait_ge(sum_made, i - 1)
                    rows = slice(HN * c, HN * c + HN)
                    if q:
                        b = b[:, 0:HN * QK].rearrange("p (h e) -> p h e", h=HN)
                        dst = q_n[:, t, rows, :]
                    else:
                        b = b.rearrange("p (h e) -> p h e", h=HN)[:, :, 0:NOPE]
                        dst = k_n[:, t, rows, 0:NOPE]
                    w = HN * (QK if q else NOPE)
                    act.activation(sq[:, i % 2, 0:w].rearrange("p (h e) -> p h e", h=HN), b, ACT.Square)\
                       .then_inc(sq_made, 1)
                    ins = act.activation(dst, b, ACT.Copy)
                    if q:
                        release(name, ins)
                    else:
                        ins.then_inc(k_copied, 1)
                    if t == 1 and n:
                        row_deviations(n - 1)
            row_deviations(2 * HC - 1)

            def q_turned(h):
                release(("ht", 0, h), act.activation(qk_t[:, h % 2, 0, :], at(("ht", 0, h))[0:QK, :], ACT.Copy,
                                                     scale=gcol[:, 0:1]))

            def exponentials(h, t):
                act.wait_ge(max_ready, h * TT + t + 1)
                act.activation(prob[:, h % 2, tri(t)], full(act, ("sc", h, t))[:, 0:(t + 1) * P], ACT.Exp,
                               scale=-1.0, bias=st[:, 8 * (h % 2) + t:8 * (h % 2) + t + 1],
                               accum_out=st[:, 16 + 8 * (h % 2) + t:17 + 8 * (h % 2) + t]).then_inc(prob_ready, 1)

            q_turned(0)
            q_turned(1)
            for t in range(TT):
                exponentials(0, t)
            for h in range(NH):
                for t in range(TT):
                    if h + 1 < NH:
                        exponentials(h + 1, t)
                if h:
                    act.wait_ge(*closed(("o", h - 1)))
                b = full(act, ("pt", h, TT - 1))
                release(("pt", h, TT - 1), act.activation(p_t[:, tri(TT - 1)], b, ACT.Copy))
                if h + 2 < NH:
                    q_turned(h + 2)
            act.wait_ge(*closed(("o", NH - 1)))
            load_gain(1, ffn_norm_2[1])
            split_rows("o_t", hi=h_hi, lo=h_lo)
            if stop == 5:
                act.wait_ge(gain_in, 48)
                ahead(len(chunk_src))
                return
            added = lambda t: ("w_o", 1, t)
            rms_and_split("ffn1", added, bank_ready(added), to_a)
            ev0[0] = evs[0]
            ffn("f3", False)
            ahead(len(chunk_src))

        @block.vector
        def _(v):
            steps, splits, evs, ev_split = [0], [0], [0], []
            pending = []

            def step(ins):
                ins.then_inc(dve_step, 1)
                steps[0] += 1
                v.wait_ge(dve_step, steps[0])

            def go(ins):
                ins.then_inc(dve_step, 1)
                steps[0] += 1

            def settle():
                v.wait_ge(dve_step, steps[0])

            def finish_split():
                if pending:
                    i, n, view, hi, lo = pending.pop()
                    v.wait_ge(hi_ready, n + 1)
                    v.tensor_tensor(lo, view(ev[:, i % 2, :]), hi.bitcast(F), ALU.subtract).then_inc(lo_ready, 1)

            def split_ev(name, write, view, hi, lo):
                i = evs[0]
                b = full(v, name)
                if i >= 2:
                    v.wait_ge(lo_ready, ev_split[i - 2] + 1)
                write(b, ev[:, i % 2, :]).then_inc(ev_ready, 1)
                finish_split()
                pending.append((i, splits[0], view, hi, lo))
                ev_split.append(splits[0])
                evs[0] += 1
                splits[0] += 1

            def split(name, view, hi, lo, scale=None):
                n = splits[0]
                b = view(full(v, name))
                v.wait_ge(hi_ready, n + 1)
                if scale is None:
                    ins = v.tensor_tensor(lo, b, hi.bitcast(F), ALU.subtract)
                else:
                    ins = v.scalar_tensor_tensor(lo, b, scale, hi.bitcast(F), ALU.mult, ALU.subtract)
                ins.then_inc(lo_ready, 1)
                splits[0] += 1

            def scaled(gain, kn=4):
                def write(b, e):
                    r = lambda a: a[:, 0:kn * P].rearrange("p (k c) -> p k c", k=kn)
                    g = gain.unsqueeze(2).to_broadcast([P, kn, P])
                    return v.tensor_tensor(r(e), r(b), g, ALU.mult)
                return write

            def split_rows(stage, nk=KT, gain=None, hi=a_hi, lo=a_lo, off=0):
                for t in range(TT):
                    for k in range(0, nk, 4):
                        kn = min(4, nk - k)
                        dst = tile_split(hi, lo, off + k, kn, t)
                        if gain is None:
                            split((stage, t, k // 4), *dst)
                        else:
                            split_ev((stage, t, k // 4), scaled(gain[:, k:k + kn], kn), *dst)
                finish_split()

            def xh_rows(first, t, gain):
                v.wait_ge(sq_ready, first + t + 1)
                step(v.reciprocal(st[:, 8 + t:9 + t], st[:, 4 + t:5 + t]))
                if gain is None:
                    ins = v.tensor_scalar(xh[:, t % 2, :], x_rows[:, t, :], st[:, 8 + t:9 + t], None, ALU.mult)
                else:
                    ins = v.scalar_tensor_tensor(xh[:, t % 2, :], x_rows[:, t, :], st[:, 8 + t:9 + t], gain[:, :],
                                                 ALU.mult, ALU.mult)
                ins.then_inc(xh_ready, 1)

            def split_tile(stage, t, dst):
                for k in range(2):
                    split((stage, t, k), *dst(t, k))

            def rms_and_split(stage, first, dst, gain=None):
                xh_rows(first, 0, gain)
                for t in range(TT):
                    if t + 1 < TT:
                        xh_rows(first, t + 1, gain)
                    split_tile(stage, t, dst)

            def to_a(t, k):
                return tile_split(a_hi, a_lo, 4 * k, 4, t)

            def to_a_s5(t, k):
                return (ev_s5, *tile_split_s5(4 * k, t))

            def add_rows(name, half, scale=None):
                for t in range(TT):
                    b = full(v, (*name, t))
                    o = x_rows[:, t, half * HALF:half * HALF + HALF]
                    if scale is None:
                        ins = v.tensor_tensor(o, b, o, ALU.add)
                    else:
                        ins = v.scalar_tensor_tensor(o, o, scale, b, ALU.mult, ALU.add)
                    last[t] = release((*name, t), ins)

            last = [None] * TT

            def ln_stats(t):
                v.wait_ge(*last[t])
                for c in range(2):
                    go(v.bn_stats(st[:, 48 + 12 * (t % 2) + 6 * c:54 + 12 * (t % 2) + 6 * c], x_rows[:, t, c * HALF:c * HALF + HALF]))
                settle()
                v.bn_aggr(st[:, 24 + 2 * t:26 + 2 * t], st[:, 48 + 12 * (t % 2):60 + 12 * (t % 2)]).then_inc(var_ready, 1)

            def ln_rows(t, i, sem_):
                v.wait_ge(ln_in[i], 32)
                v.wait_ge(ln_dev, i * TT + t + 1)
                v.wait_ge(var_ready, i * TT + t + 1)
                step(v.reciprocal(st[:, 40 + t:41 + t], st[:, 36 + t:37 + t]))
                o = x_rows[:, t, :]
                step(v.scalar_tensor_tensor(o, o, st[:, 24 + 2 * t:25 + 2 * t], ln_g[i][:, 0, :],
                                            ALU.subtract, ALU.mult))
                v.scalar_tensor_tensor(o, o, st[:, 40 + t:41 + t], ln_g[i][:, 1, :], ALU.mult, ALU.add)\
                 .then_inc(sem_, 1)

            def cmul(o_re, o_im, a_re, a_im, b_re, b_im, t1, t2):
                go(v.tensor_tensor(t1, a_re, b_re, ALU.mult))
                go(v.tensor_tensor(t2, a_im, b_im, ALU.mult))
                go(v.tensor_tensor(o_re, a_re, b_im, ALU.mult))
                go(v.tensor_tensor(o_im, a_im, b_re, ALU.mult))
                settle()
                go(v.tensor_tensor(o_im, o_im, o_re, ALU.add))
                settle()
                step(v.tensor_tensor(o_re, t1, t2, ALU.subtract))

            def reduced(ang, turns, out_):
                step(v.tensor_scalar(turns, ang, 1.0 / TWO_PI, ROUNDER, ALU.mult, ALU.add))
                step(v.tensor_scalar(turns, turns, ROUNDER, None, ALU.subtract))
                step(v.scalar_tensor_tensor(out_, turns, -PI2_A, ang, ALU.mult, ALU.add))
                step(v.scalar_tensor_tensor(out_, turns, -PI2_B, out_, ALU.mult, ALU.add))
                step(v.scalar_tensor_tensor(out_, turns, -PI2_C, out_, ALU.mult, ALU.add))
                step(v.tensor_scalar(out_, out_, PI_IN, -PI_IN, ALU.min, ALU.max))

            def quarter(out_, ang):
                step(v.scalar_tensor_tensor(out_, ang, -1.0, ang, ALU.mult, ALU.min))
                return v.tensor_scalar(out_, out_, TWO_PI / 4, None, ALU.add)

            def s5_tables():
                v.wait_ge(p_in, 16 * N_PARAM)
                r = release("lam", v.tensor_copy(lam[:, 0:2, :].rearrange("p a g -> p (a g)"), full(v, "lam")[:, 0:P]))
                v.wait_ge(*r)
                for i in range(2):
                    for h in range(2):
                        o = c_p[:, i, 32 * h:32 * h + 32, :].rearrange("p g k -> p (g k)")
                        b = full(v, ("c", i, h))
                        go(v.tensor_copy(o[0:NS], b[0:NS]))
                        r = release(("c", i, h), v.tensor_scalar(o[NS:P], b[NS:P], -1.0, None, ALU.mult))
                v.wait_ge(*r)
                for i in range(2):
                    go(v.tensor_copy(b_p[NS:P, i, :, :], b_p[0:NS, i, :, :]))
                settle()
                lr, li = lam[:, 0, :], lam[:, 1, :]
                s = lambda i: sm[:, i, :]
                v.wait_ge(tab_act, 1)
                step(v.tensor_tensor(s(1), lr, s(0), ALU.mult))
                v.tensor_tensor(s(2), li, s(0), ALU.mult).then_inc(tab_dve, 1)
                v.wait_ge(tab_dve, 1)
                reduced(s(2), s(4), s(5))
                quarter(s(6), s(5)).then_inc(tab_dve, 1)
                v.wait_ge(tab_act, 4)
                sn, cs, r = s(7), s(8), s(3)
                go(v.memset(pri[:, 0, 0, :], 1.0))
                go(v.memset(pri[:, 1, 0, :], 0.0))
                go(v.tensor_tensor(pri[:, 0, 1, :], r, cs, ALU.mult))
                go(v.tensor_tensor(pri[:, 1, 1, :], r, sn, ALU.mult))
                go(v.tensor_copy(s(9), cs))
                go(v.tensor_copy(s(10), sn))
                go(v.tensor_copy(s(11), r))
                settle()
                for _ in range(3):
                    cmul(s(12), s(13), s(9), s(10), s(9), s(10), s(14), s(15))
                    go(v.tensor_copy(s(9), s(12)))
                    go(v.tensor_copy(s(10), s(13)))
                    go(v.tensor_tensor(s(11), s(11), s(11), ALU.mult))
                    settle()
                step(v.tensor_copy(r8[:, :], s(11)))
                go(v.tensor_copy(turn[:, 0, 0, :], s(9)))
                go(v.tensor_copy(turn[:, 1, 0, :], s(10)))
                settle()
                for i in range(5):
                    a, b = turn[:, 0, i, :], turn[:, 1, i, :]
                    cmul(turn[:, 0, i + 1, :], turn[:, 1, i + 1, :], a, b, a, b, s(14), s(15))
                for lo_, n in ((1, 1), (1, 2), (1, 4)):
                    bc = lambda a: pri[:, a, n, :].unsqueeze(1).to_broadcast([P, n, G])
                    t1, t2 = (bt[:, a, 0:n * G].rearrange("p (k g) -> p k g", k=n) for a in range(2))
                    cmul(pri[:, 0, 1 + n:1 + 2 * n, :], pri[:, 1, 1 + n:1 + 2 * n, :],
                         pri[:, 0, 1:1 + n, :], pri[:, 1, 1:1 + n, :], bc(0), bc(1), t1, t2)
                ar, ai = pri[:, 0, 1, :], pri[:, 1, 1, :]
                go(v.tensor_scalar(s(9), ar, 1.0, None, ALU.subtract))
                go(v.tensor_tensor(s(10), lr, lr, ALU.mult))
                go(v.tensor_tensor(s(11), li, li, ALU.mult))
                settle()
                step(v.tensor_tensor(s(10), s(10), s(11), ALU.add))
                go(v.reciprocal(s(11), s(10)))
                go(v.tensor_tensor(s(12), s(9), lr, ALU.mult))
                go(v.tensor_tensor(s(13), ai, li, ALU.mult))
                go(v.tensor_tensor(s(14), ai, lr, ALU.mult))
                go(v.tensor_tensor(s(15), s(9), li, ALU.mult))
                settle()
                go(v.tensor_tensor(s(12), s(12), s(13), ALU.add))
                go(v.tensor_tensor(s(14), s(14), s(15), ALU.subtract))
                settle()
                go(v.tensor_tensor(s(12), s(12), s(11), ALU.mult))
                go(v.tensor_tensor(s(14), s(14), s(11), ALU.mult))
                settle()
                for q in range(2):
                    gs = slice(32 * q, 32 * q + 32)
                    br, bi = b_p[:, 0, gs, :], b_p[:, 1, gs, :]
                    fr, fi = (s(a)[:, gs].unsqueeze(2).to_broadcast([P, 32, GK]) for a in (12, 14))
                    t1, t2 = (bt[:, a, :].rearrange("p (g k) -> p g k", g=32) for a in range(2))
                    go(v.tensor_tensor(t1, bi, fi, ALU.mult))
                    go(v.tensor_tensor(t2, br, fi, ALU.mult))
                    settle()
                    go(v.tensor_tensor(br, br, fr, ALU.mult))
                    go(v.tensor_tensor(bi, bi, fr, ALU.mult))
                    settle()
                    go(v.tensor_tensor(br, br, t1, ALU.subtract))
                    go(v.tensor_tensor(bi, bi, t2, ALU.add))
                    settle()
                top, bot = slice(0, NS), slice(NS, P)
                for i, h, a, sign in ((0, top, 0, 1.0), (0, bot, 1, 1.0), (1, top, 1, -1.0), (1, bot, 0, 1.0)):
                    go(v.tensor_scalar(pw[h, i, :, :], pri[h, a, :, :], sign, None, ALU.mult))
                settle()

            go(v.memset(eps_c[:, 0:1], 1e-5))
            go(v.memset(eps_c[:, 1:2], 1e-6))
            settle()
            split_rows("x")
            v.wait_ge(c_in, 16 * N_CONST)
            for nm, dst in (("q", q_r), ("k", k_r)):
                for t in range(TT):
                    b = full(v, (nm, t)).rearrange("p (h e) -> p h e", h=RH)
                    c_ = rope_c[:, 0, t, :].unsqueeze(1).to_broadcast([P, RH, 64])
                    s_ = rope_c[:, 1, t, :].unsqueeze(1).to_broadcast([P, RH, 64])
                    lo_, hi_ = b[:, :, 0:64], b[:, :, 64:P]
                    r0, r1 = (rtmp[:, a, :].rearrange("p (h e) -> p h e", h=RH) for a in range(2))
                    go(v.tensor_tensor(dst[:, t, :, 0:64], lo_, c_, ALU.mult))
                    go(v.tensor_tensor(dst[:, t, :, 64:P], lo_, s_, ALU.mult))
                    go(v.tensor_tensor(r0, hi_, s_, ALU.mult))
                    settle()
                    w = release((nm, t), v.tensor_tensor(r1, hi_, c_, ALU.mult))
                    go(v.tensor_tensor(dst[:, t, :, 0:64], dst[:, t, :, 0:64], r0, ALU.subtract))
                    v.wait_ge(*w)
                    settle()
                    v.tensor_tensor(dst[:, t, :, 64:P], dst[:, t, :, 64:P], r1, ALU.add)\
                     .then_inc(rope_ready if nm == "k" else dve_step, 1)
                    if nm == "q":
                        steps[0] += 1
                        settle()
                    else:
                        v.wait_ge(rope_ready, t + 1)
            if stop > 1:
                s5_tables()

            for pad in (pool_p, pool_a, pool_b):
                go(v.memset(pad[:, 0:PADW], 0.0))
            settle()
            for h in range(RH):
                for nm, dst in (("q", q_t), ("k", k_t)):
                    i = bank_no[(nm, "t", h)]
                    release((nm, "t", h), v.tensor_copy(dst[:, h, :], full(v, (nm, "t", h))))
                w = release(("p", h), v.tensor_copy(pool_p[:, PADW:], full(v, ("p", h))))
                v.wait_ge(*w)
                src, win = pool_p, 1
                for r in range(h + 1):
                    dst = (pool_a, pool_b)[r % 2]
                    step(v.tensor_tensor(dst[:, PADW:], src[:, PADW:], src[:, PADW - win:PADW - win + SEQ], ALU.add))
                    src, win = dst, 2 * win
                other = (pool_a, pool_b)[(h + 1) % 2]
                go(v.tensor_tensor(other[:, PADW:2 * PADW], src[:, PADW:2 * PADW], cnt16[:, h, :], ALU.mult))
                settle()
                o = pool_out(h)
                go(v.scalar_tensor_tensor(o[:, PADW:], src[:, 2 * PADW:], 1.0 / win, pool_p[:, 2 * PADW:],
                                          ALU.mult, ALU.subtract))
                v.tensor_tensor(o[:, 0:PADW], other[:, PADW:2 * PADW], pool_p[:, PADW:2 * PADW], ALU.subtract)\
                 .then_inc(pool_ready, 1)
                settle()
                v.wait_ge(pool_ready, h + 1)
            for h in range(RH):
                for j in range(TT):
                    n = SEQ - j * P
                    off = j * SEQ - P * (j * (j - 1) // 2)
                    b = full(v, ("s", h, j))
                    v.tensor_tensor(s_t[h % 2][:, off:off + n], b[:, 0:n], decay[:, h, 0:n], ALU.mult)\
                     .then_inc(decayed, 1)
                b = full(v, ("ret", h)).rearrange("p (t e) -> p t e", t=TT)
                vh = v_r[:, :, h, :]
                w = release(("ret", h), v.tensor_copy(vh, b))
                v.wait_ge(*w)
                sqv = sqs[:, :].rearrange("p (t e) -> p t e", t=TT)
                step(v.tensor_tensor(sqv, vh, vh, ALU.mult))
                v.tensor_reduce(st[:, 4 * h:4 * h + 4], sqv, AX.X, ALU.add).then_inc(ret_raw, 1)
                split(("pool", h), *row_split(a_hi, a_lo, RH + h), scale=ps_c[:, h:h + 1])
                v.wait_ge(ret_dev, h + 1)
                step(v.reciprocal(st[:, 32:36], st[:, 16 + 4 * h:20 + 4 * h]))
                step(v.tensor_tensor(vh, vh, st[:, 32:36].unsqueeze(2).to_broadcast([P, TT, P]), ALU.mult))
                if h == 0:
                    v.wait_ge(*freed[bank_no[("g", TT - 1)]])
                v.tensor_tensor(vh, vh, g_r[:, :, h, :], ALU.mult).then_inc(ret_ready, 1)
            for h in range(RH):
                split(("ret_t", h), *row_split(a_hi, a_lo, h))
            def s5_phases(e):
                gs = slice(e * EB, e * EB + EB)
                if e:
                    v.wait_ge(e_out, 16 * e * (EB // GB))
                go(v.memset(e_t[:, 0, :, 0:1], 1.0))
                go(v.memset(e_t[:, 1, :, 0:1], 0.0))
                settle()
                n = 1
                while n < NC:
                    k = n.bit_length() - 1
                    bc = lambda a: turn[:, a, k, gs].unsqueeze(2).to_broadcast([P, EB, n])
                    t1, t2 = (a[:, 0:EB * n].rearrange("p (g c) -> p g c", g=EB) for a in (tmp1, tmp2))
                    cmul(e_t[:, 0, :, n:2 * n], e_t[:, 1, :, n:2 * n], e_t[:, 0, :, 0:n], e_t[:, 1, :, 0:n],
                         bc(0), bc(1), t1, t2)
                    n *= 2
                v.tensor_scalar(e_t[NS:P, 1, :, :], e_t[NS:P, 1, :, :], -1.0, None, ALU.mult).then_inc(e_w, 1)
                v.wait_ge(e_w, e + 1)

            def s5_batch(f):
                gs = slice(f * GB, f * GB + GB)
                t1 = tmp1[:, 0:GB * T * GK].rearrange("p (g s k) -> p g s k", g=GB, s=T)
                if f:
                    v.wait_ge(*closed(("s5k", f - 1)))
                for a, o in ((0, h_b[:, :, :, :]), (1, t1)):
                    go(v.tensor_tensor(o, b_p[:, a, gs, :].unsqueeze(2).to_broadcast([P, GB, T, GK]),
                                       pw[:, a, T - 1::-1, gs].rearrange("p s g -> p g s").unsqueeze(3)
                                       .to_broadcast([P, GB, T, GK]), ALU.mult))
                settle()
                step(v.tensor_tensor(h_b[:, :, :, :].rearrange("p g s k -> p (g s k)"),
                                     h_b[:, :, :, :].rearrange("p g s k -> p (g s k)"), tmp1[:, 0:GB * T * GK], ALU.add))
                if f:
                    v.wait_ge(st_out, 16 * f)
                cp = stage[:, P_O:P_O + GB * 144].rearrange("p (g s k) -> p g s k", g=GB, s=T + 1)
                t2 = tmp2[:, :].rearrange("p (g s k) -> p g s k", g=GB, s=T + 1)
                for a, o in ((0, cp), (1, t2)):
                    go(v.tensor_tensor(o, c_p[:, a, gs, :].unsqueeze(2).to_broadcast([P, GB, T + 1, GK]),
                                       pw[:, a, :, gs].rearrange("p s g -> p g s").unsqueeze(3)
                                       .to_broadcast([P, GB, T + 1, GK]), ALU.mult))
                settle()
                o = stage[:, P_O:P_O + GB * 144]
                step(v.tensor_tensor(o, o, tmp2[:, :], ALU.add))
                q = stage[:, Q_O:Q_O + GB * P].rearrange("p (g c) -> p g c", g=GB)
                c1 = o.rearrange("p (g c) -> p g c", g=GB)[:, :, GK:]
                go(v.tensor_copy(q[0:NS], c1[NS:P]))
                v.tensor_copy(q[NS:P], c1[0:NS]).then_inc(tables_ready, 1)

            def s5_batch_out(f):
                b = full(v, ("s5w", f)).rearrange("p (g c) -> p g c", g=GB)
                w = stage[:, W_O:W_O + 768].rearrange("p (g c) -> p g c", g=GB)
                go(v.tensor_copy(w[:, :, 0:P], b))
                r = release(("s5w", f), v.tensor_copy(w[:, :, P:], b[:, :, 0:NS]))
                v.wait_ge(*r)
                v.wait_ge(tables_ready, f + 1)
                if f:
                    v.wait_ge(k_out, 16 * T * f)
                b = full(v, ("s5k", f))[0:GK, :].rearrange("p (g c) -> p g c", g=GB)
                r = release(("s5k", f), v.tensor_copy(k_s[:, :, KPAD:], b))
                v.wait_ge(*r)
                settle()
                for g in range(GB):
                    o = k_s[:, g, KPAD:KPAD + GK]
                    ins = v.scalar_tensor_tensor(o, ident[0:GK, 0:GK], d_t[:, f * GB + g:f * GB + g + 1], o,
                                                 ALU.mult, ALU.add)
                    if g < GB - 1:
                        go(ins)
                    else:
                        ins.then_inc(k_w, 1)
                settle()
                v.memset(st[:, 191:192], 0.0).then_inc(stage_w, 1)

            if stop > 1:
                go(v.memset(k_s[:, :, 0:KPAD], 0.0))
                settle()
                s5_phases(0)
            for half in range(2):
                if stop > 1:
                    s5_batch(out_batch[half])
                    s5_batch_out(out_batch[half])
                add_rows(("w_out", half), half, ALPHA)
            if stop == 1:
                return
            ln_stats(0)
            for t in range(TT):
                if t + 1 < TT:
                    ln_stats(t + 1)
                ln_rows(t, 0, xh_ready)
                if t:
                    split_tile("ln1", t - 1, to_a)
            split_tile("ln1", TT - 1, to_a)

            def down_and_add(stage, g, scale=None):
                for half in range(2):
                    add_rows((stage, "down", g, half), half, scale if g == 0 else None)

            gbuf = xh[:, 0, 0:SEQ + 2]
            step(v.memset(gbuf[:, 0:2], 0.0))
            for g, (f0, f1) in enumerate(GROUPS):
                for f in range(f0, f1):
                    v.wait_ge(gate_pre, f + 1)
                    c_ = gconv[:, f % 2, :]
                    step(v.scalar_tensor_tensor(c_, gbuf[:, 1:1 + SEQ], cw_c[:, 1, f:f + 1], c_, ALU.mult, ALU.add))
                    v.scalar_tensor_tensor(c_, gbuf[:, 0:SEQ], cw_c[:, 0, f:f + 1], c_, ALU.mult, ALU.add)\
                     .then_inc(gate_conv, 1)
                    v.wait_ge(gate_act, f + 1)
                    split_ev(("f1", "val", f), lambda b, e: v.tensor_tensor(e, b, gconv[:, f % 2, :], ALU.mult),
                          *row_split(h_hi, h_lo, f - f0))
                    if f - 1 in up_batch:
                        s5_batch_out(up_batch[f - 1])
                    if f in up_phases:
                        s5_phases(up_phases[f])
                    if f in up_batch:
                        s5_batch(up_batch[f])
                finish_split()
                for half in range(2):
                    if (g, half) in down_phases:
                        s5_phases(down_phases[g, half])
                    if (g, half) in down_batch:
                        s5_batch(down_batch[g, half])
                        s5_batch_out(down_batch[g, half])
                    add_rows(("f1", "down", g, half), half, ALPHA if g == 0 else None)
            if stop > 2:
                v.wait_ge(gain_in, 16)
            ln_stats(0)
            for t in range(TT + 2):
                if t + 1 < TT:
                    ln_stats(t + 1)
                if t < TT:
                    ln_rows(t, 1, ln_ready)
                if stop > 2 and 1 <= t <= TT:
                    xh_rows(0, t - 1, gain_row[0])
                if stop > 2 and t >= 2:
                    split_tile("mix0", t - 2, to_a_s5)
            if stop == 2:
                return
            go(v.memset(zc[:, :, :, :, 0:1], 0.0))
            settle()
            for half in range(2):
                for j in range(4):
                    v.tensor_copy(u_c[:, 32 * half:32 * half + 32, 2 * j, :],
                                  full(v, ("u", half, j))[0:NC, :].rearrange("c (g k) -> c g k", k=GK))\
                     .then_inc(u_even, 1)
            for b_ in range(NB):
                b = full(v, ("sv", b_))
                v.wait_ge(rec_in[b_ % 3], 16 * (b_ // 3 + 1))
                cs, sn = rec[b_ % 3][:, C_O:C_O + 256], rec[b_ % 3][:, S_O:S_O + 256]
                go(v.tensor_tensor(z1[:, :], b[:, 0:256], cs, ALU.mult))
                r = release(("sv", b_), v.tensor_tensor(z2[:, :], b[:, 256:512], sn, ALU.mult))
                settle()
                v.wait_ge(*r)
                step(v.tensor_tensor(z1[:, :], z1[:, :], z2[:, :], ALU.add))
                for g in range(GB):
                    gg = b_ * GB + g
                    s = slice(g * NC, g * NC + NC)
                    go(v.tensor_tensor_scan(z3[:, s], r8[:, gg:gg + 1].to_broadcast([P, NC]), z1[:, s], 0.0,
                                            ALU.mult, ALU.add))
                settle()
                if b_ >= 2:
                    v.wait_ge(*closed(("y", b_ - 2)))
                zv = z3[:, :].rearrange("p (g c) -> p g c", g=GB)[:, :, 0:NC - 1]
                cv = cs.rearrange("p (g c) -> p g c", g=GB)[:, :, 0:NC - 1]
                sv = sn.rearrange("p (g c) -> p g c", g=GB)[:, :, 0:NC - 1]
                step(v.tensor_tensor(zc[:, b_ % 2, 0, :, 1:], zv, cv, ALU.mult))
                v.tensor_tensor(zc[:, b_ % 2, 1, :, 1:], zv, sv, ALU.mult).then_inc(zc_ready, 1)
                v.wait_ge(zc_ready, b_ + 1)
                if b_ >= 3 and b_ % 2:
                    split(("zt", (b_ - 3) // 2), *turned_back((b_ - 3) // 2))
            split(("zt", KT - 1), *turned_back(KT - 1))
            for half in range(2):
                for t in range(TT):
                    b = full(v, ("glu_v", half, t))
                    v.wait_ge(*freed[bank_no[("glu_g", half, t)]])
                    o = x_rows[:, t, half * HALF:half * HALF + HALF]
                    step(v.tensor_tensor(ev[:, 0, :], b, sig[:, t, :], ALU.mult))
                    last[t] = release(("glu_v", half, t), v.tensor_tensor(o, o, ev[:, 0, :], ALU.add))
                    v.wait_ge(*last[t])
            if stop == 3:
                return

            def swiglu(stage):
                e0 = splits[0]
                for g, (f0, f1) in enumerate(GROUPS):
                    for f in range(f0, f1):
                        n_gate[0] += 1
                        v.wait_ge(gate_act, n_gate[0])
                        split_ev((stage, "val", f), lambda b, e: v.tensor_tensor(e, b, xh[:, f % 2, 0:SEQ], ALU.mult),
                              *row_split(h_hi, h_lo, f - f0))
                    finish_split()
                    down_and_add(stage, g)

            n_gate = [FT]
            v.wait_ge(gain_in, 32)
            rms_and_split("ffn0", TT, to_a, gain_row[1])
            swiglu("f2")
            if stop == 4:
                return

            rms_and_split("mla", 2 * TT, to_a)
            v.wait_ge(m_in, 16 * 7)
            go(v.memset(gcol[NOPE:QK, :], 1.0))
            step(v.tensor_copy(st[:, 130:134], pos_i[:, :]))
            for t in range(TT):
                go(v.tensor_scalar(rot[:, 0, 4 + t, :], frq[:, :], st[:, 130 + t:131 + t], None, ALU.mult))
            settle()
            reduced(rot[:, 0, 4:8, :], rot[:, 1, 4:8, :], rot[:, 0, 0:4, :])
            quarter(rot[:, 1, 0:4, :], rot[:, 0, 0:4, :]).then_inc(tab_dve, 1)
            for t in range(TT):
                w = release(("kv_a", t), v.tensor_copy(ckv[:, t, :], full(v, ("kv_a", t))[:, 0:KVR + ROPE]))
                v.wait_ge(*w)
                v.memset(st[:, 190:191], 0.0).then_inc(lat_in, 1)
            for t in range(TT):
                v.wait_ge(lat_dev, t + 1)
                step(v.reciprocal(st[:, 16 + 2 * t:18 + 2 * t], st[:, 8 + 2 * t:10 + 2 * t]))
                c_ = ckv[:, t, 0:KVR]
                v.tensor_scalar(c_, c_, st[:, 16 + 2 * t:17 + 2 * t], None, ALU.mult).then_inc(ckv_ready, 1)
            for t in range(TT):
                w = release(("q_a", t), v.tensor_copy(cq[:, t, :], full(v, ("q_a", t))[:, 0:QR]))
                v.wait_ge(*w)
                v.memset(st[:, 190:191], 0.0).then_inc(lat_in, 1)
            for t in range(TT):
                v.wait_ge(lat_dev, TT + t + 1)
                step(v.reciprocal(st[:, 48 + t:49 + t], st[:, 40 + t:41 + t]))
                v.tensor_scalar(cq[:, t, :], cq[:, t, :], st[:, 48 + t:49 + t], None, ALU.mult).then_inc(cq_ready, 1)
            split_rows("ckv_t", KVR // P, gain=kva_g)
            split_rows("cq_t", QR // P, gain=qa_g, off=2)
            v.wait_ge(tab_act, 6)
            for i, (fn, half) in enumerate(((0, 0), (1, 1), (1, 0), (0, 1))):
                g = hg[:, ROPE + half * ROPE // 2:ROPE + (half + 1) * ROPE // 2].unsqueeze(1)\
                    .to_broadcast([P, TT, ROPE // 2])
                go(v.tensor_tensor(q_trig[:, i, :, :], trig[:, fn, :, :], g, ALU.mult))
            settle()
            v.memset(st[:, 189:190], 0.0).then_inc(trig_ready, 1)
            for t in range(TT):
                kr = ckv[:, t, KVR:]
                go(v.scalar_tensor_tensor(kr, kr, st[:, 17 + 2 * t:18 + 2 * t], hg[:, 0:ROPE], ALU.mult, ALU.mult))
            settle()
            k1, k2, t1, t2 = (rot[:, a, o:o + TT, :] for a in range(2) for o in (8, 12))
            cmul(k1, k2, ckv[:, :, KVR:KVR + ROPE // 2], ckv[:, :, KVR + ROPE // 2:],
                 trig[:, 0, :, :], trig[:, 1, :, :], t1, t2)
            for k_, o in ((k1, NOPE), (k2, NOPE + ROPE // 2)):
                go(v.tensor_copy(k_n[:, :, :, o:o + ROPE // 2],
                                 k_.unsqueeze(2).to_broadcast([P, TT, NH, ROPE // 2])))
            settle()

            def normalised(n):
                q, c = divmod(n, HC)
                v.wait_ge(dev_made, n + 1)
                rows = slice(HN * c, HN * c + HN)
                go(v.reciprocal(nrm[:, 2, q, c, :], nrm[:, 1, q, c, :]))
                if q:
                    go(v.reciprocal(nrm[:, 2, 2, c, :], nrm[:, 1, 2, c, :]))
                    for t in range(TT):
                        v.wait_ge(*freed[bank_no[("q_b", c, t)]])
                settle()
                inv = lambda a, e: nrm[:, 2, a, c, :].rearrange("p (t h) -> p t h", t=TT).unsqueeze(3)\
                    .to_broadcast([P, TT, HN, e])
                if q:
                    x_ = q_n[:, :, rows, 0:NOPE]
                    go(v.tensor_tensor(x_, x_, inv(1, NOPE), ALU.mult))
                    v.wait_ge(q_roped, c + 1)
                    x_ = q_n[:, :, rows, NOPE:]
                    settle()
                    v.tensor_tensor(x_, x_, inv(2, ROPE), ALU.mult).then_inc(qk_rows, 1)
                else:
                    x_ = k_n[:, :, rows, 0:NOPE]
                    v.tensor_tensor(x_, x_, inv(0, NOPE), ALU.mult).then_inc(qk_rows, 1)

            for n in range(2 * HC):
                q, c = divmod(n, HC)
                for t in range(TT):
                    i = n * TT + t
                    v.wait_ge(sq_made, i + 1)
                    sums = lambda a: nrm[:, 0, a, c, HN * t:HN * t + HN]
                    if q:
                        s3 = sq[:, i % 2, 0:HN * QK].rearrange("p (h e) -> p h e", h=HN)
                        step(v.tensor_reduce(sums(2), s3[:, :, NOPE:], AX.X, ALU.add))
                        v.tensor_reduce(sums(1), s3[:, :, 0:NOPE], AX.X, ALU.add).then_inc(sum_made, 1)
                    else:
                        s3 = sq[:, i % 2, 0:HN * NOPE].rearrange("p (h e) -> p h e", h=HN)
                        v.tensor_reduce(sums(0), s3, AX.X, ALU.add).then_inc(sum_made, 1)
                        v.wait_ge(k_copied, i + 1)
                        b = full(v, ("kv_b", c, t)).rearrange("p (h e) -> p h e", h=HN)
                        release(("kv_b", c, t), v.tensor_copy(v_n[:, t, HN * c:HN * c + HN, :], b[:, :, NOPE:]))
                    if t == 2 and n:
                        normalised(n - 1)
            normalised(2 * HC - 1)

            def k_turned(h):
                release(("ht", 1, h), v.tensor_scalar(qk_t[:, h % 2, 1, :], full(v, ("ht", 1, h))[0:QK, :],
                                                      gcol[:, 1:2], None, ALU.mult))

            def masked(h, t):
                b = full(v, ("sc", h, t))
                w = (t + 1) * P
                v.tensor_tensor_reduce(b[:, 0:w], b[:, 0:w], mask[:, SEQ - w:], -QK ** -0.5, 3e38, ALU.add, ALU.min,
                                       st[:, 8 * (h % 2) + t:8 * (h % 2) + t + 1]).then_inc(max_ready, 1)

            k_turned(0)
            k_turned(1)
            for t in range(TT):
                masked(0, t)
            for h in range(NH):
                for t in range(TT):
                    if h + 1 < NH:
                        masked(h + 1, t)
                    if h and t == 0:
                        v.wait_ge(*closed(("o", h - 1)))
                    if t < TT - 1:
                        release(("pt", h, t), v.tensor_copy(p_t[:, tri(t)], full(v, ("pt", h, t))[:, 0:(t + 1) * P]))
                if h + 2 < NH:
                    k_turned(h + 2)
                v.wait_ge(prob_ready, (h + 1) * TT)
                rs = st[:, 16 + 8 * (h % 2):16 + 8 * (h % 2) + TT]
                step(v.reciprocal(st[:, 32:32 + TT], rs))
                b = full(v, ("o", h))[:, 0:TT * VD].rearrange("p (t e) -> p t e", t=TT)
                w = release(("o", h), v.tensor_tensor(o_n[:, :, h * VD:h * VD + VD], b,
                                                      st[:, 32:32 + TT].unsqueeze(2).to_broadcast([P, TT, VD]),
                                                      ALU.mult))
                v.wait_ge(*w)
            split_rows("o_t", hi=h_hi, lo=h_lo)
            for half in range(2):
                add_rows(("w_o", half), half)
            if stop == 5:
                return
            v.wait_ge(gain_in, 48)
            rms_and_split("ffn1", 3 * TT, to_a, gain_row[1])
            swiglu("f3")


_INS = ['x', 'w_in', 'w_pool', 'pool_scale', 'w_out', 'ln1_g', 'ln1_b', 'w_up', 'conv_w', 'conv_b', 'w_down',
        'ln2_g', 'ln2_b', 'positions_2', 'mix_norm_2', 'ffn_norm_2', 'ffn_w_gate_up_2', 'ffn_w_down_2',
        'ssm_w_in_2', 'ssm_lambda_re_2', 'ssm_lambda_im_2', 'ssm_log_step_2', 'ssm_b_re_2', 'ssm_b_im_2',
        'ssm_c_re_2', 'ssm_c_im_2', 'ssm_d_2', 'ssm_w_glu_2', 'kv_in_norm_2', 'mla_w_kv_a_2', 'mla_kv_a_norm_2',
        'mla_w_kv_b_2', 'mla_k_nope_norm_2', 'mla_k_rope_norm_2', 'mla_w_q_a_2', 'mla_q_a_norm_2',
        'mla_w_q_b_2', 'mla_q_nope_norm_2', 'mla_q_rope_norm_2', 'mla_w_o_2']


def kernel(**inputs):
    import concourse.bacc as bacc
    from concourse.bass_utils import run_bass_kernel_spmd as run

    nc = bacc.Bacc("TRN2", target_bir_lowering=False, num_devices=1)
    arrays, args = {}, []
    given = {name: np.ascontiguousarray(inputs[name]) for name in _INS}
    given.update(constants())
    for name, a in given.items():
        arrays[f"in_{name}_dram"] = a
        args.append(nc.dram_tensor(f"in_{name}_dram", a.shape, mybir.dt.from_np(a.dtype), kind="ExternalInput").ap())
    args.append(nc.dram_tensor("out_dram", (1, SEQ, D), F, kind="ExternalOutput").ap())
    program(nc, 9, *args)
    r = run(nc, [arrays], core_ids=[0])
    return r.results[0]["out_dram"]
```

```python
from contextlib import ExitStack

import numpy as np

import concourse.bass as bass
from concourse import mybir

F = mybir.dt.float32
R = mybir.dt.float32r
I32 = mybir.dt.int32
ALU = mybir.AluOpType
ACT = mybir.ActivationFunctionType
AX = mybir.AxisListType

P = 128
SEQ, D = 512, 1024
TT = SEQ // P
KT = D // P
FF = 2816
FT = FF // P
GROUPS = ((0, 8), (8, 15), (15, 22))
HALF = 512
RH, POOLG = 4, 4
CHUNK = 64
ALPHA = 2.0 ** 0.25
RING = 3
CW = 1024
G, GK, NS = 64, 16, 64
T = P // GK
NC = SEQ // T
GB = 4
NB = G // GB
EB = 16
W_O, P_O, Q_O, M_O, C_O, S_O = 0, 768, 1344, 1856, 2368, 2624
REC = 2880
NH, NOPE, ROPE, VD = 16, 64, 32, 64
QK = NOPE + ROPE
HN = 4
HC = NH // HN
KVR, QR = 256, 384
TWO_PI = 2.0 * np.pi
ROUNDER = 1.5 * 2.0 ** 23
PI2_A = 6.28125
PI2_B = float(np.float32(round((TWO_PI - PI2_A) * 2 ** 21) / 2 ** 21))
PI2_C = float(np.float32(TWO_PI - PI2_A - PI2_B))
PI_IN = float(np.nextafter(np.float32(np.pi), np.float32(0)))
N_CONST, N_TURNED, N_PARAM = 13, 8, 4


def constants():
    f8 = np.float64
    c = {}
    c["c_ident"] = np.eye(P, dtype=np.float32)
    inv = (10000.0 ** (-np.arange(0, P, 2, dtype=np.float32) / np.float32(P))).astype(np.float32)
    ang = (np.arange(SEQ, dtype=np.float32)[:, None] * inv[None, :]).astype(np.float32).astype(f8)
    c["c_rope"] = np.stack([np.cos(ang), np.sin(ang)]).astype(np.float32)
    lg = np.log(1.0 - 2.0 ** (-5.0 - np.arange(RH, dtype=f8)))
    j, i = np.arange(P)[:, None], np.arange(SEQ)[None, :]
    seen = (j // CHUNK) <= (i // CHUNK)
    c["c_decay"] = np.stack([np.where(seen, np.exp(g * np.abs(i - j)), 0.0) * P ** -0.5 for g in lg]).astype(np.float32)
    c["c_count"] = np.stack([1.0 / np.minimum(np.arange(1, SEQ + 1), w) for w in (2, 4, 8, 16)]).astype(np.float32)
    c["c_freq"] = (10000.0 ** (-np.arange(0, ROPE, 2, dtype=np.float32) / np.float32(ROPE))).astype(np.float32)
    c["c_mask"] = np.where(np.arange(SEQ)[None, :] <= SEQ - P + np.arange(P)[:, None], 0.0, -1e30).astype(np.float32)
    return c


def program(nc, x, w_in, w_pool, pool_scale, w_out, ln1_g, ln1_b, w_up, conv_w, conv_b, w_down, ln2_g, ln2_b,
            positions_2, mix_norm_2, ffn_norm_2, ffn_w_gate_up_2, ffn_w_down_2, ssm_w_in_2,
            ssm_lambda_re_2, ssm_lambda_im_2, ssm_log_step_2, ssm_b_re_2, ssm_b_im_2, ssm_c_re_2,
            ssm_c_im_2, ssm_d_2, ssm_w_glu_2, kv_in_norm_2, mla_w_kv_a_2, mla_kv_a_norm_2, mla_w_kv_b_2,
            mla_k_nope_norm_2, mla_k_rope_norm_2, mla_w_q_a_2, mla_q_a_norm_2, mla_w_q_b_2,
            mla_q_nope_norm_2, mla_q_rope_norm_2, mla_w_o_2,
            c_ident, c_rope, c_decay, c_count, c_freq, c_mask, out):
    rec_dram = nc.dram_tensor("s5_records", [NB, P, REC], F, kind="Internal").ap()
    with ExitStack() as ctx:
        ctx.enter_context(nc.allow_non_contiguous_dma(reason="small parameter tables"))
        base = (nc.sbuf_base + 31) // 32 * 32
        KB = 1024
        at_now = [base]

        def fixed(name, shape, dt):
            t = nc.alloc_sbuf_tensor_at(name, shape, dt, offset=at_now[0])
            at_now[0] += (int(np.prod(shape[1:])) * 4 + 31) // 32 * 32
            return t

        x_rows = fixed("x_rows", [P, TT, D], F)
        a_hi = fixed("a_hi", [P, KT, SEQ], R)
        a_lo = fixed("a_lo", [P, KT, SEQ], R)
        w_raw = fixed("w_raw", [P, RING, CW], F)
        w_hi = fixed("w_hi", [P, RING, CW], R)
        w_lo = fixed("w_lo", [P, RING, CW], R)
        xh = fixed("xh", [P, 2, D], F)
        ev = fixed("ev", [P, 2, HALF], F)
        ident = fixed("ident", [P, P], F)
        gains = fixed("gains", [P, 2, KT], F)
        kva_g = fixed("kva_g", [P, 2], F)
        qa_g = fixed("qa_g", [P, 3], F)
        cw_c = fixed("cw_c", [P, 3, FT], F)
        cb_c = fixed("cb_c", [P, FT], F)
        ps_c = fixed("ps_c", [P, POOLG], F)
        st = fixed("st", [P, 192], F)
        eps_c = fixed("eps_c", [P, 4], F)
        arena = at_now[0]
        room = nc.sbuf_top - arena

        def scratch(name, shape, dt, kb, extra=0):
            size = int(np.prod(shape[1:])) * 4
            off = int(kb * KB) + extra
            assert off + size <= room, (name, off + size, room)
            return nc.alloc_sbuf_tensor_at(name, shape, dt, offset=arena + off)

        h_hi = scratch("h_hi", [P, 8, SEQ], R, 0)
        h_lo = scratch("h_lo", [P, 8, SEQ], R, 16)
        q_r = scratch("q_r", [P, TT, RH, P], F, 0)
        k_r = scratch("k_r", [P, TT, RH, P], F, 8)
        v_r = scratch("v_r", [P, TT, RH, P], F, 16)
        g_r = scratch("g_r", [P, TT, RH, P], F, 24)
        q_t = scratch("q_t", [P, RH, SEQ], F, 32)
        k_t = scratch("k_t", [P, RH, SEQ], F, 40)
        decay = scratch("decay", [P, RH, SEQ], F, 48)
        PADW = 16
        pool_p = scratch("pool_p", [P, PADW + SEQ], F, 56)
        pool_a = scratch("pool_a", [P, PADW + SEQ], F, 56, 4 * (PADW + SEQ))
        pool_b = scratch("pool_b", [P, PADW + SEQ], F, 84)
        wpool = scratch("wpool", [P, POOLG, P], F, 80)
        rope_c = scratch("rope_c", [P, 2, TT, 64], F, 78)
        rtmp = scratch("rtmp", [P, 2, HALF // 2], F, 84)
        s_t = [scratch(f"s_t{i}", [P, 1280], F, 8 * i) for i in range(2)]
        ln_g = [scratch("ln1_gb", [P, 2, D], F, 32), scratch("ln2_gb", [P, 2, D], F, 62)]
        cnt16 = scratch("cnt16", [P, POOLG, PADW], F, 82)
        b_p = scratch("b_p", [P, 2, G, GK], F, 62)
        c_p = scratch("c_p", [P, 2, G, GK], F, 70)
        c_nat = scratch("c_nat", [P, 2, 8, 2, NS], F, 40)
        lam_nat = scratch("lam_nat", [G, 2, 2, NS], F, 96)
        pri = scratch("pri", [P, 2, T + 1, G], F, 32)
        sm = scratch("sm", [P, 18, G], F, 37)
        bt = scratch("bt", [P, 2, HALF], F, 42)
        pw = scratch("pw", [P, 2, T + 1, G], F, 88)
        turn = scratch("turn", [P, 2, 6, G], F, 92.75)
        r8 = scratch("r8", [P, G], F, 95.75)
        lam = scratch("lam", [P, 3, G], F, 97)
        d_t = scratch("d_t", [GK, G], F, 97.75)
        stage = scratch("stage", [P, M_O], F, 41)
        tmp1 = scratch("tmp1", [P, 576], F, 48.5)
        tmp2 = scratch("tmp2", [P, 576], F, 50.75)
        h_b = scratch("h_b", [P, GB, T, GK], F, 53)
        KPAD = P - GK
        k_s = scratch("k_s", [GK, GB, KPAD + P], F, 55)
        e_t = scratch("e_t", [P, 2, EB, NC], F, 78)
        u_c = scratch("u_c", [NC, G, T, GK], F, 0)
        rec = [scratch(f"rec{i}", [P, REC], F, 32 + 11.25 * i) for i in range(3)]
        u_t = scratch("u_t", [P, 3, GB * NC], F, 66)
        z1 = scratch("z1", [P, GB * NC], F, 69)
        z2 = scratch("z2", [P, GB * NC], F, 70)
        z3 = scratch("z3", [P, GB * NC], F, 71)
        zc = scratch("zc", [P, 2, 2, GB, NC], F, 72)
        y_c = scratch("y_c", [NC, 2, T, P], F, 76)
        gain_row = [scratch("gain_row0", [P, D], F, 70), scratch("gain_row1", [P, D], F, 40)]
        sig = scratch("sig", [P, TT, HALF], F, 68)
        q_n = scratch("q_n", [P, TT, NH, QK], F, 0)
        v_n = scratch("v_n", [P, TT, NH, VD], F, 24)
        k_n = scratch("k_n", [P, TT, NH, QK], F, 40)
        ckv = scratch("ckv", [P, TT, KVR + ROPE], F, 64)
        cq = scratch("cq", [P, TT, QR], F, 68.5)
        sq = xh[:, 0, 0:2 * HALF].rearrange("p (a c) -> p a c", a=2)
        nrm = xh[:, 1, 0:9 * HC * TT * HN].rearrange("p (a b c e) -> p a b c e", a=3, b=3, c=HC)
        rot = scratch("rot", [P, 2, NH, ROPE // 2], F, 81)
        o_n = nc.alloc_sbuf_tensor_at("o_n", [P, TT, NH * VD], F, offset=base + 32 * KB)
        qk_t = scratch("qk_t", [QK, 2, 2, SEQ], F, 64)
        TRI = P * TT * (TT + 1) // 2
        tri = lambda t: slice(P * t * (t + 1) // 2, P * (t + 1) * (t + 2) // 2)
        prob = scratch("prob", [P, 2, TRI], F, 72)
        p_t = scratch("p_t", [P, TRI], F, 82)
        q_rot = scratch("q_rot", [P, 2, 2, TT, HN, ROPE // 2], F, 87)
        q_trig = scratch("q_trig", [P, 4, TT, ROPE // 2], F, 91)
        hg = scratch("hg", [P, 2 * ROPE], F, 94)
        gcol = scratch("gcol", [QK, 2], F, 96)
        mask = scratch("mask", [P, SEQ], F, 92)
        trig = scratch("trig", [P, 2, TT, ROPE // 2], F, 94.75)
        frq = scratch("frq", [P, ROPE // 2], F, 95.25)
        pos_i = scratch("pos_i", [P, TT], I32, 95.5)
        gconv = xh[:, 1, :].rearrange("p (a c) -> p a c", a=2)
        sqs = scratch("sqs", [P, SEQ], F, 78)

        ps = ctx.enter_context(nc.psum_tensor("ps", [P, 8, HALF], F))

        def sem(name):
            return ctx.enter_context(nc.semaphore(name))

        bank_full = [sem(f"bank_full{b}") for b in range(8)]
        bank_free = [sem(f"bank_free{b}") for b in range(8)]
        w_landed = [sem(f"w_landed{b}") for b in range(RING)]
        hi_made = sem("hi_made")
        lo_made = sem("lo_made")
        w_used = sem("w_used")
        ev_ready = sem("ev_ready")
        hi_ready = sem("hi_ready")
        lo_ready = sem("lo_ready")
        xh_ready = sem("xh_ready")
        ln_dev = sem("ln_dev")
        sq_ready = sem("sq_ready")
        dve_step = sem("dve_step")
        act_step = sem("act_step")
        var_ready = sem("var_ready")
        ln_ready = sem("ln_ready")
        rope_ready = sem("rope_ready")
        pool_ready = sem("pool_ready")
        decayed = sem("decayed")
        ret_dev = sem("ret_dev")
        ret_ready = sem("ret_ready")
        tab_dve = sem("tab_dve")
        tab_act = sem("tab_act")
        tables_ready = sem("tables_ready")
        gate_pre = sem("gate_pre")
        gate_conv = sem("gate_conv")
        gate_act = sem("gate_act")
        u_even = sem("u_even")
        zc_ready = sem("zc_ready")
        sig_ready = sem("sig_ready")
        ckv_ready = sem("ckv_ready")
        cq_ready = sem("cq_ready")
        lat_in = sem("lat_in")
        lat_dev = sem("lat_dev")
        sq_made = sem("sq_made")
        sum_made = sem("sum_made")
        k_copied = sem("k_copied")
        dev_made = sem("dev_made")
        trig_ready = sem("trig_ready")
        q_roped = sem("q_roped")
        qk_rows = sem("qk_rows")
        pool_step = sem("pool_step")
        max_ready = sem("max_ready")
        prob_ready = sem("prob_ready")
        x_in = [sem(f"x_in{t}") for t in range(TT)]
        id_in = sem("id_in")
        c_in = sem("c_in")
        gain_in = sem("gain_in")
        turn_in = sem("turn_in")
        p_in = sem("p_in")
        ln_in = [sem("ln1_in"), sem("ln2_in")]
        m_in = sem("m_in")
        st_out = sem("st_out")
        e_out = sem("e_out")
        k_out = sem("k_out")
        stage_w = sem("stage_w")
        e_w = sem("e_w")
        k_w = sem("k_w")
        rec_in = [sem(f"rec_in{i}") for i in range(3)]
        o_out = sem("o_out")

        block = ctx.enter_context(nc.Block())

        out_batch = {3: 0}
        up_batch = {0: 1, 2: 2, 4: 3, 6: 4, 8: 7, 10: 8, 12: 9, 15: 12, 17: 13, 19: 14}
        down_batch = {(0, 0): 5, (0, 1): 6, (1, 0): 10, (1, 1): 11, (2, 0): 15}
        up_phases = {3: 1}
        down_phases = {(0, 1): 2, (1, 0): 3}
        bank_no, freed, free_count = {}, [], [0] * 8
        chunks_at = {}
        chunk_src, chunk_done = [], []

        w_in0, w_out0 = w_in[0], w_out[0]

        def rows_of(w, k0, kn, c0, cn):
            return w[k0 * P:(k0 + kn) * P, c0:c0 + cn].rearrange("(k p) c -> p k c", p=P)

        def pool_out(h):
            return xh[:, h // 2, (h % 2) * HALF:(h % 2) * HALF + HALF]

        @block.tensor
        def _(pe):
            n_split = [0]
            n_ev = [0]

            def split_bank(name, through_ev=False):
                n_split[0] += 1
                n_ev[0] += through_ev
                return open_bank(name, freed_by=(ev_ready, n_ev[0]) if through_ev else (lo_ready, n_split[0]))

            def open_bank(name, freed_by=None):
                i = len(bank_no)
                bank_no[name] = i
                if i >= 8:
                    pe.wait_ge(*freed[i - 8])
                if freed_by is None:
                    free_count[i % 8] += 1
                    freed_by = (bank_free[i % 8], free_count[i % 8])
                freed.append(freed_by)
                return ps[:, i % 8, :]

            def close_bank(name, ins):
                i = bank_no[name]
                ins.then_inc(bank_full[i % 8], 1)
                chunks_at[name] = len(chunk_src)
                return bank_full[i % 8], i // 8 + 1

            def take_chunk(src, kn, cn, gain=None):
                n = len(chunk_src)
                chunk_src.append((src, kn, cn, gain))
                pe.wait_ge(hi_made, n + 1)
                pe.wait_ge(lo_made, n + 1)
                hi = w_hi[:, n % RING, 0:kn * cn].rearrange("p (k c) -> p k c", k=kn)
                lo = w_lo[:, n % RING, 0:kn * cn].rearrange("p (k c) -> p k c", k=kn)
                return hi, lo

            def chunk_over(ins):
                ins.then_inc(w_used, 1)
                n_plain[0] += 1
                chunk_done.append((w_used, n_plain[0]))

            n_plain = [0]

            def three(bank, wh, wl, xh_, xl_, first, last):
                pe.matmul(bank, wh, xh_, start=first, stop=False)
                pe.matmul(bank, wh, xl_, start=False, stop=False)
                return pe.matmul(bank, wl, xh_, start=False, stop=last)

            def rows_product(stage, w, ah, al, nk, c0, cn, per, row0=0, wait_k=None, wait_t=None, between=None,
                             gain=None, first_k=0):
                stage = stage if isinstance(stage, tuple) else (stage,)
                banks = [open_bank((*stage, t)) for t in range(TT)]
                starts = list(range(first_k, nk, per)) + list(range(0, first_k, per))
                for n, k in enumerate(starts):
                    kn = min(per, nk - k)
                    wh, wl = take_chunk(rows_of(w, row0 + k, kn, c0, cn), kn, cn,
                                        None if gain is None else gains[:, gain, k:k + kn])
                    for t in range(TT):
                        if wait_t is not None:
                            pe.wait_ge(lo_ready, wait_t(t, k + kn - 1))
                        for kk in range(kn):
                            if wait_k is not None and t == 0:
                                pe.wait_ge(lo_ready, wait_k(k + kk))
                            s = slice(t * P, t * P + P)
                            o = banks[t][:, 0:cn]
                            end = n == len(starts) - 1 and kk == kn - 1
                            pe.matmul(o, ah[:, k + kk, s], wh[:, kk, :], start=(n == 0 and kk == 0), stop=False)
                            pe.matmul(o, ah[:, k + kk, s], wl[:, kk, :], start=False, stop=False)
                            m = pe.matmul(o, al[:, k + kk, s], wh[:, kk, :], start=False, stop=end)
                            if end:
                                over = close_bank((*stage, t), m)
                    if n < len(starts) - 1:
                        chunk_over(m)
                    else:
                        chunk_done.append(over)
                    if between:
                        between(n + 1)

            def turned_tiles():
                before = n_split[0] - 2 * TT
                return lambda t, k: before + 2 * t + k // 4 + 1

            def cols_product(stage, w, c0, freed_by=None):
                b = open_bank(stage, freed_by=freed_by)
                wh, wl = take_chunk(rows_of(w, 0, KT, c0, P), KT, P)
                for k in range(KT):
                    m = three(b, wh[:, k, :], wl[:, k, :], a_hi[:, k, :], a_lo[:, k, :], k == 0, k == KT - 1)
                chunk_done.append(close_bank(stage, m))

            def turn_rows(stage, src, nk, ready=None, through_ev=False):
                for t in range(TT):
                    if ready:
                        ready(t)
                    k = 0
                    while k < nk:
                        kn = min(4, nk - k)
                        b = split_bank((stage, t, k // 4), through_ev)
                        for q in range(kn):
                            m = pe.transpose(b[:, q * P:q * P + P], src(t, k + q), ident[:, :])
                        close_bank((stage, t, k // 4), m)
                        k += kn

            def xh_turn(stage):
                def ready(t):
                    n_xh[0] += 1
                    pe.wait_ge(xh_ready, n_xh[0])
                turn_rows(stage, lambda t, k: xh[:, t % 2, k * P:k * P + P], KT, ready)

            n_xh = [0]

            def ffn(stage, wup, wdown, swap, extra=None):
                gate0, val0 = swap
                for g, (f0, f1) in enumerate(GROUPS):
                    base_split = n_split[0]
                    for f in range(f0, f1):
                        n_split[0] += 1
                        n_ev[0] += 1
                        cols_product((stage, "gate", f), wup, gate0 + f * P, freed_by=(ev_ready, n_ev[0]))
                        cols_product((stage, "val", f), wup, val0 + f * P, freed_by=(ev_ready, n_ev[0]))
                        if extra and f - 1 in up_batch:
                            extra(up_batch[f - 1])
                    for half in range(2):
                        b_ = down_batch.get((g, half)) if extra else None
                        between = (lambda k, b_=b_: extra(b_) if b_ is not None and k == 3 else None)
                        rows_product((stage, "down", g, half), wdown, h_hi, h_lo, f1 - f0, half * HALF, HALF, 2,
                                     row0=f0, wait_k=lambda k: base_split + k + 1, between=between)

            pe.wait_ge(id_in, 16)
            def turn_parameters():
                pe.wait_ge(turn_in, 16 * N_TURNED)
                b = open_bank("lam")
                for i in range(2):
                    m = pe.transpose(b[:, i * G:i * G + G], lam_nat[:, i, :, :].rearrange("g a n -> g (a n)"),
                                     ident[0:G, 0:G])
                close_bank("lam", m)
                for i in range(2):
                    for h in range(2):
                        b = open_bank(("c", i, h))
                        for q in range(4):
                            m = pe.transpose(b[:, q * P:q * P + P],
                                             c_nat[:, i, 4 * h + q, :, :].rearrange("p a n -> p (a n)"), ident[:, :])
                        close_bank(("c", i, h), m)

            turn_rows("x", lambda t, k: x_rows[:, t, k * P:k * P + P], KT, ready=lambda t: pe.wait_ge(x_in[t], 16))
            by_tile = turned_tiles()
            for i, nm in enumerate("qkvg"):
                if nm == "v":
                    turn_parameters()
                rows_product(nm, w_in0, a_hi, a_lo, KT, i * HALF, HALF, 2, wait_t=by_tile if i == 0 else None)
            pe.wait_ge(c_in, 16 * N_CONST)
            pe.wait_ge(rope_ready, TT)
            for h in range(RH):
                for nm, src in (("q", q_r), ("k", k_r)):
                    b = open_bank((nm, "t", h))
                    for t in range(TT):
                        m = pe.transpose(b[:, t * P:t * P + P], src[:, t, h, :], ident[:, :])
                    close_bank((nm, "t", h), m)
            for h in range(RH + 1):
                if h < RH:
                    cols_product(("p", h), w_in0, 4 * HALF + h * P)
                    if h == 0:
                        for hh in range(RH):
                            pe.wait_ge(*freed[bank_no[("q", "t", hh)]])
                            pe.wait_ge(*freed[bank_no[("k", "t", hh)]])
                        pe.wait_ge(*freed[bank_no[("v", TT - 1)]])
                    for j in range(TT):
                        b = open_bank(("s", h, j), freed_by=(decayed, TT * h + j + 1))
                        m = pe.matmul(b[:, 0:SEQ - j * P], k_t[:, h, j * P:j * P + P], q_t[:, h, j * P:SEQ],
                                      start=True, stop=True)
                        close_bank(("s", h, j), m)
                else:
                    pe.wait_ge(pool_ready, RH + 1)
                    for g in range(RH):
                        b = split_bank(("pool", g))
                        m = pe.matmul(b, wpool[:, g, :], pool_out(g), start=True, stop=True)
                        close_bank(("pool", g), m)
                if h:
                    g = h - 1
                    pe.wait_ge(decayed, TT * (g + 1))
                    b = open_bank(("ret", g))
                    for t in range(TT):
                        for j in range(t + 1):
                            off = j * SEQ - P * (j * (j - 1) // 2)
                            m = pe.matmul(b[:, t * P:t * P + P],
                                          s_t[g % 2][:, off + (t - j) * P:off + (t - j) * P + P],
                                          v_r[:, j, g, :], start=(j == 0), stop=(j == t))
                    close_bank(("ret", g), m)
            def prepare(f):
                pe.wait_ge(tables_ready, f + 1)
                b = open_bank(("s5w", f))
                for g in range(GB):
                    m = pe.transpose(b[:, g * P:g * P + P], h_b[:, g, :, :].rearrange("p s k -> p (s k)"), ident[:, :])
                close_bank(("s5w", f), m)
                b = open_bank(("s5k", f))
                for g in range(GB):
                    m = pe.matmul(b[0:GK, g * P:g * P + P], h_b[:, g, T - 1, :],
                                  stage[:, P_O + g * 144:P_O + g * 144 + P], start=True, stop=True)
                close_bank(("s5k", f), m)

            pool_split = n_split[0]

            def turn_retention():
                for g in range(RH):
                    pe.wait_ge(ret_ready, g + 1)
                    b = split_bank(("ret_t", g))
                    for t in range(TT):
                        m = pe.transpose(b[:, t * P:t * P + P], v_r[:, t, g, :], ident[:, :])
                    close_bank(("ret_t", g), m)

            rows_product(("w_out", 0), w_out0, a_hi, a_lo, KT, 0, HALF, 2, first_k=RH,
                         wait_k=lambda k: pool_split + k + 1 - (2 * RH if k >= RH else 0),
                         between=lambda n: turn_retention() if n == 2 else None)
            rows_product(("w_out", 1), w_out0, a_hi, a_lo, KT, HALF, HALF, 2,
                         between=lambda n: prepare(out_batch[n]) if n in out_batch else None)

            def ready_x(t):
                n_xh[0] += 1
                pe.wait_ge(xh_ready, n_xh[0])
            turn_rows("ln1", lambda t, k: x_rows[:, t, k * P:k * P + P], KT, ready=ready_x)
            pe.wait_ge(lo_ready, n_split[0])

            ffn("f1", w_up[0], w_down[0], (FF, 0), prepare)

            xh_turn("mix0")
            pe.wait_ge(lo_ready, n_split[0])
            for half in range(2):
                rows_product(("u", half), ssm_w_in_2[0], a_hi, a_lo, KT, half * HALF, HALF, 2)

            def s5_states(b_):
                if b_ == 0:
                    pe.wait_ge(*freed[bank_no[("u", 1, 3)]])
                b = open_bank(("ut", b_))
                for g in range(GB):
                    gg = b_ * GB + g
                    m = pe.transpose(b[:, g * NC:g * NC + NC], u_c[:, gg, :, :].rearrange("c s k -> c (s k)"),
                                     ident[0:NC, 0:NC])
                close_bank(("ut", b_), m)

            def s5_inc(b_):
                i = b_ % 2
                pe.wait_ge(rec_in[b_ % 3], 16 * (b_ // 3 + 1))
                pe.wait_ge(*freed[bank_no[("ut", b_)]])
                b = open_bank(("sv", b_))
                for sw in range(2):
                    for g in range(GB):
                        o = W_O + g * 192 + 64 * sw
                        m = pe.matmul(b[:, sw * 256 + g * NC:sw * 256 + g * NC + NC], rec[b_ % 3][:, o:o + P],
                                      u_t[:, b_ % 3, g * NC:g * NC + NC], start=True, stop=True)
                close_bank(("sv", b_), m)

            def s5_out(b_):
                i = b_ % 2
                pe.wait_ge(zc_ready, b_ + 1)
                b = open_bank(("y", b_))
                for g in range(GB):
                    o = b[0:NC, g * P:g * P + P]
                    pe.matmul(o, u_t[:, b_ % 3, g * NC:g * NC + NC], rec[b_ % 3][:, M_O + g * P:M_O + g * P + P],
                              start=True, stop=False)
                    pe.matmul(o, zc[:, i, 0, g, :], rec[b_ % 3][:, P_O + g * 144 + GK:P_O + g * 144 + 144],
                              start=False, stop=False)
                    m = pe.matmul(o, zc[:, i, 1, g, :], rec[b_ % 3][:, Q_O + g * P:Q_O + g * P + P],
                                  start=False, stop=True)
                close_bank(("y", b_), m)

            def s5_turn_back(k):
                pe.wait_ge(*freed[bank_no[("y", 2 * k + 1)]])
                b = split_bank(("zt", k))
                for s in range(T):
                    m = pe.transpose(b[:, s * NC:s * NC + NC], y_c[:, k % 2, s, :], ident[0:NC, 0:NC])
                close_bank(("zt", k), m)

            s5_states(0)
            for b_ in range(NB):
                if b_ + 1 < NB:
                    s5_states(b_ + 1)
                s5_inc(b_)
                if b_:
                    s5_out(b_ - 1)
                if b_ >= 3 and b_ % 2:
                    s5_turn_back((b_ - 3) // 2)
            s5_out(NB - 1)
            s5_turn_back(KT - 1)
            pe.wait_ge(lo_ready, n_split[0])
            for half in range(2):
                rows_product(("glu_g", half), ssm_w_glu_2[0], a_hi, a_lo, KT, D + half * HALF, HALF, 2)
                rows_product(("glu_v", half), ssm_w_glu_2[0], a_hi, a_lo, KT, half * HALF, HALF, 2)
            xh_turn("ffn0")
            pe.wait_ge(lo_ready, n_split[0])
            ffn("f2", ffn_w_gate_up_2[0], ffn_w_down_2[0], (0, FF))

            xh_turn("mla")
            by_tile = turned_tiles()
            rows_product("kv_a", mla_w_kv_a_2, a_hi, a_lo, KT, 0, KVR + ROPE, 2, gain=0, wait_t=by_tile)
            rows_product("q_a", mla_w_q_a_2[0], a_hi, a_lo, KT, 0, QR, 2, gain=1)

            turn_rows("ckv_t", lambda t, k: ckv[:, t, k * P:k * P + P], KVR // P,
                      ready=lambda t: pe.wait_ge(ckv_ready, t + 1), through_ev=True)
            kv_split = n_split[0] - TT
            turn_rows("cq_t", lambda t, k: cq[:, t, k * P:k * P + P], QR // P,
                      ready=lambda t: pe.wait_ge(cq_ready, t + 1), through_ev=True)
            for c in range(HC):
                rows_product(("kv_b", c), mla_w_kv_b_2, a_hi, a_lo, KVR // P, c * HALF, HALF, 2,
                             wait_t=(lambda t, k: kv_split + t + 1) if c == 0 else None)
            pe.wait_ge(lo_ready, n_split[0])
            for c in range(HC):
                rows_product(("q_b", c), mla_w_q_b_2[0], a_hi[:, 2:5, :], a_lo[:, 2:5, :], QR // P,
                             c * HN * QK, HN * QK, 2)

            def head_turn(h):
                pe.wait_ge(qk_rows, HC + h // HN + 1)
                for i, src in enumerate((q_n, k_n)):
                    b = open_bank(("ht", i, h))
                    for t in range(TT):
                        m = pe.transpose(b[0:QK, t * P:t * P + P], src[:, t, h, :], ident[:, :])
                    close_bank(("ht", i, h), m)

            def head_scores(h, t):
                if t == 0:
                    pe.wait_ge(*freed[bank_no[("ht", 0, h)]])
                    pe.wait_ge(*freed[bank_no[("ht", 1, h)]])
                b = open_bank(("sc", h, t), freed_by=(prob_ready, h * TT + t + 1))
                m = pe.matmul(b[:, 0:(t + 1) * P], qk_t[:, h % 2, 0, t * P:t * P + P],
                              qk_t[:, h % 2, 1, 0:(t + 1) * P], start=True, stop=True)
                close_bank(("sc", h, t), m)

            def head_probs(h, t):
                pe.wait_ge(prob_ready, h * TT + t + 1)
                b = open_bank(("pt", h, t))
                for j in range(t + 1):
                    o = P * t * (t + 1) // 2 + j * P
                    m = pe.transpose(b[:, j * P:j * P + P], prob[:, h % 2, o:o + P], ident[:, :])
                close_bank(("pt", h, t), m)

            def head_out(h):
                b = open_bank(("o", h))
                for t in range(TT):
                    pe.wait_ge(*freed[bank_no[("pt", h, t)]])
                    for j in range(t + 1):
                        o = P * t * (t + 1) // 2 + j * P
                        m = pe.matmul(b[:, t * VD:t * VD + VD], p_t[:, o:o + P], v_n[:, j, h, :],
                                      start=(j == 0), stop=(j == t))
                close_bank(("o", h), m)

            head_turn(0)
            head_turn(1)
            for t in range(TT):
                head_scores(0, t)
            for h in range(NH):
                for t in range(TT):
                    if h + 1 < NH:
                        head_scores(h + 1, t)
                    head_probs(h, t)
                if h + 2 < NH:
                    head_turn(h + 2)
                head_out(h)
            pe.wait_ge(*freed[bank_no[("o", NH - 1)]])
            turn_rows("o_t", lambda t, k: o_n[:, t, k * P:k * P + P], KT)
            by_tile = turned_tiles()
            for half in range(2):
                rows_product(("w_o", half), mla_w_o_2[0], h_hi, h_lo, KT, half * HALF, HALF, 2,
                             wait_t=by_tile if half == 0 else None)
            xh_turn("ffn1")
            pe.wait_ge(lo_ready, n_split[0])
            ffn("f3", ffn_w_gate_up_2[1], ffn_w_down_2[1], (0, FF))

        def full(eng, name):
            i = bank_no[name]
            eng.wait_ge(bank_full[i % 8], i // 8 + 1)
            return ps[:, i % 8, :]

        def release(name, ins):
            sem_, value = freed[bank_no[name]]
            assert sem_ is bank_free[bank_no[name] % 8]
            ins.then_inc(sem_, 1)
            return sem_, value

        def closed(name):
            i = bank_no[name]
            return bank_full[i % 8], i // 8 + 1

        def tile_split(hi, lo, k0, kn, t):
            s = slice(t * P, t * P + P)
            return (lambda e: e[:, 0:kn * P].rearrange("p (k c) -> p k c", k=kn),
                    hi[:, k0:k0 + kn, s], lo[:, k0:k0 + kn, s])

        def tile_split_s5(k0, t):
            c = slice(t * P // T, (t + 1) * P // T)
            dst = [a[:, k0:k0 + 4, :].rearrange("p k (s c) -> p k s c", s=T)[:, :, :, c] for a in (a_hi, a_lo)]
            return dst

        def ev_s5(e):
            return e.rearrange("p (k c s) -> p k s c", k=4, s=T)

        def turned_back(k):
            return (lambda e: e.rearrange("p (s c) -> p s c", s=T),
                    *[a[:, k, :].rearrange("p (c s) -> p s c", s=T) for a in (a_hi, a_lo)])

        def row_split(hi, lo, k):
            return lambda e: e, hi[:, k, :], lo[:, k, :]

        def rope_chunk(eng, c, r, step):
            x1, x2 = (q_n[:, :, HN * c:HN * c + HN, o:o + ROPE // 2] for o in (NOPE, NOPE + ROPE // 2))
            tab = [q_trig[:, i, :, :].unsqueeze(2).to_broadcast([P, TT, HN, ROPE // 2]) for i in range(4)]
            step(eng.tensor_tensor(r[:, 0, :, :, :], x2, tab[1], ALU.mult))
            step(eng.tensor_tensor(r[:, 1, :, :, :], x1, tab[2], ALU.mult))
            step(eng.tensor_tensor(x1, x1, tab[0], ALU.mult))
            step(eng.tensor_tensor(x2, x2, tab[3], ALU.mult))
            step(eng.tensor_tensor(x1, x1, r[:, 0, :, :, :], ALU.subtract))
            return eng.tensor_tensor(x2, x2, r[:, 1, :, :, :], ALU.add)

        @block.gpsimd
        def _(pool):
            steps = [0]

            def step(ins):
                ins.then_inc(pool_step, 1)
                steps[0] += 1
                pool.wait_ge(pool_step, steps[0])

            def rope_queries(c):
                if c == 0:
                    pool.wait_ge(trig_ready, 1)
                for t in range(TT):
                    pool.wait_ge(*freed[bank_no[("q_b", c, t)]])
                rope_chunk(pool, c, q_rot[:, 0, :, :, :, :], step).then_inc(q_roped, 1)

            for n, (_, kn, cn, _) in enumerate(chunk_src):
                w = kn * cn
                pool.wait_ge(hi_made, n + 1)
                if n >= RING:
                    pool.wait_ge(*chunk_done[n - RING])
                pool.tensor_tensor(w_lo[:, n % RING, 0:w], w_raw[:, n % RING, 0:w],
                                   w_hi[:, n % RING, 0:w].bitcast(F), ALU.subtract).then_inc(lo_made, 1)
                for c in range(0, HC, 2):
                    if n == chunks_at[("q_b", c, 0)] + 1:
                        rope_queries(c)

        @block.sync
        def _(sp):
            for t in range(TT):
                sp.dma_start(x_rows[:, t, :], x[0, t * P:t * P + P, :]).then_inc(x_in[t], 16)

            def store_batch(f):
                sp.wait_ge(stage_w, f + 1)
                sp.dma_start(rec_dram[f, :, 0:M_O], stage[:, :]).then_inc(st_out, 16)
                sp.wait_ge(k_w, f + 1)
                for s in range(T):
                    o = KPAD - GK * s
                    sp.dma_start(rec_dram[f, GK * s:GK * s + GK, M_O:C_O].rearrange("p (g c) -> p g c", g=GB),
                                 k_s[:, :, o:o + P]).then_inc(k_out, 16)
                if f % (EB // GB) == 0:
                    sp.wait_ge(e_w, f * GB // EB + 1)
                    for i in range(EB // GB):
                        sp.dma_start(rec_dram[f + i, :, C_O:REC].rearrange("p (a g c) -> p a g c", a=2, g=GB),
                                     e_t[:, :, GB * i:GB * i + GB, :]).then_inc(e_out, 16)

            for n, (src, kn, cn, _) in enumerate(chunk_src):
                if n >= RING:
                    sp.wait_ge(hi_made, n - RING + 1)
                    sp.wait_ge(lo_made, n - RING + 1)
                sp.dma_start(w_raw[:, n % RING, 0:kn * cn].rearrange("p (k c) -> p k c", k=kn), src)\
                  .then_inc(w_landed[n % RING], 16)
                for f in range(NB):
                    if chunks_at[("s5k", f)] + RING == n:
                        store_batch(f)
            sp.wait_ge(st_out, 16 * NB)
            sp.wait_ge(k_out, 16 * NB * T)
            sp.wait_ge(e_out, 16 * NB)
            for half in range(2):
                c = slice(half * HALF, half * HALF + HALF)
                for t in range(TT):
                    sp.wait_ge(*freed[bank_no[("f3", "down", len(GROUPS) - 1, half, t)]])
                    sp.dma_start(out[0, t * P:t * P + P, c], x_rows[:, t, c]).then_inc(o_out, 16)
            sp.wait_ge(o_out, 16 * 2 * TT)

        @block.scalar
        def _(act):
            steps, evs = [0], [0]

            def step(ins):
                ins.then_inc(act_step, 1)
                steps[0] += 1
                act.wait_ge(act_step, steps[0])

            made = [0]

            def ahead(count):
                while made[0] < min(count + RING, len(chunk_src)):
                    n = made[0]
                    _, kn, cn, gain = chunk_src[n]
                    w = kn * cn
                    act.wait_ge(w_landed[n % RING], 16 * (n // RING + 1))
                    if n >= RING:
                        act.wait_ge(*chunk_done[n - RING])
                    if gain is not None:
                        for k in range(kn):
                            r = w_raw[:, n % RING, k * cn:k * cn + cn]
                            ins = act.activation(r, r, ACT.Copy, scale=gain[:, k:k + 1])
                            if k < kn - 1:
                                ins.then_inc(act_step, 1)
                                steps[0] += 1
                        step(ins)
                    act.activation(w_hi[:, n % RING, 0:w], w_raw[:, n % RING, 0:w], ACT.Copy).then_inc(hi_made, 1)
                    made[0] += 1

            def at(name):
                ahead(chunks_at[name])
                return full(act, name)

            def split(name, view, hi, lo, scale=1.0):
                act.activation(hi, view(at(name)), ACT.Copy, scale=scale).then_inc(hi_ready, 1)

            def split_ev(name, view, hi, lo):
                ahead(chunks_at[name])
                i = evs[0]
                act.wait_ge(ev_ready, i + 1)
                act.activation(hi, view(ev[:, i % 2, :]), ACT.Copy).then_inc(hi_ready, 1)
                evs[0] += 1

            def split_rows(stage, nk=KT, hi=a_hi, lo=a_lo, off=0, splitter=split):
                for t in range(TT):
                    for k in range(0, nk, 4):
                        kn = min(4, nk - k)
                        splitter((stage, t, k // 4), *tile_split(hi, lo, off + k, kn, t))

            def deviation(stage, added, ready, t):
                ahead(chunks_at[added(t)])
                act.wait_ge(*ready(t))
                if t >= 2:
                    act.wait_ge(*closed((stage, t - 2, 1)))
                step(act.activation(xh[:, t % 2, :], x_rows[:, t, :], ACT.Square, accum_out=st[:, t:t + 1]))
                act.activation(st[:, 4 + t:5 + t], st[:, t:t + 1], ACT.Sqrt, scale=1.0 / D,
                               bias=eps_c[:, 1:2]).then_inc(sq_ready, 1)

            def split_tile(stage, t, dst):
                for k in range(2):
                    split((stage, t, k), *dst(t, k))

            def rms_and_split(stage, added, ready, dst):
                deviation(stage, added, ready, 0)
                for t in range(TT):
                    if t + 1 < TT:
                        deviation(stage, added, ready, t + 1)
                    split_tile(stage, t, dst)

            def load_gain(i, src):
                act.dma_start(gain_row[i][:, :], src.partition_broadcast(P)).then_inc(gain_in, 16)

            def bank_ready(added):
                return lambda t: freed[bank_no[added(t)]]

            def to_a(t, k):
                return tile_split(a_hi, a_lo, 4 * k, 4, t)

            def to_a_s5(t, k):
                return (ev_s5, *tile_split_s5(4 * k, t))

            def ffn(stage, swish_from_conv):
                for g, (f0, f1) in enumerate(GROUPS):
                    for f in range(f0, f1):
                        b = at((stage, "gate", f))
                        if swish_from_conv:
                            if f >= 1:
                                act.wait_ge(gate_conv, f)
                            step(act.activation(gbuf[:, 2:2 + SEQ], b, ACT.Copy))
                            act.activation(gconv[:, f % 2, :], b, ACT.Identity, scale=cw_c[:, 2, f:f + 1],
                                           bias=cb_c[:, f:f + 1]).then_inc(gate_pre, 1)
                            act.wait_ge(gate_conv, f + 1)
                            act.activation(gconv[:, f % 2, :], gconv[:, f % 2, :], ACT.Silu).then_inc(gate_act, 1)
                        else:
                            if f >= 2:
                                act.wait_ge(ev_ready, ev0[0] + f - 1)
                            act.activation(xh[:, f % 2, 0:SEQ], b, ACT.Silu).then_inc(gate_act, 1)
                        split_ev((stage, "val", f), *row_split(h_hi, h_lo, f - f0))

            def load_constants():
                act.dma_start(wpool[:, :, :], w_pool[0].rearrange("g c d -> c g d")).then_inc(c_in, 16)
                act.dma_start(decay[:, :, :], c_decay.rearrange("h j i -> j h i")).then_inc(c_in, 16)
                act.dma_start(rope_c[:, :, :, :], c_rope.rearrange("a (t p) d -> p a t d", p=P)).then_inc(c_in, 16)
                act.dma_start(ps_c[:, :], pool_scale[0].rearrange("(g p) -> p g", p=P)).then_inc(c_in, 16)
                act.dma_start(cnt16[:, :, :], c_count[:, 0:PADW].partition_broadcast(P)).then_inc(c_in, 16)
                cols = ((gains[:, 0, :], kv_in_norm_2), (gains[:, 1, :], mix_norm_2[1]), (kva_g[:, :], mla_kv_a_norm_2),
                        (qa_g[:, :], mla_q_a_norm_2[0]), (cb_c[:, :], conv_b[0]))
                for dst, src in cols:
                    act.dma_start(dst, src.rearrange("(k p) -> p k", p=P)).then_inc(c_in, 16)
                for j in range(3):
                    act.dma_start(cw_c[:, j, :], conv_w[0, j].rearrange("(k p) -> p k", p=P)).then_inc(c_in, 16)

            def load_turned():
                for i, src in enumerate((ssm_lambda_re_2, ssm_lambda_im_2)):
                    for a in range(2):
                        act.dma_start(lam_nat[:, i, a, :], src[0]).then_inc(turn_in, 16)
                for i, src in enumerate((ssm_c_re_2, ssm_c_im_2)):
                    v = src[0].rearrange("(h g) k n -> (g k) h n", g=8)
                    for a in range(2):
                        act.dma_start(c_nat[:, i, :, a, :], v).then_inc(turn_in, 16)

            def load_parameters():
                act.dma_start(lam[:, 2, :], ssm_log_step_2.to_broadcast([P, G])).then_inc(p_in, 16)
                for i, src in enumerate((ssm_b_re_2, ssm_b_im_2)):
                    act.dma_start(b_p[0:NS, i, :, :], src[0].rearrange("g n k -> n g k")).then_inc(p_in, 16)
                act.dma_start(d_t[:, :], ssm_d_2[0].rearrange("(g k) -> k g", g=G)).then_inc(p_in, 16)

            ev0 = [0]
            act.dma_start(ident[:, :], c_ident).then_inc(id_in, 16)
            split_rows("x")
            load_turned()
            load_constants()
            load_parameters()
            ahead(chunks_at["lam"])
            act.wait_ge(*closed(("c", 1, 1)))
            act.wait_ge(p_in, 16 * N_PARAM)
            act.activation(sm[:, 0, :], lam[:, 2, :], ACT.Exp).then_inc(tab_act, 1)
            act.wait_ge(tab_dve, 1)
            act.activation(sm[:, 3, :], sm[:, 1, :], ACT.Exp).then_inc(tab_act, 1)
            act.wait_ge(tab_dve, 2)
            act.activation(sm[:, 7, :], sm[:, 5, :], ACT.Sin).then_inc(tab_act, 1)
            act.activation(sm[:, 8, :], sm[:, 6, :], ACT.Sin).then_inc(tab_act, 1)
            for t in range(TT):
                release(("v", t), act.activation(v_r[:, t, :, :].rearrange("p h e -> p (h e)"), at(("v", t)), ACT.Copy))
            for t in range(TT):
                release(("g", t), act.activation(g_r[:, t, :, :].rearrange("p h e -> p (h e)"), at(("g", t)), ACT.Silu))
            for h in range(RH):
                act.wait_ge(*freed[bank_no[("q", "t", h)]])
                release(("k", "t", h), act.activation(k_t[:, h, :], at(("k", "t", h)), ACT.Copy))
            for h in range(RH + 1):
                if h < RH:
                    b = at(("p", h))
                    act.wait_ge(pool_ready, h + 1)
                    release(("p", h), act.activation(pool_p[:, PADW:], b, ACT.Copy))
                else:
                    for g in range(RH):
                        split(("pool", g), *row_split(a_hi, a_lo, RH + g), scale=ps_c[:, g:g + 1])
                if h:
                    g = h - 1
                    b = at(("ret", g))
                    for t in range(TT):
                        ins = act.activation(sqs[:, t * P:t * P + P], b[:, t * P:t * P + P], ACT.Square,
                                             accum_out=st[:, 4 * g + t:4 * g + t + 1])
                        if t < TT - 1:
                            ins.then_inc(act_step, 1)
                            steps[0] += 1
                    step(ins)
                    act.activation(st[:, 16 + 4 * g:20 + 4 * g], st[:, 4 * g:4 * g + 4], ACT.Sqrt, scale=1.0 / P,
                                   bias=eps_c[:, 1:2]).then_inc(ret_dev, 1)
            for i, src in enumerate((ln1_g, ln1_b)):
                act.dma_start(ln_g[0][:, i, :], src.to_broadcast([P, D])).then_inc(ln_in[0], 16)
            for g in range(RH):
                split(("ret_t", g), *row_split(a_hi, a_lo, g))

            def ln_deviation(added, i, t):
                ahead(chunks_at[added(t)])
                act.wait_ge(var_ready, i * TT + t + 1)
                act.activation(st[:, 36 + t:37 + t], st[:, 24 + 2 * t + 1:24 + 2 * t + 2], ACT.Sqrt,
                               bias=eps_c[:, 0:1]).then_inc(ln_dev, 1)

            ln_deviation(lambda t: ("w_out", 1, t), 0, 0)
            for t in range(TT):
                if t + 1 < TT:
                    ln_deviation(lambda t: ("w_out", 1, t), 0, t + 1)
                if t:
                    split_tile("ln1", t - 1, to_a)
            split_tile("ln1", TT - 1, to_a)
            gbuf = xh[:, 0, 0:SEQ + 2]
            ffn("f1", True)
            act.wait_ge(tables_ready, NB)
            for i, src in enumerate((ln2_g, ln2_b)):
                act.dma_start(ln_g[1][:, i, :], src.to_broadcast([P, D])).then_inc(ln_in[1], 16)
            load_gain(0, mix_norm_2[0])
            down = lambda t: ("f1", "down", 2, 1, t)

            whole = lambda t: (ln_ready, t + 1)
            ln_deviation(down, 1, 0)
            for t in range(TT):
                if t + 1 < TT:
                    ln_deviation(down, 1, t + 1)
                deviation("mix0", down, whole, t)
                if t:
                    split_tile("mix0", t - 1, to_a_s5)
            split_tile("mix0", TT - 1, to_a_s5)
            act.wait_ge(st_out, 16 * NB)
            act.wait_ge(k_out, 16 * NB * T)
            act.wait_ge(e_out, 16 * NB)

            def load_rec(b_):
                act.dma_start(rec[b_ % 3][:, :], rec_dram[b_]).then_inc(rec_in[b_ % 3], 16)

            load_rec(0)
            load_rec(1)
            load_rec(2)
            for dst, src in ((hg[:, 0:ROPE], mla_k_rope_norm_2), (hg[:, ROPE:], mla_q_rope_norm_2[0]),
                             (frq[:, :], c_freq)):
                act.dma_start(dst, src.partition_broadcast(P)).then_inc(m_in, 16)
            for i, src in enumerate((mla_q_nope_norm_2[0], mla_k_nope_norm_2)):
                act.dma_start(gcol[0:NOPE, i:i + 1], src.rearrange("(e a) -> e a", a=1)).then_inc(m_in, 16)
            act.dma_start(mask[:, :], c_mask).then_inc(m_in, 16)
            act.dma_start(pos_i[:, :], positions_2[0].rearrange("(t p) -> p t", p=P)).then_inc(m_in, 16)
            for half in range(2):
                for j in range(4):
                    b = at(("u", half, j))
                    act.wait_ge(u_even, 4 * half + j + 1)
                    release(("u", half, j), act.activation(u_c[:, 32 * half:32 * half + 32, 2 * j + 1, :],
                                                           b[NC:P, :].rearrange("c (g k) -> c g k", k=GK), ACT.Copy))

            def s5_turned(b_):
                if b_ >= 3:
                    act.wait_ge(*closed(("y", b_ - 3)))
                release(("ut", b_), act.activation(u_t[:, b_ % 3, :], at(("ut", b_))[:, 0:GB * NC], ACT.Copy))

            def s5_gelu(b_):
                y = at(("y", b_))[0:NC, :].rearrange("c (g t k) -> c t g k", g=GB, t=T)
                k, j = divmod(b_, 2)
                if j == 0 and k >= 2:
                    act.wait_ge(*closed(("zt", k - 2)))
                o = y_c[:, k % 2, :, 64 * j:64 * j + 64].rearrange("c t (g k) -> c t g k", g=GB)
                release(("y", b_), act.activation(o, y, ACT.Gelu_apprx_tanh))
                if b_ + 3 < NB:
                    load_rec(b_ + 3)

            s5_turned(0)
            for b_ in range(NB):
                if b_ + 1 < NB:
                    s5_turned(b_ + 1)
                if b_:
                    s5_gelu(b_ - 1)
                if b_ >= 3 and b_ % 2:
                    split(("zt", (b_ - 3) // 2), *turned_back((b_ - 3) // 2))
            s5_gelu(NB - 1)
            load_gain(1, ffn_norm_2[0])
            split(("zt", KT - 1), *turned_back(KT - 1))
            for half in range(2):
                for t in range(TT):
                    b = at(("glu_g", half, t))
                    if half:
                        act.wait_ge(*freed[bank_no[("glu_v", 0, t)]])
                    release(("glu_g", half, t), act.activation(sig[:, t, :], b, ACT.Sigmoid))
                ahead(chunks_at[("glu_v", half, TT - 1)])
            added = lambda t: ("glu_v", 1, t)
            rms_and_split("ffn0", added, bank_ready(added), to_a)
            ev0[0] = evs[0]
            ffn("f2", False)

            added = lambda t: ("f2", "down", 2, 1, t)
            rms_and_split("mla", added, bank_ready(added), to_a)
            act.wait_ge(tab_dve, 3)
            act.activation(trig[:, 1, :, :], rot[:, 0, 0:TT, :], ACT.Sin).then_inc(tab_act, 1)
            act.activation(trig[:, 0, :, :], rot[:, 1, 0:TT, :], ACT.Sin).then_inc(tab_act, 1)
            for t in range(TT):
                ahead(chunks_at[("kv_a", t)])
                act.wait_ge(lat_in, t + 1)
                step(act.activation(sq[:, 0, 0:KVR], ckv[:, t, 0:KVR], ACT.Square, accum_out=st[:, 2 * t:2 * t + 1]))
                step(act.activation(sq[:, 1, 0:ROPE], ckv[:, t, KVR:], ACT.Square,
                                    accum_out=st[:, 2 * t + 1:2 * t + 2]))
                step(act.activation(st[:, 8 + 2 * t:9 + 2 * t], st[:, 2 * t:2 * t + 1], ACT.Sqrt, scale=1.0 / KVR,
                                    bias=eps_c[:, 1:2]))
                act.activation(st[:, 9 + 2 * t:10 + 2 * t], st[:, 2 * t + 1:2 * t + 2], ACT.Sqrt, scale=1.0 / ROPE,
                               bias=eps_c[:, 1:2]).then_inc(lat_dev, 1)
            for t in range(TT):
                ahead(chunks_at[("q_a", t)])
                act.wait_ge(lat_in, TT + t + 1)
                step(act.activation(sq[:, 0, 0:QR], cq[:, t, :], ACT.Square, accum_out=st[:, 32 + t:33 + t]))
                act.activation(st[:, 40 + t:41 + t], st[:, 32 + t:33 + t], ACT.Sqrt, scale=1.0 / QR,
                               bias=eps_c[:, 1:2]).then_inc(lat_dev, 1)
            split_rows("ckv_t", KVR // P, splitter=split_ev)
            split_rows("cq_t", QR // P, off=2, splitter=split_ev)

            def row_deviations(n):
                act.wait_ge(sum_made, (n + 1) * TT)
                q, c = divmod(n, HC)
                if q:
                    step(act.activation(nrm[:, 1, 2, c, :], nrm[:, 0, 2, c, :], ACT.Sqrt, scale=1.0 / ROPE,
                                        bias=eps_c[:, 1:2]))
                act.activation(nrm[:, 1, q, c, :], nrm[:, 0, q, c, :], ACT.Sqrt, scale=1.0 / NOPE,
                               bias=eps_c[:, 1:2]).then_inc(dev_made, 1)

            for n in range(2 * HC):
                q, c = divmod(n, HC)
                for t in range(TT):
                    i = n * TT + t
                    name = (("kv_b", "q_b")[q], c, t)
                    b = at(name)
                    if i >= 2:
                        act.wait_ge(sum_made, i - 1)
                    rows = slice(HN * c, HN * c + HN)
                    if q:
                        b = b[:, 0:HN * QK].rearrange("p (h e) -> p h e", h=HN)
                        dst = q_n[:, t, rows, :]
                    else:
                        b = b.rearrange("p (h e) -> p h e", h=HN)[:, :, 0:NOPE]
                        dst = k_n[:, t, rows, 0:NOPE]
                    w = HN * (QK if q else NOPE)
                    act.activation(sq[:, i % 2, 0:w].rearrange("p (h e) -> p h e", h=HN), b, ACT.Square)\
                       .then_inc(sq_made, 1)
                    ins = act.activation(dst, b, ACT.Copy)
                    if q:
                        release(name, ins)
                    else:
                        ins.then_inc(k_copied, 1)
                    if t == 1 and n:
                        row_deviations(n - 1)
            def q_turned(h):
                release(("ht", 0, h), act.activation(qk_t[:, h % 2, 0, :], at(("ht", 0, h))[0:QK, :], ACT.Copy,
                                                     scale=gcol[:, 0:1]))

            def exponentials(h, t):
                act.wait_ge(max_ready, h * TT + t + 1)
                act.activation(prob[:, h % 2, tri(t)], full(act, ("sc", h, t))[:, 0:(t + 1) * P], ACT.Exp,
                               scale=-1.0, bias=st[:, 8 * (h % 2) + t:8 * (h % 2) + t + 1],
                               accum_out=st[:, 16 + 8 * (h % 2) + t:17 + 8 * (h % 2) + t]).then_inc(prob_ready, 1)

            q_turned(0)
            q_turned(1)
            row_deviations(2 * HC - 1)
            for t in range(TT):
                exponentials(0, t)
            for h in range(NH):
                for t in range(TT):
                    if h + 1 < NH:
                        exponentials(h + 1, t)
                if h:
                    act.wait_ge(*closed(("o", h - 1)))
                b = full(act, ("pt", h, TT - 1))
                release(("pt", h, TT - 1), act.activation(p_t[:, tri(TT - 1)], b, ACT.Copy))
                if h + 2 < NH:
                    q_turned(h + 2)
            act.wait_ge(*closed(("o", NH - 1)))
            load_gain(1, ffn_norm_2[1])
            split_rows("o_t", hi=h_hi, lo=h_lo)
            added = lambda t: ("w_o", 1, t)
            rms_and_split("ffn1", added, bank_ready(added), to_a)
            ev0[0] = evs[0]
            ffn("f3", False)
            ahead(len(chunk_src))

        @block.vector
        def _(v):
            steps, splits, evs, ev_split = [0], [0], [0], []
            pending = []

            def step(ins):
                ins.then_inc(dve_step, 1)
                steps[0] += 1
                v.wait_ge(dve_step, steps[0])

            def go(ins):
                ins.then_inc(dve_step, 1)
                steps[0] += 1

            def settle():
                v.wait_ge(dve_step, steps[0])

            def finish_split():
                if pending:
                    i, n, view, hi, lo = pending.pop()
                    v.wait_ge(hi_ready, n + 1)
                    v.tensor_tensor(lo, view(ev[:, i % 2, :]), hi.bitcast(F), ALU.subtract).then_inc(lo_ready, 1)

            def split_ev(name, write, view, hi, lo):
                i = evs[0]
                b = full(v, name)
                if i >= 2:
                    v.wait_ge(lo_ready, ev_split[i - 2] + 1)
                write(b, ev[:, i % 2, :]).then_inc(ev_ready, 1)
                finish_split()
                pending.append((i, splits[0], view, hi, lo))
                ev_split.append(splits[0])
                evs[0] += 1
                splits[0] += 1

            def split(name, view, hi, lo, scale=None):
                n = splits[0]
                b = view(full(v, name))
                v.wait_ge(hi_ready, n + 1)
                if scale is None:
                    ins = v.tensor_tensor(lo, b, hi.bitcast(F), ALU.subtract)
                else:
                    ins = v.scalar_tensor_tensor(lo, b, scale, hi.bitcast(F), ALU.mult, ALU.subtract)
                ins.then_inc(lo_ready, 1)
                splits[0] += 1

            def scaled(gain, kn=4):
                def write(b, e):
                    r = lambda a: a[:, 0:kn * P].rearrange("p (k c) -> p k c", k=kn)
                    g = gain.unsqueeze(2).to_broadcast([P, kn, P])
                    return v.tensor_tensor(r(e), r(b), g, ALU.mult)
                return write

            def split_rows(stage, nk=KT, gain=None, hi=a_hi, lo=a_lo, off=0):
                for t in range(TT):
                    for k in range(0, nk, 4):
                        kn = min(4, nk - k)
                        dst = tile_split(hi, lo, off + k, kn, t)
                        if gain is None:
                            split((stage, t, k // 4), *dst)
                        else:
                            split_ev((stage, t, k // 4), scaled(gain[:, k:k + kn], kn), *dst)
                finish_split()

            def xh_rows(first, t, gain):
                v.wait_ge(sq_ready, first + t + 1)
                step(v.reciprocal(st[:, 8 + t:9 + t], st[:, 4 + t:5 + t]))
                if gain is None:
                    ins = v.tensor_scalar(xh[:, t % 2, :], x_rows[:, t, :], st[:, 8 + t:9 + t], None, ALU.mult)
                else:
                    ins = v.scalar_tensor_tensor(xh[:, t % 2, :], x_rows[:, t, :], st[:, 8 + t:9 + t], gain[:, :],
                                                 ALU.mult, ALU.mult)
                ins.then_inc(xh_ready, 1)

            def split_tile(stage, t, dst):
                for k in range(2):
                    split((stage, t, k), *dst(t, k))

            def rms_and_split(stage, first, dst, gain=None):
                xh_rows(first, 0, gain)
                for t in range(TT):
                    if t + 1 < TT:
                        xh_rows(first, t + 1, gain)
                    split_tile(stage, t, dst)

            def to_a(t, k):
                return tile_split(a_hi, a_lo, 4 * k, 4, t)

            def to_a_s5(t, k):
                return (ev_s5, *tile_split_s5(4 * k, t))

            def add_rows(name, half, scale=None):
                for t in range(TT):
                    b = full(v, (*name, t))
                    o = x_rows[:, t, half * HALF:half * HALF + HALF]
                    if scale is None:
                        ins = v.tensor_tensor(o, b, o, ALU.add)
                    else:
                        ins = v.scalar_tensor_tensor(o, o, scale, b, ALU.mult, ALU.add)
                    last[t] = release((*name, t), ins)

            last = [None] * TT

            def ln_stats(t):
                v.wait_ge(*last[t])
                o = 48 + 12 * (t % 2)
                for c in range(2):
                    go(v.bn_stats(st[:, o + 6 * c:o + 6 * c + 6], x_rows[:, t, c * HALF:c * HALF + HALF]))
                settle()
                v.bn_aggr(st[:, 24 + 2 * t:26 + 2 * t], st[:, o:o + 12]).then_inc(var_ready, 1)

            def ln_rows(t, i, sem_):
                v.wait_ge(ln_in[i], 32)
                v.wait_ge(ln_dev, i * TT + t + 1)
                v.wait_ge(var_ready, i * TT + t + 1)
                step(v.reciprocal(st[:, 40 + t:41 + t], st[:, 36 + t:37 + t]))
                o = x_rows[:, t, :]
                step(v.scalar_tensor_tensor(o, o, st[:, 24 + 2 * t:25 + 2 * t], ln_g[i][:, 0, :],
                                            ALU.subtract, ALU.mult))
                v.scalar_tensor_tensor(o, o, st[:, 40 + t:41 + t], ln_g[i][:, 1, :], ALU.mult, ALU.add)\
                 .then_inc(sem_, 1)

            def cmul(o_re, o_im, a_re, a_im, b_re, b_im, t1, t2):
                go(v.tensor_tensor(t1, a_re, b_re, ALU.mult))
                go(v.tensor_tensor(t2, a_im, b_im, ALU.mult))
                go(v.tensor_tensor(o_re, a_re, b_im, ALU.mult))
                go(v.tensor_tensor(o_im, a_im, b_re, ALU.mult))
                settle()
                go(v.tensor_tensor(o_im, o_im, o_re, ALU.add))
                settle()
                step(v.tensor_tensor(o_re, t1, t2, ALU.subtract))

            def reduced(ang, turns, out_):
                step(v.tensor_scalar(turns, ang, 1.0 / TWO_PI, ROUNDER, ALU.mult, ALU.add))
                step(v.tensor_scalar(turns, turns, ROUNDER, None, ALU.subtract))
                step(v.scalar_tensor_tensor(out_, turns, -PI2_A, ang, ALU.mult, ALU.add))
                step(v.scalar_tensor_tensor(out_, turns, -PI2_B, out_, ALU.mult, ALU.add))
                step(v.scalar_tensor_tensor(out_, turns, -PI2_C, out_, ALU.mult, ALU.add))
                step(v.tensor_scalar(out_, out_, PI_IN, -PI_IN, ALU.min, ALU.max))

            def quarter(out_, ang):
                step(v.scalar_tensor_tensor(out_, ang, -1.0, ang, ALU.mult, ALU.min))
                return v.tensor_scalar(out_, out_, TWO_PI / 4, None, ALU.add)

            def s5_tables():
                v.wait_ge(p_in, 16 * N_PARAM)
                r = release("lam", v.tensor_copy(lam[:, 0:2, :].rearrange("p a g -> p (a g)"), full(v, "lam")[:, 0:P]))
                v.wait_ge(*r)
                for i in range(2):
                    for h in range(2):
                        o = c_p[:, i, 32 * h:32 * h + 32, :].rearrange("p g k -> p (g k)")
                        b = full(v, ("c", i, h))
                        go(v.tensor_copy(o[0:NS], b[0:NS]))
                        r = release(("c", i, h), v.tensor_scalar(o[NS:P], b[NS:P], -1.0, None, ALU.mult))
                v.wait_ge(*r)
                for i in range(2):
                    go(v.tensor_copy(b_p[NS:P, i, :, :], b_p[0:NS, i, :, :]))
                settle()
                lr, li = lam[:, 0, :], lam[:, 1, :]
                s = lambda i: sm[:, i, :]
                v.wait_ge(tab_act, 1)
                step(v.tensor_tensor(s(1), lr, s(0), ALU.mult))
                v.tensor_tensor(s(2), li, s(0), ALU.mult).then_inc(tab_dve, 1)
                v.wait_ge(tab_dve, 1)
                reduced(s(2), s(4), s(5))
                quarter(s(6), s(5)).then_inc(tab_dve, 1)
                v.wait_ge(tab_act, 4)
                sn, cs, r = s(7), s(8), s(3)
                go(v.memset(pri[:, 0, 0, :], 1.0))
                go(v.memset(pri[:, 1, 0, :], 0.0))
                go(v.tensor_tensor(pri[:, 0, 1, :], r, cs, ALU.mult))
                go(v.tensor_tensor(pri[:, 1, 1, :], r, sn, ALU.mult))
                go(v.tensor_copy(s(9), cs))
                go(v.tensor_copy(s(10), sn))
                go(v.tensor_copy(s(11), r))
                settle()
                for _ in range(3):
                    cmul(s(12), s(13), s(9), s(10), s(9), s(10), s(14), s(15))
                    go(v.tensor_copy(s(9), s(12)))
                    go(v.tensor_copy(s(10), s(13)))
                    go(v.tensor_tensor(s(11), s(11), s(11), ALU.mult))
                    settle()
                step(v.tensor_copy(r8[:, :], s(11)))
                go(v.tensor_copy(turn[:, 0, 0, :], s(9)))
                go(v.tensor_copy(turn[:, 1, 0, :], s(10)))
                settle()
                for i in range(5):
                    a, b = turn[:, 0, i, :], turn[:, 1, i, :]
                    cmul(turn[:, 0, i + 1, :], turn[:, 1, i + 1, :], a, b, a, b, s(14), s(15))
                for lo_, n in ((1, 1), (1, 2), (1, 4)):
                    bc = lambda a: pri[:, a, n, :].unsqueeze(1).to_broadcast([P, n, G])
                    t1, t2 = (bt[:, a, 0:n * G].rearrange("p (k g) -> p k g", k=n) for a in range(2))
                    cmul(pri[:, 0, 1 + n:1 + 2 * n, :], pri[:, 1, 1 + n:1 + 2 * n, :],
                         pri[:, 0, 1:1 + n, :], pri[:, 1, 1:1 + n, :], bc(0), bc(1), t1, t2)
                ar, ai = pri[:, 0, 1, :], pri[:, 1, 1, :]
                go(v.tensor_scalar(s(9), ar, 1.0, None, ALU.subtract))
                go(v.tensor_tensor(s(10), lr, lr, ALU.mult))
                go(v.tensor_tensor(s(11), li, li, ALU.mult))
                settle()
                step(v.tensor_tensor(s(10), s(10), s(11), ALU.add))
                go(v.reciprocal(s(11), s(10)))
                go(v.tensor_tensor(s(12), s(9), lr, ALU.mult))
                go(v.tensor_tensor(s(13), ai, li, ALU.mult))
                go(v.tensor_tensor(s(14), ai, lr, ALU.mult))
                go(v.tensor_tensor(s(15), s(9), li, ALU.mult))
                settle()
                go(v.tensor_tensor(s(12), s(12), s(13), ALU.add))
                go(v.tensor_tensor(s(14), s(14), s(15), ALU.subtract))
                settle()
                go(v.tensor_tensor(s(12), s(12), s(11), ALU.mult))
                go(v.tensor_tensor(s(14), s(14), s(11), ALU.mult))
                settle()
                for q in range(2):
                    gs = slice(32 * q, 32 * q + 32)
                    br, bi = b_p[:, 0, gs, :], b_p[:, 1, gs, :]
                    fr, fi = (s(a)[:, gs].unsqueeze(2).to_broadcast([P, 32, GK]) for a in (12, 14))
                    t1, t2 = (bt[:, a, :].rearrange("p (g k) -> p g k", g=32) for a in range(2))
                    go(v.tensor_tensor(t1, bi, fi, ALU.mult))
                    go(v.tensor_tensor(t2, br, fi, ALU.mult))
                    settle()
                    go(v.tensor_tensor(br, br, fr, ALU.mult))
                    go(v.tensor_tensor(bi, bi, fr, ALU.mult))
                    settle()
                    go(v.tensor_tensor(br, br, t1, ALU.subtract))
                    go(v.tensor_tensor(bi, bi, t2, ALU.add))
                    settle()
                top, bot = slice(0, NS), slice(NS, P)
                for i, h, a, sign in ((0, top, 0, 1.0), (0, bot, 1, 1.0), (1, top, 1, -1.0), (1, bot, 0, 1.0)):
                    go(v.tensor_scalar(pw[h, i, :, :], pri[h, a, :, :], sign, None, ALU.mult))
                settle()

            go(v.memset(eps_c[:, 0:1], 1e-5))
            go(v.memset(eps_c[:, 1:2], 1e-6))
            settle()
            split_rows("x")
            v.wait_ge(c_in, 16 * N_CONST)
            for nm, dst in (("q", q_r), ("k", k_r)):
                for t in range(TT):
                    b = full(v, (nm, t)).rearrange("p (h e) -> p h e", h=RH)
                    c_ = rope_c[:, 0, t, :].unsqueeze(1).to_broadcast([P, RH, 64])
                    s_ = rope_c[:, 1, t, :].unsqueeze(1).to_broadcast([P, RH, 64])
                    lo_, hi_ = b[:, :, 0:64], b[:, :, 64:P]
                    r0, r1 = (rtmp[:, a, :].rearrange("p (h e) -> p h e", h=RH) for a in range(2))
                    go(v.tensor_tensor(dst[:, t, :, 0:64], lo_, c_, ALU.mult))
                    go(v.tensor_tensor(dst[:, t, :, 64:P], lo_, s_, ALU.mult))
                    go(v.tensor_tensor(r0, hi_, s_, ALU.mult))
                    settle()
                    w = release((nm, t), v.tensor_tensor(r1, hi_, c_, ALU.mult))
                    go(v.tensor_tensor(dst[:, t, :, 0:64], dst[:, t, :, 0:64], r0, ALU.subtract))
                    v.wait_ge(*w)
                    settle()
                    v.tensor_tensor(dst[:, t, :, 64:P], dst[:, t, :, 64:P], r1, ALU.add)\
                     .then_inc(rope_ready if nm == "k" else dve_step, 1)
                    if nm == "q":
                        steps[0] += 1
                        settle()
                    else:
                        v.wait_ge(rope_ready, t + 1)
            s5_tables()

            for h in range(RH):
                release(("q", "t", h), v.tensor_copy(q_t[:, h, :], full(v, ("q", "t", h))))
            for pad in (pool_a, pool_b):
                go(v.memset(pad[:, 0:PADW], 0.0))
            v.memset(pool_p[:, 0:PADW], 0.0).then_inc(pool_ready, 1)

            def pooled(h):
                v.wait_ge(*freed[bank_no[("p", h)]])
                settle()
                src, win = pool_p, 1
                for r in range(h + 1):
                    dst = (pool_a, pool_b)[r % 2]
                    step(v.tensor_tensor(dst[:, PADW:], src[:, PADW:], src[:, PADW - win:PADW - win + SEQ], ALU.add))
                    src, win = dst, 2 * win
                other = (pool_a, pool_b)[(h + 1) % 2]
                step(v.tensor_tensor(other[:, PADW:2 * PADW], src[:, PADW:2 * PADW], cnt16[:, h, :], ALU.mult))
                o = pool_out(h)
                go(v.scalar_tensor_tensor(o[:, PADW:], src[:, 2 * PADW:], 1.0 / win, pool_p[:, 2 * PADW:],
                                          ALU.mult, ALU.subtract))
                settle()
                v.tensor_tensor(o[:, 0:PADW], other[:, PADW:2 * PADW], pool_p[:, PADW:2 * PADW], ALU.subtract)\
                 .then_inc(pool_ready, 1)
                v.wait_ge(pool_ready, h + 2)

            for h in range(RH + 1):
                if h < RH:
                    pooled(h)
                    for j in range(TT):
                        n = SEQ - j * P
                        off = j * SEQ - P * (j * (j - 1) // 2)
                        v.tensor_tensor(s_t[h % 2][:, off:off + n], full(v, ("s", h, j))[:, 0:n],
                                        decay[:, h, 0:n], ALU.mult).then_inc(decayed, 1)
                else:
                    for g in range(RH):
                        split(("pool", g), *row_split(a_hi, a_lo, RH + g), scale=ps_c[:, g:g + 1])
                if h:
                    g = h - 1
                    b = full(v, ("ret", g)).rearrange("p (t e) -> p t e", t=TT)
                    vh = v_r[:, :, g, :]
                    v.wait_ge(ret_dev, h)
                    step(v.reciprocal(st[:, 32:36], st[:, 16 + 4 * g:20 + 4 * g]))
                    w = release(("ret", g), v.tensor_tensor(vh, b, st[:, 32:36].unsqueeze(2)
                                                            .to_broadcast([P, TT, P]), ALU.mult))
                    v.wait_ge(*w)
                    if g == 0:
                        v.wait_ge(*freed[bank_no[("g", TT - 1)]])
                    v.tensor_tensor(vh, vh, g_r[:, :, g, :], ALU.mult).then_inc(ret_ready, 1)
            for g in range(RH):
                split(("ret_t", g), *row_split(a_hi, a_lo, g))
            def s5_phases(e):
                gs = slice(e * EB, e * EB + EB)
                if e:
                    v.wait_ge(e_out, 16 * e * (EB // GB))
                go(v.memset(e_t[:, 0, :, 0:1], 1.0))
                go(v.memset(e_t[:, 1, :, 0:1], 0.0))
                settle()
                n = 1
                while n < NC:
                    k = n.bit_length() - 1
                    bc = lambda a: turn[:, a, k, gs].unsqueeze(2).to_broadcast([P, EB, n])
                    t1, t2 = (a[:, 0:EB * n].rearrange("p (g c) -> p g c", g=EB) for a in (tmp1, tmp2))
                    cmul(e_t[:, 0, :, n:2 * n], e_t[:, 1, :, n:2 * n], e_t[:, 0, :, 0:n], e_t[:, 1, :, 0:n],
                         bc(0), bc(1), t1, t2)
                    n *= 2
                v.tensor_scalar(e_t[NS:P, 1, :, :], e_t[NS:P, 1, :, :], -1.0, None, ALU.mult).then_inc(e_w, 1)
                v.wait_ge(e_w, e + 1)

            def s5_batch(f):
                gs = slice(f * GB, f * GB + GB)
                t1 = tmp1[:, 0:GB * T * GK].rearrange("p (g s k) -> p g s k", g=GB, s=T)
                if f:
                    v.wait_ge(*closed(("s5k", f - 1)))
                for a, o in ((0, h_b[:, :, :, :]), (1, t1)):
                    go(v.tensor_tensor(o, b_p[:, a, gs, :].unsqueeze(2).to_broadcast([P, GB, T, GK]),
                                       pw[:, a, T - 1::-1, gs].rearrange("p s g -> p g s").unsqueeze(3)
                                       .to_broadcast([P, GB, T, GK]), ALU.mult))
                settle()
                step(v.tensor_tensor(h_b[:, :, :, :].rearrange("p g s k -> p (g s k)"),
                                     h_b[:, :, :, :].rearrange("p g s k -> p (g s k)"), tmp1[:, 0:GB * T * GK],
                                     ALU.add))
                if f:
                    v.wait_ge(st_out, 16 * f)
                cp = stage[:, P_O:P_O + GB * 144].rearrange("p (g s k) -> p g s k", g=GB, s=T + 1)
                t2 = tmp2[:, :].rearrange("p (g s k) -> p g s k", g=GB, s=T + 1)
                for a, o in ((0, cp), (1, t2)):
                    go(v.tensor_tensor(o, c_p[:, a, gs, :].unsqueeze(2).to_broadcast([P, GB, T + 1, GK]),
                                       pw[:, a, :, gs].rearrange("p s g -> p g s").unsqueeze(3)
                                       .to_broadcast([P, GB, T + 1, GK]), ALU.mult))
                settle()
                o = stage[:, P_O:P_O + GB * 144]
                step(v.tensor_tensor(o, o, tmp2[:, :], ALU.add))
                q = stage[:, Q_O:Q_O + GB * P].rearrange("p (g c) -> p g c", g=GB)
                c1 = o.rearrange("p (g c) -> p g c", g=GB)[:, :, GK:]
                go(v.tensor_copy(q[0:NS], c1[NS:P]))
                v.tensor_copy(q[NS:P], c1[0:NS]).then_inc(tables_ready, 1)

            def s5_batch_out(f):
                b = full(v, ("s5w", f)).rearrange("p (g c) -> p g c", g=GB)
                w = stage[:, W_O:W_O + 768].rearrange("p (g c) -> p g c", g=GB)
                go(v.tensor_copy(w[:, :, 0:P], b))
                r = release(("s5w", f), v.tensor_copy(w[:, :, P:], b[:, :, 0:NS]))
                v.wait_ge(*r)
                v.wait_ge(tables_ready, f + 1)
                if f:
                    v.wait_ge(k_out, 16 * T * f)
                b = full(v, ("s5k", f))[0:GK, :].rearrange("p (g c) -> p g c", g=GB)
                r = release(("s5k", f), v.tensor_copy(k_s[:, :, KPAD:], b))
                v.wait_ge(*r)
                settle()
                for g in range(GB):
                    o = k_s[:, g, KPAD:KPAD + GK]
                    ins = v.scalar_tensor_tensor(o, ident[0:GK, 0:GK], d_t[:, f * GB + g:f * GB + g + 1], o,
                                                 ALU.mult, ALU.add)
                    if g < GB - 1:
                        go(ins)
                    else:
                        ins.then_inc(k_w, 1)
                settle()
                v.memset(st[:, 191:192], 0.0).then_inc(stage_w, 1)

            go(v.memset(k_s[:, :, 0:KPAD], 0.0))
            settle()
            add_rows(("w_out", 0), 0, ALPHA)
            s5_phases(0)
            s5_batch(0)
            s5_batch_out(0)
            add_rows(("w_out", 1), 1, ALPHA)
            ln_stats(0)
            for t in range(TT):
                if t + 1 < TT:
                    ln_stats(t + 1)
                ln_rows(t, 0, xh_ready)
                if t:
                    split_tile("ln1", t - 1, to_a)
            split_tile("ln1", TT - 1, to_a)

            def down_and_add(stage, g, scale=None):
                for half in range(2):
                    add_rows((stage, "down", g, half), half, scale if g == 0 else None)

            gbuf = xh[:, 0, 0:SEQ + 2]
            step(v.memset(gbuf[:, 0:2], 0.0))
            for g, (f0, f1) in enumerate(GROUPS):
                for f in range(f0, f1):
                    v.wait_ge(gate_pre, f + 1)
                    c_ = gconv[:, f % 2, :]
                    step(v.scalar_tensor_tensor(c_, gbuf[:, 1:1 + SEQ], cw_c[:, 1, f:f + 1], c_, ALU.mult, ALU.add))
                    v.scalar_tensor_tensor(c_, gbuf[:, 0:SEQ], cw_c[:, 0, f:f + 1], c_, ALU.mult, ALU.add)\
                     .then_inc(gate_conv, 1)
                    v.wait_ge(gate_act, f + 1)
                    split_ev(("f1", "val", f), lambda b, e: v.tensor_tensor(e, b, gconv[:, f % 2, :], ALU.mult),
                          *row_split(h_hi, h_lo, f - f0))
                    if f - 1 in up_batch:
                        s5_batch_out(up_batch[f - 1])
                    if f in up_phases:
                        s5_phases(up_phases[f])
                    if f in up_batch:
                        s5_batch(up_batch[f])
                finish_split()
                for half in range(2):
                    if (g, half) in down_phases:
                        s5_phases(down_phases[g, half])
                    if (g, half) in down_batch:
                        s5_batch(down_batch[g, half])
                        s5_batch_out(down_batch[g, half])
                    add_rows(("f1", "down", g, half), half, ALPHA if g == 0 else None)
            v.wait_ge(gain_in, 16)
            ln_stats(0)
            for t in range(TT + 2):
                if t + 1 < TT:
                    ln_stats(t + 1)
                if t < TT:
                    ln_rows(t, 1, ln_ready)
                if 1 <= t <= TT:
                    xh_rows(0, t - 1, gain_row[0])
                if t >= 2:
                    split_tile("mix0", t - 2, to_a_s5)
            go(v.memset(zc[:, :, :, :, 0:1], 0.0))
            settle()
            for half in range(2):
                for j in range(4):
                    v.tensor_copy(u_c[:, 32 * half:32 * half + 32, 2 * j, :],
                                  full(v, ("u", half, j))[0:NC, :].rearrange("c (g k) -> c g k", k=GK))\
                     .then_inc(u_even, 1)
            for b_ in range(NB):
                b = full(v, ("sv", b_))
                v.wait_ge(rec_in[b_ % 3], 16 * (b_ // 3 + 1))
                cs, sn = rec[b_ % 3][:, C_O:C_O + 256], rec[b_ % 3][:, S_O:S_O + 256]
                go(v.tensor_tensor(z1[:, :], b[:, 0:256], cs, ALU.mult))
                r = release(("sv", b_), v.tensor_tensor(z2[:, :], b[:, 256:512], sn, ALU.mult))
                settle()
                v.wait_ge(*r)
                step(v.tensor_tensor(z1[:, :], z1[:, :], z2[:, :], ALU.add))
                for g in range(GB):
                    gg = b_ * GB + g
                    s = slice(g * NC, g * NC + NC)
                    go(v.tensor_tensor_scan(z3[:, s], r8[:, gg:gg + 1].to_broadcast([P, NC]), z1[:, s], 0.0,
                                            ALU.mult, ALU.add))
                settle()
                if b_ >= 2:
                    v.wait_ge(*closed(("y", b_ - 2)))
                zv = z3[:, :].rearrange("p (g c) -> p g c", g=GB)[:, :, 0:NC - 1]
                cv = cs.rearrange("p (g c) -> p g c", g=GB)[:, :, 0:NC - 1]
                sv = sn.rearrange("p (g c) -> p g c", g=GB)[:, :, 0:NC - 1]
                step(v.tensor_tensor(zc[:, b_ % 2, 0, :, 1:], zv, cv, ALU.mult))
                v.tensor_tensor(zc[:, b_ % 2, 1, :, 1:], zv, sv, ALU.mult).then_inc(zc_ready, 1)
                v.wait_ge(zc_ready, b_ + 1)
                if b_ >= 3 and b_ % 2:
                    split(("zt", (b_ - 3) // 2), *turned_back((b_ - 3) // 2))
            split(("zt", KT - 1), *turned_back(KT - 1))
            for half in range(2):
                for t in range(TT):
                    b = full(v, ("glu_v", half, t))
                    v.wait_ge(*freed[bank_no[("glu_g", half, t)]])
                    o = x_rows[:, t, half * HALF:half * HALF + HALF]
                    step(v.tensor_tensor(ev[:, 0, :], b, sig[:, t, :], ALU.mult))
                    last[t] = release(("glu_v", half, t), v.tensor_tensor(o, o, ev[:, 0, :], ALU.add))
                    v.wait_ge(*last[t])

            def swiglu(stage):
                for g, (f0, f1) in enumerate(GROUPS):
                    for f in range(f0, f1):
                        n_gate[0] += 1
                        v.wait_ge(gate_act, n_gate[0])
                        split_ev((stage, "val", f), lambda b, e: v.tensor_tensor(e, b, xh[:, f % 2, 0:SEQ], ALU.mult),
                              *row_split(h_hi, h_lo, f - f0))
                    finish_split()
                    down_and_add(stage, g)

            n_gate = [FT]
            v.wait_ge(gain_in, 32)
            rms_and_split("ffn0", TT, to_a, gain_row[1])
            swiglu("f2")

            rms_and_split("mla", 2 * TT, to_a)
            v.wait_ge(m_in, 16 * 7)
            go(v.memset(gcol[NOPE:QK, :], 1.0))
            step(v.tensor_copy(st[:, 130:134], pos_i[:, :]))
            for t in range(TT):
                go(v.tensor_scalar(rot[:, 0, 4 + t, :], frq[:, :], st[:, 130 + t:131 + t], None, ALU.mult))
            settle()
            reduced(rot[:, 0, 4:8, :], rot[:, 1, 4:8, :], rot[:, 0, 0:4, :])
            quarter(rot[:, 1, 0:4, :], rot[:, 0, 0:4, :]).then_inc(tab_dve, 1)
            for t in range(TT):
                w = release(("kv_a", t), v.tensor_copy(ckv[:, t, :], full(v, ("kv_a", t))[:, 0:KVR + ROPE]))
                v.wait_ge(*w)
                v.memset(st[:, 190:191], 0.0).then_inc(lat_in, 1)
            for t in range(TT):
                v.wait_ge(lat_dev, t + 1)
                step(v.reciprocal(st[:, 16 + 2 * t:18 + 2 * t], st[:, 8 + 2 * t:10 + 2 * t]))
                c_ = ckv[:, t, 0:KVR]
                v.tensor_scalar(c_, c_, st[:, 16 + 2 * t:17 + 2 * t], None, ALU.mult).then_inc(ckv_ready, 1)
            for t in range(TT):
                w = release(("q_a", t), v.tensor_copy(cq[:, t, :], full(v, ("q_a", t))[:, 0:QR]))
                v.wait_ge(*w)
                v.memset(st[:, 190:191], 0.0).then_inc(lat_in, 1)
            for t in range(TT):
                v.wait_ge(lat_dev, TT + t + 1)
                step(v.reciprocal(st[:, 48 + t:49 + t], st[:, 40 + t:41 + t]))
                v.tensor_scalar(cq[:, t, :], cq[:, t, :], st[:, 48 + t:49 + t], None, ALU.mult).then_inc(cq_ready, 1)
            split_rows("ckv_t", KVR // P, gain=kva_g)
            split_rows("cq_t", QR // P, gain=qa_g, off=2)
            v.wait_ge(tab_act, 6)
            for i, (fn, half) in enumerate(((0, 0), (1, 1), (1, 0), (0, 1))):
                g = hg[:, ROPE + half * ROPE // 2:ROPE + (half + 1) * ROPE // 2].unsqueeze(1)\
                    .to_broadcast([P, TT, ROPE // 2])
                go(v.tensor_tensor(q_trig[:, i, :, :], trig[:, fn, :, :], g, ALU.mult))
            settle()
            v.memset(st[:, 189:190], 0.0).then_inc(trig_ready, 1)
            for t in range(TT):
                kr = ckv[:, t, KVR:]
                go(v.scalar_tensor_tensor(kr, kr, st[:, 17 + 2 * t:18 + 2 * t], hg[:, 0:ROPE], ALU.mult, ALU.mult))
            settle()
            k1, k2, t1, t2 = (rot[:, a, o:o + TT, :] for a in range(2) for o in (8, 12))
            cmul(k1, k2, ckv[:, :, KVR:KVR + ROPE // 2], ckv[:, :, KVR + ROPE // 2:],
                 trig[:, 0, :, :], trig[:, 1, :, :], t1, t2)
            for k_, o in ((k1, NOPE), (k2, NOPE + ROPE // 2)):
                go(v.tensor_copy(k_n[:, :, :, o:o + ROPE // 2],
                                 k_.unsqueeze(2).to_broadcast([P, TT, NH, ROPE // 2])))
            settle()

            def normalised(n):
                q, c = divmod(n, HC)
                v.wait_ge(dev_made, n + 1)
                rows = slice(HN * c, HN * c + HN)
                go(v.reciprocal(nrm[:, 2, q, c, :], nrm[:, 1, q, c, :]))
                if q:
                    go(v.reciprocal(nrm[:, 2, 2, c, :], nrm[:, 1, 2, c, :]))
                    for t in range(TT):
                        v.wait_ge(*freed[bank_no[("q_b", c, t)]])
                settle()
                inv = lambda a, e: nrm[:, 2, a, c, :].rearrange("p (t h) -> p t h", t=TT).unsqueeze(3)\
                    .to_broadcast([P, TT, HN, e])
                if q:
                    x_ = q_n[:, :, rows, 0:NOPE]
                    go(v.tensor_tensor(x_, x_, inv(1, NOPE), ALU.mult))
                    x_ = q_n[:, :, rows, NOPE:]
                    if c % 2:
                        go(rope_chunk(v, c, q_rot[:, 1, :, :, :, :], step))
                    else:
                        v.wait_ge(q_roped, c // 2 + 1)
                    settle()
                    v.tensor_tensor(x_, x_, inv(2, ROPE), ALU.mult).then_inc(qk_rows, 1)
                else:
                    x_ = k_n[:, :, rows, 0:NOPE]
                    v.tensor_tensor(x_, x_, inv(0, NOPE), ALU.mult).then_inc(qk_rows, 1)

            for n in range(2 * HC):
                q, c = divmod(n, HC)
                for t in range(TT):
                    i = n * TT + t
                    v.wait_ge(sq_made, i + 1)
                    sums = lambda a: nrm[:, 0, a, c, HN * t:HN * t + HN]
                    if q:
                        s3 = sq[:, i % 2, 0:HN * QK].rearrange("p (h e) -> p h e", h=HN)
                        step(v.tensor_reduce(sums(2), s3[:, :, NOPE:], AX.X, ALU.add))
                        v.tensor_reduce(sums(1), s3[:, :, 0:NOPE], AX.X, ALU.add).then_inc(sum_made, 1)
                    else:
                        s3 = sq[:, i % 2, 0:HN * NOPE].rearrange("p (h e) -> p h e", h=HN)
                        v.tensor_reduce(sums(0), s3, AX.X, ALU.add).then_inc(sum_made, 1)
                        v.wait_ge(k_copied, i + 1)
                        b = full(v, ("kv_b", c, t)).rearrange("p (h e) -> p h e", h=HN)
                        release(("kv_b", c, t), v.tensor_copy(v_n[:, t, HN * c:HN * c + HN, :], b[:, :, NOPE:]))
                    if t == 2 and n:
                        normalised(n - 1)
            def k_turned(h):
                release(("ht", 1, h), v.tensor_scalar(qk_t[:, h % 2, 1, :], full(v, ("ht", 1, h))[0:QK, :],
                                                      gcol[:, 1:2], None, ALU.mult))

            def masked(h, t):
                b = full(v, ("sc", h, t))
                w = (t + 1) * P
                v.tensor_tensor_reduce(b[:, 0:w], b[:, 0:w], mask[:, SEQ - w:], -QK ** -0.5, 3e38, ALU.add, ALU.min,
                                       st[:, 8 * (h % 2) + t:8 * (h % 2) + t + 1]).then_inc(max_ready, 1)

            k_turned(0)
            k_turned(1)
            for t in range(TT):
                masked(0, t)
            normalised(2 * HC - 1)
            for h in range(NH):
                for t in range(TT):
                    if h + 1 < NH:
                        masked(h + 1, t)
                    if h and t == 0:
                        v.wait_ge(*closed(("o", h - 1)))
                    if t < TT - 1:
                        release(("pt", h, t), v.tensor_copy(p_t[:, tri(t)], full(v, ("pt", h, t))[:, 0:(t + 1) * P]))
                if h + 2 < NH:
                    k_turned(h + 2)
                v.wait_ge(prob_ready, (h + 1) * TT)
                rs = st[:, 16 + 8 * (h % 2):16 + 8 * (h % 2) + TT]
                step(v.reciprocal(st[:, 32:32 + TT], rs))
                b = full(v, ("o", h))[:, 0:TT * VD].rearrange("p (t e) -> p t e", t=TT)
                w = release(("o", h), v.tensor_tensor(o_n[:, :, h * VD:h * VD + VD], b,
                                                      st[:, 32:32 + TT].unsqueeze(2).to_broadcast([P, TT, VD]),
                                                      ALU.mult))
                v.wait_ge(*w)
            split_rows("o_t", hi=h_hi, lo=h_lo)
            for half in range(2):
                add_rows(("w_o", half), half)
            v.wait_ge(gain_in, 48)
            rms_and_split("ffn1", 3 * TT, to_a, gain_row[1])
            swiglu("f3")


_INS = ['x', 'w_in', 'w_pool', 'pool_scale', 'w_out', 'ln1_g', 'ln1_b', 'w_up', 'conv_w', 'conv_b', 'w_down',
        'ln2_g', 'ln2_b', 'positions_2', 'mix_norm_2', 'ffn_norm_2', 'ffn_w_gate_up_2', 'ffn_w_down_2',
        'ssm_w_in_2', 'ssm_lambda_re_2', 'ssm_lambda_im_2', 'ssm_log_step_2', 'ssm_b_re_2', 'ssm_b_im_2',
        'ssm_c_re_2', 'ssm_c_im_2', 'ssm_d_2', 'ssm_w_glu_2', 'kv_in_norm_2', 'mla_w_kv_a_2', 'mla_kv_a_norm_2',
        'mla_w_kv_b_2', 'mla_k_nope_norm_2', 'mla_k_rope_norm_2', 'mla_w_q_a_2', 'mla_q_a_norm_2',
        'mla_w_q_b_2', 'mla_q_nope_norm_2', 'mla_q_rope_norm_2', 'mla_w_o_2']


def kernel(**inputs):
    import concourse.bacc as bacc
    from concourse.bass_utils import run_bass_kernel_spmd as run

    nc = bacc.Bacc("TRN2", target_bir_lowering=False, num_devices=1)
    arrays, args = {}, []
    given = {name: np.ascontiguousarray(inputs[name]) for name in _INS}
    given.update(constants())
    for name, a in given.items():
        arrays[f"in_{name}_dram"] = a
        args.append(nc.dram_tensor(f"in_{name}_dram", a.shape, mybir.dt.from_np(a.dtype), kind="ExternalInput").ap())
    args.append(nc.dram_tensor("out_dram", (1, SEQ, D), F, kind="ExternalOutput").ap())
    program(nc, *args)
    r = run(nc, [arrays], core_ids=[0])
    return r.results[0]["out_dram"]
```
